# Optimizing a Trainium2 kernel written in Bass

```python
import jax, jax.numpy as jnp
from jax import lax
import numpy as np
import math

D_MODEL = 2048
BATCH = 1
SEQ = 256
DEPTH = 1

CHUNK = 64
QUERY_BLOCK = 128
SB_HEADS = 8
SB_HEAD_DIM = 128
MLA_HEADS = 8
MLA_NOPE_DIM = 128
MLA_ROPE_DIM = 64
MLA_V_DIM = 128
MLA_Q_RANK = 768
MLA_KV_RANK = 512
N_BRANCHES = 2
D_FF = -(-8 * D_MODEL // (3 * 256)) * 256
ROPE_THETA = 10000.0
NORM_EPS = 1e-6
NEG_INF = -1e30

SB_WIDTH = SB_HEADS * SB_HEAD_DIM
MLA_QK_DIM = MLA_NOPE_DIM + MLA_ROPE_DIM
IN_WIDTHS = [SB_WIDTH, SB_WIDTH, SB_WIDTH, MLA_Q_RANK, MLA_KV_RANK, MLA_ROPE_DIM, N_BRANCHES * D_MODEL]
D_IN = int(sum(IN_WIDTHS))
IN_OFFSETS = [int(o) for o in np.cumsum(IN_WIDTHS)[:-1]]


def rms_norm(x, g):
    xf = x.astype(jnp.float32)
    y = xf * lax.rsqrt(jnp.mean(xf * xf, axis=-1, keepdims=True) + NORM_EPS)
    return (y * g.astype(jnp.float32)).astype(x.dtype)

def rope(x, positions):
    half = MLA_ROPE_DIM // 2
    inv_freq = ROPE_THETA ** (-jnp.arange(half, dtype=jnp.float32) / half)
    ang = positions.astype(jnp.float32)[..., None] * inv_freq
    if x.ndim == 4:
        ang = ang[:, :, None, :]
    cos, sin = jnp.cos(ang), jnp.sin(ang)
    xf = x.astype(jnp.float32)
    x1, x2 = xf[..., :half], xf[..., half:]
    return jnp.concatenate([x1 * cos - x2 * sin, x2 * cos + x1 * sin], axis=-1).astype(x.dtype)

def to_blocks(t):
    b, s = t.shape[:2]
    return jnp.moveaxis(t.reshape(b, s // QUERY_BLOCK, QUERY_BLOCK, *t.shape[2:]), 1, 0)

def from_blocks(t):
    t = jnp.moveaxis(t, 0, 1)
    return t.reshape(t.shape[0], -1, *t.shape[3:])

def stick_breaking_attention(q, k, v):
    seq = k.shape[1]
    scale = SB_HEAD_DIM ** -0.5
    key_pos = jnp.arange(seq)

    def one_block(args):
        qb, blk = args
        z = jnp.einsum('bqhd,bkhd->bhqk', qb, k).astype(jnp.float32) * scale
        q_pos = blk * QUERY_BLOCK + jnp.arange(QUERY_BLOCK)
        valid = key_pos[None, :] < q_pos[:, None]
        log_keep = jnp.where(valid, jax.nn.log_sigmoid(-z), 0.0)
        log_suffix = lax.cumsum(log_keep, axis=3, reverse=True) - log_keep
        w = jnp.where(valid, jnp.exp(jax.nn.log_sigmoid(z) + log_suffix), 0.0)
        return jnp.einsum('bhqk,bkhd->bqhd', w.astype(v.dtype), v)

    n_blocks = q.shape[1] // QUERY_BLOCK
    return from_blocks(lax.map(one_block, (to_blocks(q), jnp.arange(n_blocks))))

def mla_attention(q_nope, q_rope, k_nope, k_rope, v):
    seq = k_nope.shape[1]
    scale = MLA_QK_DIM ** -0.5
    key_chunk = jnp.arange(seq) // CHUNK

    def one_block(args):
        qn, qr, blk = args
        s = (jnp.einsum('bqhd,bkhd->bhqk', qn, k_nope)
             + jnp.einsum('bqhr,bkr->bhqk', qr, k_rope)).astype(jnp.float32) * scale
        q_chunk = (blk * QUERY_BLOCK + jnp.arange(QUERY_BLOCK)) // CHUNK
        allowed = key_chunk[None, :] <= q_chunk[:, None]
        p = jax.nn.softmax(jnp.where(allowed, s, NEG_INF), axis=-1)
        return jnp.einsum('bhqk,bkhd->bqhd', p.astype(v.dtype), v)

    n_blocks = q_nope.shape[1] // QUERY_BLOCK
    out = lax.map(one_block, (to_blocks(q_nope), to_blocks(q_rope), jnp.arange(n_blocks)))
    return from_blocks(out)

def first_inputs(seed: int = 0) -> dict:
    key = jax.random.key(seed)
    ks = jax.random.split(key, 20)
    f32 = jnp.float32

    def w(k, shape, fan_in):
        return jax.random.normal(k, shape, f32) * fan_in ** -0.5

    def gain(k, dim):
        return 1.0 + 0.1 * jax.random.normal(k, (DEPTH, dim), f32)

    x = jax.random.normal(ks[0], (BATCH, SEQ, D_MODEL), f32)
    offsets = jax.random.randint(ks[1], (BATCH, 1), 0, 4096) * CHUNK
    positions = (offsets + jnp.arange(SEQ, dtype=jnp.int32)[None, :]).astype(jnp.int32)
    return {
        "x": x,
        "positions": positions,
        "norm_pre_mix": gain(ks[2], D_MODEL),
        "w_in": w(ks[3], (DEPTH, D_MODEL, D_IN), D_MODEL),
        "b_gate": 0.1 * jax.random.normal(ks[4], (DEPTH, N_BRANCHES * D_MODEL), f32),
        "q_norm": gain(ks[5], MLA_Q_RANK),
        "w_uq": w(ks[6], (DEPTH, MLA_Q_RANK, MLA_HEADS * MLA_QK_DIM), MLA_Q_RANK),
        "kv_norm": gain(ks[7], MLA_KV_RANK),
        "w_ukv": w(ks[8], (DEPTH, MLA_KV_RANK, MLA_HEADS * (MLA_NOPE_DIM + MLA_V_DIM)), MLA_KV_RANK),
        "w_o_sb": w(ks[9], (DEPTH, SB_WIDTH, D_MODEL), SB_WIDTH),
        "w_o_mla": w(ks[10], (DEPTH, MLA_HEADS * MLA_V_DIM, D_MODEL), MLA_HEADS * MLA_V_DIM),
        "w_out": w(ks[11], (DEPTH, D_MODEL, D_MODEL), D_MODEL),
        "norm_post_mix": gain(ks[12], D_MODEL),
        "norm_pre_ffn": gain(ks[13], D_MODEL),
        "w_gate_up": w(ks[14], (DEPTH, D_MODEL, 2 * D_FF), D_MODEL),
        "w_down": w(ks[15], (DEPTH, D_FF, D_MODEL), D_FF),
        "norm_post_ffn": gain(ks[16], D_MODEL),
    }

def first_block(x, positions, norm_pre_mix, w_in, b_gate, q_norm, w_uq, kv_norm, w_ukv,
              w_o_sb, w_o_mla, w_out, norm_post_mix, norm_pre_ffn, w_gate_up, w_down,
              norm_post_ffn):
    b, s, _ = x.shape
    h = x
    for l in range(DEPTH):
        u = rms_norm(h, norm_pre_mix[l])
        proj = u @ w_in[l]
        q_sb, k_sb, v_sb, q_lat, kv_lat, k_r, gate_logits = jnp.split(proj, IN_OFFSETS, axis=-1)

        q_sb = q_sb.reshape(b, s, SB_HEADS, SB_HEAD_DIM)
        k_sb = k_sb.reshape(b, s, SB_HEADS, SB_HEAD_DIM)
        v_sb = v_sb.reshape(b, s, SB_HEADS, SB_HEAD_DIM)
        y_sb = stick_breaking_attention(q_sb, k_sb, v_sb).reshape(b, s, SB_WIDTH) @ w_o_sb[l]

        q = (rms_norm(q_lat, q_norm[l]) @ w_uq[l]).reshape(b, s, MLA_HEADS, MLA_QK_DIM)
        q_nope, q_rope = q[..., :MLA_NOPE_DIM], rope(q[..., MLA_NOPE_DIM:], positions)
        kv = (rms_norm(kv_lat, kv_norm[l]) @ w_ukv[l]).reshape(b, s, MLA_HEADS, MLA_NOPE_DIM + MLA_V_DIM)
        k_nope, v_mla = kv[..., :MLA_NOPE_DIM], kv[..., MLA_NOPE_DIM:]
        k_rope = rope(k_r, positions)
        y_mla = mla_attention(q_nope, q_rope, k_nope, k_rope, v_mla).reshape(b, s, MLA_HEADS * MLA_V_DIM) @ w_o_mla[l]

        gates = jax.nn.sigmoid((gate_logits + b_gate[l]).astype(jnp.float32)).astype(h.dtype)
        g_sb, g_mla = gates[..., :D_MODEL], gates[..., D_MODEL:]
        mixed = (g_sb * y_sb + g_mla * y_mla) @ w_out[l]
        h = h + rms_norm(mixed, norm_post_mix[l])

        gu = rms_norm(h, norm_pre_ffn[l]) @ w_gate_up[l]
        g, up = gu[..., :D_FF], gu[..., D_FF:]
        h = h + rms_norm((jax.nn.silu(g) * up) @ w_down[l], norm_post_ffn[l])
    return h


DEPTH_2 = 2

GRID_W = 64
N_MIXERS = 2
BLOCK_Q = 128
CHUNK_2 = 128
RMS_EPS = 1e-6
LN_EPS = 1e-5

A_HEADS = 16
A_KV_HEADS = 4
A_HEAD_DIM = D_MODEL // A_HEADS
A_GROUP = A_HEADS // A_KV_HEADS
A_WIDTH = A_HEADS * A_HEAD_DIM
A_KV_WIDTH = A_KV_HEADS * A_HEAD_DIM
A_IN = 2 * A_WIDTH + 2 * A_KV_WIDTH

R_HEADS = 8
R_QK_DIM = D_MODEL // R_HEADS
R_V_DIM = 2 * R_QK_DIM
R_QK_WIDTH = R_HEADS * R_QK_DIM
R_V_WIDTH = R_HEADS * R_V_DIM
R_IN = 2 * R_QK_WIDTH + 2 * R_V_WIDTH
R_DECAY_BASE = 5.0

N_A_LAYERS = (DEPTH_2 + 1) // N_MIXERS
N_R_LAYERS = DEPTH_2 // N_MIXERS
ALPHA = (2.0 * DEPTH_2) ** 0.25
BETA = (8.0 * DEPTH_2) ** -0.25


def axial_rope_tables(seq_len, head_dim):
    rows_n = seq_len // GRID_W
    row = jnp.repeat(jnp.arange(rows_n, dtype=jnp.float32), GRID_W)
    col = jnp.tile(jnp.arange(GRID_W, dtype=jnp.float32), rows_n)
    half = head_dim // 2
    inv_freq = ROPE_THETA ** (-jnp.arange(0, half, 2, dtype=jnp.float32) / half)
    ang_r = row[:, None] * inv_freq
    ang_c = col[:, None] * inv_freq
    ang = jnp.concatenate([ang_r, ang_r, ang_c, ang_c], axis=-1)
    return jnp.cos(ang), jnp.sin(ang)

def apply_rope(x, cos, sin):
    x32 = x.astype(jnp.float32)
    a, b, c, d = jnp.split(x32, 4, axis=-1)
    rot = jnp.concatenate([-b, a, -d, c], axis=-1)
    out = x32 * cos[None, :, None, :] + rot * sin[None, :, None, :]
    return out.astype(x.dtype)

def rms_norm_2(x, gain):
    x32 = x.astype(jnp.float32)
    y = x32 * lax.rsqrt(jnp.mean(x32 * x32, axis=-1, keepdims=True) + RMS_EPS)
    return (y * gain.astype(jnp.float32)).astype(x.dtype)

def layer_norm(x, gain, bias):
    x32 = x.astype(jnp.float32)
    mu = jnp.mean(x32, axis=-1, keepdims=True)
    var = jnp.mean(jnp.square(x32 - mu), axis=-1, keepdims=True)
    y = (x32 - mu) * lax.rsqrt(var + LN_EPS)
    return (y * gain.astype(jnp.float32) + bias.astype(jnp.float32)).astype(x.dtype)

def head_group_norm(x):
    x32 = x.astype(jnp.float32)
    mu = jnp.mean(x32, axis=-1, keepdims=True)
    var = jnp.mean(jnp.square(x32 - mu), axis=-1, keepdims=True)
    return ((x32 - mu) * lax.rsqrt(var + LN_EPS)).astype(x.dtype)

def attention_mixer(h, w_in, q_gain, k_gain, w_out, cos, sin):
    B, S, _ = h.shape
    proj = h @ w_in
    q, k, v, g = jnp.split(proj, [A_WIDTH, A_WIDTH + A_KV_WIDTH, A_WIDTH + 2 * A_KV_WIDTH], axis=-1)
    q = q.reshape(B, S, A_HEADS, A_HEAD_DIM)
    k = k.reshape(B, S, A_KV_HEADS, A_HEAD_DIM)
    v = v.reshape(B, S, A_KV_HEADS, A_HEAD_DIM)
    q = apply_rope(rms_norm_2(q, q_gain), cos, sin) * (A_HEAD_DIM ** -0.5)
    k = apply_rope(rms_norm_2(k, k_gain), cos, sin)
    n_blocks = S // BLOCK_Q
    qb_all = q.reshape(B, n_blocks, BLOCK_Q, A_KV_HEADS, A_GROUP, A_HEAD_DIM).transpose(1, 0, 3, 4, 2, 5)

    def block(qb):
        s = jnp.einsum('bkgqd,bskd->bkgqs', qb, k).astype(jnp.float32)
        p = jax.nn.softmax(s, axis=-1).astype(v.dtype)
        return jnp.einsum('bkgqs,bskd->bkgqd', p, v)

    o = lax.map(block, qb_all)
    o = o.transpose(1, 0, 4, 2, 3, 5).reshape(B, S, A_WIDTH)
    return (o * jax.nn.silu(g)) @ w_out

def chunk_retention(q, k, v, log_g, strict):
    B, S, H, dk = q.shape
    dv = v.shape[-1]
    nc = S // CHUNK_2

    def to_chunks(t):
        return t.reshape(B, nc, CHUNK_2, H, t.shape[-1]).transpose(1, 0, 3, 2, 4)

    qc, kc, vc = to_chunks(q), to_chunks(k), to_chunks(v)
    log_g = log_g.astype(jnp.float32)
    pos = jnp.arange(CHUNK_2, dtype=jnp.float32)
    diff = pos[:, None] - pos[None, :]
    mask = (diff > 0) if strict else (diff >= 0)
    intra_decay = jnp.where(mask[None], jnp.exp(log_g[:, None, None] * jnp.maximum(diff, 0.0)[None]), 0.0)
    q_decay = jnp.exp(log_g[:, None] * (pos + 1.0))[..., None]
    k_decay = jnp.exp(log_g[:, None] * (CHUNK_2 - 1.0 - pos))[..., None]
    chunk_decay = jnp.exp(log_g * CHUNK_2)[:, None, None]

    def step(state, xs):
        qb, kb, vb = xs
        q32, k32, v32 = qb.astype(jnp.float32), kb.astype(jnp.float32), vb.astype(jnp.float32)
        s = jnp.einsum('bhqd,bhkd->bhqk', q32, k32) * intra_decay
        inner = jnp.einsum('bhqk,bhkv->bhqv', s, v32)
        cross = jnp.einsum('bhqd,bhdv->bhqv', q32, state) * q_decay
        new_state = state * chunk_decay + jnp.einsum('bhkd,bhkv->bhdv', k32 * k_decay, v32)
        return new_state, (inner + cross).astype(vb.dtype)

    state0 = jnp.zeros((B, H, dk, dv), jnp.float32)
    _, out = lax.scan(step, state0, (qc, kc, vc))
    return out.transpose(1, 0, 3, 2, 4).reshape(B, S, H, dv)

def retention_mixer(h, w_in, decay_exp, w_out, cos, sin):
    B, S, _ = h.shape
    proj = h @ w_in
    q, k, v, g = jnp.split(proj, [R_QK_WIDTH, 2 * R_QK_WIDTH, 2 * R_QK_WIDTH + R_V_WIDTH], axis=-1)
    q = apply_rope(q.reshape(B, S, R_HEADS, R_QK_DIM), cos, sin)
    k = apply_rope(k.reshape(B, S, R_HEADS, R_QK_DIM), cos, sin) * (R_QK_DIM ** -0.5)
    v = v.reshape(B, S, R_HEADS, R_V_DIM)
    log_g = jnp.log1p(-jnp.exp2(-decay_exp.astype(jnp.float32)))
    fwd = chunk_retention(q, k, v, log_g[0], strict=False)
    bwd = jnp.flip(chunk_retention(jnp.flip(q, 1), jnp.flip(k, 1), jnp.flip(v, 1), log_g[1], strict=True), 1)
    o = head_group_norm(fwd + bwd).reshape(B, S, R_V_WIDTH)
    return (o * jax.nn.silu(g)) @ w_out

def second_inputs(seed: int = 0) -> dict:
    key = jax.random.key(seed)
    ks = jax.random.split(key, 12)
    f32 = jnp.float32
    x = jax.random.normal(ks[0], (BATCH, SEQ, D_MODEL), f32)

    a_col_scale = jnp.concatenate([jnp.ones((A_WIDTH + A_KV_WIDTH,), f32),
                                   jnp.full((A_KV_WIDTH,), BETA, f32),
                                   jnp.ones((A_WIDTH,), f32)])
    attn_w_in = jax.random.normal(ks[1], (N_A_LAYERS, D_MODEL, A_IN), f32) * (D_MODEL ** -0.5) * a_col_scale
    attn_q_gain = 1.0 + 0.02 * jax.random.normal(ks[2], (N_A_LAYERS, A_HEAD_DIM), f32)
    attn_k_gain = 1.0 + 0.02 * jax.random.normal(ks[3], (N_A_LAYERS, A_HEAD_DIM), f32)
    attn_w_out = jax.random.normal(ks[4], (N_A_LAYERS, A_WIDTH, D_MODEL), f32) * (A_WIDTH ** -0.5) * BETA

    r_col_scale = jnp.concatenate([jnp.ones((2 * R_QK_WIDTH,), f32),
                                   jnp.full((R_V_WIDTH,), BETA, f32),
                                   jnp.ones((R_V_WIDTH,), f32)])
    ret_w_in = jax.random.normal(ks[5], (N_R_LAYERS, D_MODEL, R_IN), f32) * (D_MODEL ** -0.5) * r_col_scale
    base = R_DECAY_BASE + jnp.arange(R_HEADS, dtype=f32)
    base2 = jnp.stack([base, base[::-1]], axis=0)
    ret_decay_exp = base2[None] + 0.1 * jax.random.normal(ks[6], (N_R_LAYERS, 2, R_HEADS), f32)
    ret_w_out = jax.random.normal(ks[7], (N_R_LAYERS, R_V_WIDTH, D_MODEL), f32) * (R_V_WIDTH ** -0.5) * BETA

    ln_gain = 1.0 + 0.02 * jax.random.normal(ks[8], (DEPTH_2, D_MODEL), f32)
    ln_bias = 0.02 * jax.random.normal(ks[9], (DEPTH_2, D_MODEL), f32)
    return {"x": x, "attn_w_in": attn_w_in, "attn_q_gain": attn_q_gain, "attn_k_gain": attn_k_gain,
            "attn_w_out": attn_w_out, "ret_w_in": ret_w_in, "ret_decay_exp": ret_decay_exp,
            "ret_w_out": ret_w_out, "ln_gain": ln_gain, "ln_bias": ln_bias}

def second_block(x, attn_w_in, attn_q_gain, attn_k_gain, attn_w_out, ret_w_in, ret_decay_exp,
              ret_w_out, ln_gain, ln_bias):
    S = x.shape[1]
    cos_a, sin_a = axial_rope_tables(S, A_HEAD_DIM)
    cos_r, sin_r = axial_rope_tables(S, R_QK_DIM)
    for i in range(DEPTH_2):
        j = i // N_MIXERS
        if i % N_MIXERS == 0:
            y = attention_mixer(x, attn_w_in[j], attn_q_gain[j], attn_k_gain[j], attn_w_out[j], cos_a, sin_a)
        else:
            y = retention_mixer(x, ret_w_in[j], ret_decay_exp[j], ret_w_out[j], cos_r, sin_r)
        x = layer_norm(ALPHA * x + y, ln_gain[i], ln_bias[i])
    return x


def setup_inputs(seed=0):
    out = dict(first_inputs(seed))
    for name, value in second_inputs(seed + 1).items():
        if name != "x":
            out[name + "_2"] = value
    return out


def reference(
    x, positions, norm_pre_mix, w_in, b_gate, q_norm, w_uq, kv_norm, w_ukv, w_o_sb, w_o_mla,
    w_out, norm_post_mix, norm_pre_ffn, w_gate_up, w_down, norm_post_ffn, attn_w_in_2,
    attn_q_gain_2, attn_k_gain_2, attn_w_out_2, ret_w_in_2, ret_decay_exp_2, ret_w_out_2,
    ln_gain_2, ln_bias_2,
):
    x = first_block(
        x, positions, norm_pre_mix, w_in, b_gate, q_norm, w_uq, kv_norm, w_ukv, w_o_sb, w_o_mla,
        w_out, norm_post_mix, norm_pre_ffn, w_gate_up, w_down, norm_post_ffn,
    )
    return second_block(
        x, attn_w_in_2, attn_q_gain_2, attn_k_gain_2, attn_w_out_2, ret_w_in_2, ret_decay_exp_2,
        ret_w_out_2, ln_gain_2, ln_bias_2,
    )


_drawn_inputs = setup_inputs


def setup_inputs(seed=0):
    import zlib

    import numpy as np

    out = dict(_drawn_inputs(seed))
    spreads = {}
    factors = {'q_norm': 2.935, 'attn_q_gain_2': 8.0, 'attn_k_gain_2': 8.0}
    for name, (base, spread) in spreads.items():
        noise = np.random.default_rng([zlib.crc32(name.encode()), seed]).standard_normal(out[name].shape)
        drawn = base * np.exp(spread * noise) if base else spread * noise
        out[name] = __import__('jax').numpy.asarray(drawn.astype(out[name].dtype))
    for name, factor in factors.items():
        out[name] = (out[name] * factor).astype(out[name].dtype)
    return out
```

```python
from contextlib import ExitStack

import numpy as np

import concourse.bass as bass
from concourse import mybir

F32, F32R, I32 = mybir.dt.float32, mybir.dt.float32r, mybir.dt.int32
ALU = mybir.AluOpType
ACT = mybir.ActivationFunctionType
AX = mybir.AxisListType
ds = bass.ds

P = 128
T = 2
TOK = T * P
D = 2048
DK = D // P
SB_H, HD = 8, 128
MLA_H, ROPE, QK_DIM = 8, 64, 192
Q_RANK, KV_RANK = 768, 512
D_FF = 5632
A_H, A_KV = 16, 4
R_H, R_QK, R_V = 8, 256, 512
EPS, LN_EPS = 1e-6, 1e-5
ALPHA = (2.0 * 2) ** 0.25
BIG = -1e30
RSQRT_SEED = float(0x5F3759DF)
ROUND = 12582912.0
PI_F = 3.1415925

R = 4
UE = 1024
CW = 512

UNITS = {}
_n = 0
for _name, _u in [("qkv", 6 * 8), ("lat", 3 * 8), ("uq", 4 * 3), ("ukv", 4 * 2), ("gate", 8 * 8), ("mix", 4 * 8),
                  ("out", 2 * DK), ("up", 11 * 16), ("down", 2 * D_FF // P), ("aqkv", 6 * 8), ("ag", 4 * 8),
                  ("aout", 2 * DK), ("ret", 4 * 48), ("rout", 2 * 32)]:
    UNITS[_name] = _n
    _n += _u
N_UNITS = _n
DVE_STAGE = {name: i + 1 for i, name in enumerate(('r1', 'ang', 'krot_done', 'rlat', 'mla_end', 'r2', 'attn_end', 'ret_end'))}
ACT_STAGE = {name: i + 1 for i, name in enumerate(('ss_x', 'sines', 'ss_lat', 'kr_hi', 'lg'))}


def at_least(eng, sem, value):
    if not (isinstance(value, int) and value <= 0):
        eng.wait_ge(sem, value)


def repeat(eng, n, body, own=None, last=False):
    if own:
        own.enter()
    body(0)
    if own:
        own.measured()
    end = n - 1 if last else n
    if end > 1:
        with eng.Fori(1, end) as i:
            if own:
                own.at(i)
            body(i)
    if last:
        if own:
            own.at(n - 1)
        body(n - 1)
    if own:
        own.leave(n)


class Own:

    def __init__(self, eng, sem):
        self.eng, self.sem = eng, sem
        self.base, self.k, self.i, self.per = 0, 0, 0, 0

    def mark(self, instruction):
        instruction.then_inc(self.sem, 1)
        self.k += 1

    def wait(self):
        at_least(self.eng, self.sem, self.base + self.i * self.per + self.k)

    def step(self, instruction):
        self.mark(instruction)
        self.wait()

    def enter(self):
        self.base, self.k, self.i, self.per = self.base + self.k, 0, 0, 0

    def measured(self):
        self.per = self.k

    def at(self, i):
        assert self.k == self.per or not self.i, (self.k, self.per)
        self.k, self.i = 0, i

    def leave(self, n):
        assert self.k == self.per, (self.k, self.per)
        self.base, self.k, self.i, self.per = self.base + n * self.per, 0, 0, 0


def slot_of(base, i, per):
    return base % R, base // R + i * (per // R), base + i * per


def build(nc, x, xT, positions, g_pre, w_in, b_gate, g_lat, w_uq, w_ukv, w_o_sb, w_o_mla, w_out, g_post_mix,
          g_ffn, w_gate_up, w_down, g_post_ffn, a_w_in, a_q_gain, a_k_gain, a_w_out, r_w_in, r_decay, r_w_out,
          ln_gain, ln_bias, c_ident, c_ntri, c_nones, c_mask_sb, c_mask_mla, c_invf, c_cos_a, c_sin_a,
          c_cos_r, c_sin_r, c_dist_f, c_dist_b, out):
    gates_dram = nc.dram_tensor("gates_scratch", (TOK, 2 * D), F32, kind="Internal").ap()
    with ExitStack() as ctx:
        lo_end = -(-nc.sbuf_base // 64) * 64
        top = [lo_end]
        size = nc.sbuf_usable_end - lo_end

        def place(name, shape, dt, offset):
            n = 4
            for s in shape[1:]:
                n *= s
            assert offset + n <= lo_end + size, (name, offset + n - lo_end, size)
            return nc.alloc_sbuf_tensor_at(name, shape, dt, offset=offset)

        def put(name, shape, dt):
            t = place(name, shape, dt, top[0])
            n = 4
            for s in shape[1:]:
                n *= s
            top[0] += -(-n // 32) * 32
            return t

        raw = put("raw", [P, R, UE], F32)
        whi = put("whi", [P, R, UE], F32R)
        wlo = put("wlo", [P, R, UE], F32R)
        xh = put("xh", [P, DK, TOK], F32R)
        xl = put("xl", [P, DK, TOK], F32R)
        s0 = put("s0", [P, T, CW], F32)
        s1 = put("s1", [P, T, CW], F32)
        ident = put("ident", [P, P], F32)
        ident_r = put("ident_r", [P, P], F32R)
        ntri = put("ntri", [P, P], F32R)
        nones = put("nones", [P, P], F32R)
        mask_sb = put("mask_sb", [P, 3 * P], F32R)
        mask_mla = put("mask_mla", [P, T * TOK], F32R)
        gpre_c = put("gpre_c", [P, DK], F32)
        gffn_c = put("gffn_c", [P, DK], F32)
        glat_c = put("glat_c", [P, 10], F32)
        cos_m = put("cos_m", [P, T, ROPE], F32)
        sin_m = put("sin_m", [P, T, ROPE], F32)
        r1 = put("r1", [P, 2], F32)
        rlat = put("rlat", [P, 4], F32)
        r2 = put("r2", [P, 2], F32)
        ssum = put("ssum", [P, 16], F32)
        rs_v = put("rs_v", [P, 16], F32)
        rs_y = put("rs_y", [P, 16], F32)
        rs_t = put("rs_t", [P, 16], F32)
        mark = put("mark", [P, 1], F32)
        rs_i = put("rs_i", [P, 16], I32)
        nmax = put("nmax", [P, 4, 2], F32)
        psum_ = put("psum_", [P, 4, 2], F32)
        prec = put("prec", [P, 4, 2], F32)
        stats = put("stats", [P, 2, 4, 6], F32)
        mv = put("mv", [P, 2, 2], F32)
        lg = put("lg", [P, 16], F32)
        h0 = top[0]
        h = place("h", [P, T, D], F32, h0)
        K = 1024
        qkT = place("qkT", [P, 16, TOK], F32, h0)
        v_sb = place("v_sb", [P, T, 1024], F32, h0 + 16 * K)
        qnT = place("qnT", [P, MLA_H, TOK], F32, h0 + 24 * K)
        qrT = place("qrT", [P, MLA_H // 2, TOK], F32, h0 + 32 * K)
        knT = place("knT", [P, MLA_H, TOK], F32, h0 + 36 * K)
        krh = place("krh", [P, TOK], F32R, h0 + 44 * K)
        krl = place("krl", [P, TOK], F32R, h0 + 45 * K)
        vm = place("vm", [P, T, MLA_H, HD], F32, h0 + 46 * K)
        yTh = place("yTh", [P, 16, TOK], F32R, h0 + 54 * K)
        yTl = place("yTl", [P, 16, TOK], F32R, h0 + 70 * K)
        latTh = place("latTh", [P, 10, TOK], F32R, h0 + 54 * K)
        latTl = place("latTl", [P, 10, TOK], F32R, h0 + 64 * K)
        lat = place("lat", [P, T, 1344], F32, h0 + 74 * K)
        x_tok = place("x_tok", [P, T, D], F32, h0 + 54 * K)
        xT_raw = place("xT_raw", [P, DK, TOK], F32, h0 + 70 * K)
        W = h0 + 86 * K
        sth = place("sth", [P, 2, 3, TOK], F32R, W)
        stl = place("stl", [P, 2, 3, TOK], F32R, W + 6 * K)
        sbt = place("sbt", [P, 384], F32, W + 12 * K)
        sbL = place("sbL", [P, 384], F32, W + 12 * K + 1536)
        sbh = place("sbh", [P, 384], F32R, W + 15 * K)
        sbl = place("sbl", [P, 384], F32R, W + 15 * K + 1536)
        mqh = place("mqh", [P, 4, TOK], F32R, W)
        mql = place("mql", [P, 4, TOK], F32R, W + 4 * K)
        mp = place("mp", [P, T, TOK], F32, W + 8 * K)
        mph = place("mph", [P, T, TOK], F32R, W + 10 * K)
        mpl = place("mpl", [P, T, TOK], F32R, W + 12 * K)
        bias_t = place("bias_t", [P, CW], F32, W + 18 * K)
        pos_i = place("pos_i", [P, T], I32, W)
        pos_f = place("pos_f", [P, T], F32, W + 64)
        invf = place("invf", [P, 32], F32, W + 128)
        ang = place("ang", [P, T, 32], F32, W + 512)
        kk = place("kk", [P, T, 32], F32, W + 1024)
        angc = place("angc", [P, T, 32], F32, W + 1536)
        krot = place("krot", [P, T, P], F32, W + 2 * K)
        rtmp = place("rtmp", [P, T, P], F32, W + 4 * K)
        rtm2 = place("rtm2", [P, T, P], F32, W + 5 * K)
        gt = place("gt", [P, 2, T, CW], F32, h0 + 16 * K)
        mixT = place("mixT", [P, DK, TOK], F32, h0 + 24 * K)
        osh1 = place("osh1", [P, 2, TOK], F32R, h0 + 40 * K)
        osl1 = place("osl1", [P, 2, TOK], F32R, h0 + 42 * K)
        gbc1 = place("gbc1", [P, D], F32, W)
        tmp1 = place("tmp1", [P, D], F32, W + 8 * K)
        actT = place("actT", [P, 44, TOK], F32, h0 + 16 * K)
        osh2 = place("osh2", [P, 2, TOK], F32R, h0 + 60 * K)
        osl2 = place("osl2", [P, 2, TOK], F32R, h0 + 62 * K)
        gbc2 = place("gbc2", [P, D], F32, h0 + 64 * K)
        tmp2 = place("tmp2", [P, D], F32, h0 + 72 * K)
        aqT = place("aqT", [P, A_H + A_KV, TOK], F32, h0 + 16 * K)
        av = place("av", [P, T, CW], F32, h0 + 36 * K)
        agT = place("agT", [P, DK, TOK], F32, h0 + 40 * K)
        osh3 = place("osh3", [P, 2, TOK], F32R, h0 + 56 * K)
        osl3 = place("osl3", [P, 2, TOK], F32R, h0 + 58 * K)
        cgs = place("cgs", [P, 4, T, HD], F32, h0 + 60 * K)
        kvh = place("kvh", [P, 2, TOK], F32R, h0 + 64 * K)
        kvl = place("kvl", [P, 2, TOK], F32R, h0 + 66 * K)
        aqh = place("aqh", [P, 2, TOK], F32R, h0 + 68 * K)
        aql = place("aql", [P, 2, TOK], F32R, h0 + 70 * K)
        ap_ = place("ap_", [P, 2, T, TOK], F32, h0 + 72 * K)
        aph = place("aph", [P, T, TOK], F32R, h0 + 76 * K)
        apl = place("apl", [P, T, TOK], F32R, h0 + 78 * K)
        obuf = place("obuf", [P, T, CW], F32, h0 + 84 * K)
        sqt = place("sqt", [P, T, CW], F32, h0 + 88 * K)
        gtab = place("gtab", [P, 2, HD], F32, h0 + 92 * K)
        ctab = place("ctab", [P, 2, T, HD], F32, h0 + 93 * K)
        lng1 = place("lng1", [P, 2, D], F32, h0 + 64 * K)
        rqh = place("rqh", [P, 2, 4, TOK], F32R, h0 + 16 * K)
        rql = place("rql", [P, 2, 4, TOK], F32R, h0 + 24 * K)
        pth = place("pth", [P, 2, T, TOK], F32R, h0 + 32 * K)
        ptl = place("ptl", [P, 2, T, TOK], F32R, h0 + 36 * K)
        rvh = place("rvh", [P, 2, T, R_V], F32R, h0 + 40 * K)
        rvl = place("rvl", [P, 2, T, R_V], F32R, h0 + 48 * K)
        rcs = place("rcs", [P, 2, T, R_QK], F32, h0 + 56 * K)
        dist = place("dist", [P, 2, T, TOK], F32, h0 + 60 * K)
        dmat = place("dmat", [P, 2, T, TOK], F32, h0 + 64 * K)
        onorm = place("onorm", [P, 2, T, R_V], F32, h0 + 68 * K)
        rgT = place("rgT", [P, 32, TOK], F32, h0 + 76 * K)
        rt = place("rt", [P, CW], F32, h0 + 108 * K)
        osh4 = place("osh4", [P, 2, TOK], F32R, h0 + 16 * K)
        osl4 = place("osl4", [P, 2, TOK], F32R, h0 + 18 * K)
        lng2 = place("lng2", [P, 2, D], F32, h0 + 32 * K)

        acc = ctx.enter_context(nc.psum_tensor("acc", [P, 2, T, CW], F32))
        aux = ctx.enter_context(nc.psum_tensor("aux", [P, 4, CW], F32))
        banks = [acc[:, 0, 0], acc[:, 0, 1], acc[:, 1, 0], acc[:, 1, 1], aux[:, 0], aux[:, 1], aux[:, 2], aux[:, 3]]
        whole = [acc[:].rearrange("p a b c -> p (a b c)"), aux[:].rearrange("p a c -> p (a c)")]

        names = {}

        def sem(name):
            if name not in names:
                names[name] = ctx.enter_context(nc.semaphore(name))
            return names[name]

        landed = [sem(f"weights_landed{s}") for s in range(R)]
        hi_done, lo_done, used = sem("hi_done"), sem("lo_done"), sem("unit_used")
        consts, act_own, dve_own = sem("consts"), sem("act_own"), sem("dve_own")

        block = ctx.enter_context(nc.Block())

        @block.sync
        def _(sp):
            def load(base, i, per, src, width):
                slot, turn, n = slot_of(base, i, per)
                at_least(sp, lo_done, n - R + 1)
                if width == UE:
                    dst = raw[:, slot]
                else:
                    dst = raw[:, slot, 0:2 * width].rearrange("p (k n) -> p k n", k=2)
                sp.dma_start(dst, src).then_inc(landed[slot], 16)

            def chunk(base, i, per, w, units, col, width=CW, row0=0):
                for u in range(units):
                    src = w[row0 + u * 2 * P:row0 + (u + 1) * 2 * P, ds(col, width)].rearrange("(k p) n -> p k n", p=P)
                    load(base + u, i, per, src, width)

            def rows(name, n_kt, w):
                def body(i):
                    for k in range(2):
                        for half in range(2):
                            load(UNITS[name] + 2 * k + half, i, 4,
                                 w[ds(i * 2 * P + k * P, P), half * UE:(half + 1) * UE], UE)
                repeat(sp, n_kt // 2, body)

            repeat(sp, 3, lambda i: [chunk(UNITS["qkv"] + 8 * c, i, 16, w_in, 8, i * 1024 + c * CW) for c in range(2)])
            for c in range(3):
                chunk(UNITS["lat"] + 8 * c, 0, 8, w_in, 8, 3072 + c * 448, 448)
            for c in range(4):
                chunk(UNITS["uq"] + 3 * c, 0, 4, w_uq, 3, c * 384, 384)
            for c in range(4):
                chunk(UNITS["ukv"] + 2 * c, 0, 4, w_ukv, 2, c * CW)

            def gate(i):
                chunk(UNITS["gate"], i, 8, w_in, 8, i * CW + 4416)
            repeat(sp, 8, gate)

            def mix(i):
                chunk(UNITS["mix"], i, 8, w_o_sb, 4, i * CW)
                chunk(UNITS["mix"] + 4, i, 8, w_o_mla, 4, i * CW)
            repeat(sp, 4, mix)
            rows("out", DK, w_out)

            def up(i):
                chunk(UNITS["up"], i, 16, w_gate_up, 8, i * CW)
                chunk(UNITS["up"] + 8, i, 16, w_gate_up, 8, i * CW + D_FF)
            repeat(sp, 11, up)
            rows("down", 44, w_down)
            repeat(sp, 3, lambda i: [chunk(UNITS["aqkv"] + 8 * c, i, 16, a_w_in, 8, i * 1024 + c * CW) for c in range(2)])
            repeat(sp, 4, lambda i: chunk(UNITS["ag"], i, 8, a_w_in, 8, i * CW + 3072))
            rows("aout", DK, a_w_out)

            def ret(i):
                cols = [i * CW, i * CW + 2048, i * 1024 + 4096, i * 1024 + 4608, i * 1024 + 8192, i * 1024 + 8704]
                for c, col in enumerate(cols):
                    chunk(UNITS["ret"] + 8 * c, i, 48, r_w_in, 8, col)
            repeat(sp, 4, ret)
            rows("rout", 32, r_w_out)
            sp.wait_ge(sem("stored"), 16 * T)

        @block.gpsimd
        def _(pool):
            def bring(name, pairs):
                for dst, src in pairs:
                    pool.dma_start(dst, src).then_inc(sem(name), 16)

            bring("x_in", [(xT_raw[:], xT.rearrange("(k p) t -> p k t", p=P)), (gpre_c[:], g_pre),
                           (x_tok[:], x.rearrange("(t p) n -> p t n", p=P))])
            bring("consts", [(ident[:], c_ident), (gffn_c[:], g_ffn), (glat_c[:], g_lat),
                             (pos_i[:], positions), (invf[:], c_invf.partition_broadcast(P))])
            bring("masks", [(s1[:, 0, 0:P], c_ntri), (s1[:, 0, P:2 * P], c_nones), (s1[:, 1, 0:384], c_mask_sb),
                            (s0[:, 0], c_mask_mla)])

            pool.wait_ge(sem("dve_stage"), DVE_STAGE["mla_end"])
            pool.dma_start(h[:], x.rearrange("(t p) n -> p t n", p=P)).then_inc(sem("x_again"), 16)

            bring("gains_in", [(gbc1[:], g_post_mix.partition_broadcast(P))])
            pool.wait_ge(sem("mixer_done"), 1)
            bring("gains_in", [(gbc2[:], g_post_ffn.partition_broadcast(P))])
            pool.wait_ge(sem("ffn_done"), 1)
            bring("tables_in", [(gtab[:, 0], a_q_gain.partition_broadcast(P)), (gtab[:, 1], a_k_gain.partition_broadcast(P)),
                              (ctab[:, 0], c_cos_a.rearrange("(t p) n -> p t n", p=P)),
                              (ctab[:, 1], c_sin_a.rearrange("(t p) n -> p t n", p=P))])
            pool.wait_ge(sem("dve_stage"), DVE_STAGE["attn_end"])
            bring("gains_in", [(lng1[:, 0], ln_gain[0].partition_broadcast(P)), (lng1[:, 1], ln_bias[0].partition_broadcast(P))])
            pool.wait_ge(sem("attn_done"), 1)
            bring("tables_in", [(rcs[:, 0], c_cos_r.rearrange("(t p) n -> p t n", p=P)),
                              (rcs[:, 1], c_sin_r.rearrange("(t p) n -> p t n", p=P)),
                              (dist[:, 0], c_dist_f.rearrange("(t p) n -> p t n", p=P)),
                              (dist[:, 1], c_dist_b.rearrange("(t p) n -> p t n", p=P)),
                              (lg[:], r_decay.partition_broadcast(P))])
            pool.wait_ge(sem("dve_stage"), DVE_STAGE["ret_end"])
            bring("gains_in", [(lng2[:, 0], ln_gain[1].partition_broadcast(P)), (lng2[:, 1], ln_bias[1].partition_broadcast(P))])
            for t in range(T):
                pool.wait_ge(sem("result"), t + 1)
                pool.dma_start(out[t * P:(t + 1) * P, :], h[:, t]).then_inc(sem("stored"), 16)

        @block.tensor
        def _(pe):
            def three(dst, lh, ll, rh, rl, start, stop):
                pe.matmul(dst, lh, rh, start=start, stop=False, skip_group_check=True)
                pe.matmul(dst, lh, rl, start=False, stop=False, skip_group_check=True)
                return pe.matmul(dst, ll, rh, start=False, stop=stop, skip_group_check=True)

            def unit(base, i, per, pair, kt0, n_kt, sh=xh, sl=xl, width=CW):
                slot, turn, n = slot_of(base, i, per)
                pe.wait_ge(lo_done, n + 1)
                for k in range(2):
                    for t in range(T):
                        tok = slice(t * P, (t + 1) * P)
                        last = three(acc[:, pair, t, 0:width], sh[:, kt0 + k, tok], sl[:, kt0 + k, tok],
                                     whi[:, slot, k * width:(k + 1) * width], wlo[:, slot, k * width:(k + 1) * width],
                                     start=kt0 + k == 0 or (k == 0 and kt0 == n_kt), stop=False)
                last.then_inc(used, 1)

            def turn_blocks(src, blocks, bank0=0):
                for b in range(blocks):
                    for t in range(T):
                        last = pe.transpose(aux[:, bank0 + b // 2, (b % 2) * TOK + t * P:(b % 2) * TOK + (t + 1) * P],
                                            src[:, t, b * P:(b + 1) * P], ident[:])
                return last

            def rows(name, n_kt, sh, sl):
                def body(i):
                    for k in range(2):
                        pe.wait_ge(sem(name + "_stage"), i * 2 + k + 1)
                        for half in range(2):
                            slot, turn, n = slot_of(UNITS[name] + 2 * k + half, i, 4)
                            pe.wait_ge(lo_done, n + 1)
                            for c in range(2):
                                for t in range(T):
                                    tok = slice(t * P, (t + 1) * P)
                                    cols = slice(c * CW, (c + 1) * CW)
                                    last = three(banks[4 * t + 2 * half + c], sh[:, k, tok], sl[:, k, tok],
                                                 whi[:, slot, cols], wlo[:, slot, cols],
                                                 start=isinstance(i, int) and i == 0 and k == 0, stop=False)
                            last.then_inc(used, 1)
                repeat(pe, n_kt // 2, body)

            pe.wait_ge(consts, 16 * 5)
            pe.wait_ge(sem("x_split"), DK)

            def turned(name, c):
                pe.wait_ge(sem(name + "_evA"), c + 1)
                pe.wait_ge(sem(name + "_evD"), c + 1)
                at_least(pe, sem(name + "_cpA"), c)
                at_least(pe, sem(name + "_cpD"), c)

            def qkv(i):
                for c in range(2):
                    at_least(pe, sem("qkv_evA"), i * 2 + c - 1)
                    at_least(pe, sem("qkv_evD"), i * 2 + c - 1)
                    for u in range(8):
                        unit(UNITS["qkv"] + 8 * c + u, i, 16, c, 2 * u, 99)
                        if u == 3 and not (isinstance(i, int) and i == 0 and c == 0):
                            turned("qkv", i * 2 + c - 1)
                            turn_blocks(s0, 4).then_inc(sem("qkv_tr"), 1)
            repeat(pe, 2, qkv)
            for c in range(2):
                pe.wait_ge(sem("qkv_evA"), 4 + c - 1)
                pe.wait_ge(sem("qkv_evD"), 4 + c - 1)
                for u in range(8):
                    unit(UNITS["qkv"] + 32 + 8 * c + u, 0, 8, c, 2 * u, 99)
                    if u == 3 and c == 0:
                        turned("qkv", 3)
                        turn_blocks(s0, 4).then_inc(sem("qkv_tr"), 1)
            for c in range(3):
                pe.wait_ge(sem("qkv_evA"), 6 + c - 1)
                pe.wait_ge(sem("qkv_evD"), 6 + c - 1)
                for u in range(8):
                    unit(UNITS["lat"] + 8 * c + u, 0, 8, c % 2, 2 * u, 99, width=448)
            pe.wait_ge(sem("qkv_evA"), 9)
            pe.wait_ge(sem("qkv_evD"), 9)
            pe.wait_ge(sem("qkv_cpA"), 4)
            pe.wait_ge(sem("qkv_cpD"), 4)
            for b in range(10):
                if b >= 8:
                    pe.wait_ge(sem("lat_lo"), 2)
                for t in range(T):
                    last = pe.transpose(aux[:, b // 2 % 4, (b % 2) * TOK + t * P:(b % 2) * TOK + (t + 1) * P],
                                        lat[:, t, b * P:(b + 1) * P], ident[:])
                if b % 2 == 1:
                    last.then_inc(sem("lat_tr"), 1)
            pe.wait_ge(sem("dve_stage"), DVE_STAGE["krot_done"])
            pe.wait_ge(sem("lat_lo"), 4)
            for t in range(T):
                last = pe.transpose(aux[:, 1, t * P:(t + 1) * P], krot[:, t], ident[:])
            last.then_inc(sem("kr_tr"), 1)
            pe.wait_ge(sem("lat_lo"), 10)
            pe.wait_ge(sem("kr_lo"), 1)

            def uq_turn(c):
                pe.wait_ge(sem("uq_evA"), c + 1)
                pe.wait_ge(sem("uq_rope"), c + 1)
                at_least(pe, sem("uq_cpA"), c)
                at_least(pe, sem("uq_cpD"), c)
                for hh in range(2):
                    for t in range(T):
                        pe.transpose(aux[:, 0, hh * TOK + t * P:hh * TOK + (t + 1) * P],
                                     s0[:, t, hh * QK_DIM:hh * QK_DIM + HD], ident[:])
                for t in range(T):
                    last = pe.transpose(aux[:, 1, t * P:(t + 1) * P], s1[:, t, 0:P], ident[:])
                last.then_inc(sem("uq_tr"), 1)
            for c in range(4):
                at_least(pe, sem("uq_evA"), c - 1)
                at_least(pe, sem("uq_evD"), c - 1)
                for u in range(3):
                    unit(UNITS["uq"] + 3 * c + u, 0, 4, c % 2, 2 * u, 99, latTh, latTl, 384)
                    if u == 1 and c:
                        uq_turn(c - 1)

            def ukv_turn(c):
                pe.wait_ge(sem("ukv_evA"), c + 1)
                pe.wait_ge(sem("ukv_evD"), c + 1)
                at_least(pe, sem("ukv_cpA"), c)
                turn_blocks(s0, 2, 2).then_inc(sem("ukv_tr"), 1)
            for c in range(4):
                if c < 2:
                    pe.wait_ge(sem("uq_evA"), 3 + c)
                    pe.wait_ge(sem("uq_evD"), 3 + c)
                else:
                    pe.wait_ge(sem("ukv_evA"), c - 1)
                    pe.wait_ge(sem("ukv_evD"), c - 1)
                for u in range(2):
                    slot, turn, n = slot_of(UNITS["ukv"] + 2 * c + u, 0, 4)
                    pe.wait_ge(lo_done, n + 1)
                    for k in range(2):
                        for t in range(T):
                            tok = slice(t * P, (t + 1) * P)
                            last = three(acc[:, c % 2, t], latTh[:, 6 + 2 * u + k, tok], latTl[:, 6 + 2 * u + k, tok],
                                         whi[:, slot, k * CW:(k + 1) * CW], wlo[:, slot, k * CW:(k + 1) * CW],
                                         start=u == 0 and k == 0, stop=False)
                    last.then_inc(used, 1)
                    if u == 0 and c == 0:
                        uq_turn(3)
                    if u == 0 and c:
                        ukv_turn(c - 1)
            ukv_turn(3)
            pe.wait_ge(sem("ukv_evA"), 4)
            pe.wait_ge(sem("ukv_evD"), 4)
            pe.wait_ge(sem("ukv_cpA"), 4)
            pe.wait_ge(sem("uq_cpD"), 4)

            def sb_logits(n, hh):
                pe.wait_ge(sem("sb_stage"), n + 1)
                at_least(pe, sem("sb_w"), n - 1)
                z = aux[:, hh]
                pe.matmul(z[:, 0:384], ident_r[:], mask_sb[:], start=True, stop=False, skip_group_check=True)
                three(z[:, 0:TOK], sth[:, hh, 1, 0:P], stl[:, hh, 1, 0:P], sth[:, hh, 0], stl[:, hh, 0], False, False)
                three(z[:, TOK:384], sth[:, hh, 1, P:TOK], stl[:, hh, 1, P:TOK], sth[:, hh, 0, P:TOK], stl[:, hh, 0, P:TOK],
                      False, False).then_inc(sem("sb_z"), 1)

            def sb_sums(n, hh):
                pe.wait_ge(sem("sb_split"), 2 * n + 1)
                z = aux[:, hh]
                for part in (sbh, sbl):
                    pe.matmul(z[:, 0:384], ntri[:], part[:], start=False, stop=False, skip_group_check=True)
                    last = pe.matmul(z[:, P:TOK], nones[:], part[:, TOK:384], start=False, stop=False,
                                     skip_group_check=True)
                last.then_inc(sem("sb_s"), 1)

            def sb_values(n, hh):
                pe.wait_ge(sem("sb_split"), 2 * n + 2)
                at_least(pe, sem("sb_y"), n - 1)
                y = aux[:, 2 + hh]
                three(y[:, 0:TOK], sth[:, hh, 2, 0:P], stl[:, hh, 2, 0:P], sbh[:, 0:TOK], sbl[:, 0:TOK], True, False)
                three(y[:, P:TOK], sth[:, hh, 2, P:TOK], stl[:, hh, 2, P:TOK], sbh[:, TOK:384], sbl[:, TOK:384],
                      False, False).then_inc(sem("sb_v"), 1)

            def gates_sb(i):
                at_least(pe, sem("gate_dve"), i)
                for u in range(8):
                    unit(UNITS["gate"] + u, i, 8, 0, 2 * u, 99)
                    for hh in range(2):
                        if u == 3 * hh:
                            sb_logits(i * 2 + hh, hh)
                        if u == 3 * hh + 2:
                            sb_sums(i * 2 + hh, hh)
                        if u == 3 * hh + 3:
                            sb_values(i * 2 + hh, hh)
            repeat(pe, 4, gates_sb)
            pe.wait_ge(sem("sb_y"), 8)

            def mla_logits(n, hh):
                pe.wait_ge(sem("mla_stage"), n + 1)
                at_least(pe, sem("mla_exp"), n)
                half = slice(hh * ROPE, (hh + 1) * ROPE)
                s = aux[:, 0]
                pe.matmul(s, ident_r[:], mask_mla[:], start=True, stop=False, skip_group_check=True)
                for t in range(T):
                    tok, cols = slice(t * P, (t + 1) * P), slice(t * TOK, (t + 1) * TOK)
                    three(s[:, cols], mqh[:, 0, tok], mql[:, 0, tok], mqh[:, 2], mql[:, 2], False, False)
                    last = three(s[:, cols], mqh[half, 1, tok], mql[half, 1, tok], krh[half, :], krl[half, :], False, False)
                last.then_inc(sem("mla_s"), 1)

            def mla_turn(n):
                pe.wait_ge(sem("mla_norm"), n + 1)
                at_least(pe, sem("mla_pl"), n)
                for kt in range(T):
                    for t in range(T):
                        last = pe.transpose(aux[:, 1, kt * TOK + t * P:kt * TOK + (t + 1) * P],
                                            mp[:, t, kt * P:(kt + 1) * P], ident[:])
                last.then_inc(sem("mla_tr"), 1)

            def mla_values(n):
                pe.wait_ge(sem("mla_pl"), n + 1)
                at_least(pe, sem("mla_y"), n)
                for kt in range(T):
                    rows_ = slice(kt * P, (kt + 1) * P)
                    last = three(aux[:, 2, 0:TOK], mqh[:, 3, rows_], mql[:, 3, rows_], mph[:, kt], mpl[:, kt],
                                 kt == 0, False)
                last.then_inc(sem("mla_v"), 1)

            def gates_mla(i):
                at_least(pe, sem("gate_dve"), i + 4)
                for u in range(8):
                    unit(UNITS["gate"] + 32 + u, i, 8, 0, 2 * u, 99)
                    for hh in range(2):
                        if u == 3 * hh:
                            mla_logits(i * 2 + hh, hh)
                        if u == 3 * hh + 1:
                            mla_turn(i * 2 + hh)
                        if u == 3 * hh + 2:
                            mla_values(i * 2 + hh)
            repeat(pe, 4, gates_mla)
            pe.wait_ge(sem("mla_y"), 8)
            pe.wait_ge(sem("gate_dve"), 8)

            def mix_turn(j):
                pe.wait_ge(sem("mix_dve"), j + 1)
                at_least(pe, sem("mix_cpA"), j)
                at_least(pe, sem("mix_cpD"), j)
                turn_blocks(s0, 4).then_inc(sem("mix_tr"), 1)

            def mix(i):
                at_least(pe, sem("mix_dve"), i)
                for u in range(8):
                    unit(UNITS["mix"] + u, i, 8, u // 4, 2 * u, 8, yTh, yTl)
                    if u == 3 and not (isinstance(i, int) and i == 0):
                        mix_turn(i - 1)
            repeat(pe, 4, mix)
            mix_turn(3)
            pe.wait_ge(sem("mix_cpA"), 4)
            pe.wait_ge(sem("mix_cpD"), 4)
            rows("out", DK, osh1, osl1)

            def turn_all(src, name):
                for b in range(8):
                    for k in range(2):
                        for t in range(T):
                            last = pe.transpose(banks[b][:, k * TOK + t * P:k * TOK + (t + 1) * P],
                                                h[:, t, (2 * b + k) * P:(2 * b + k + 1) * P], ident[:])
                    last.then_inc(sem(name), 1)

            pe.wait_ge(sem("mixer_done"), 2)
            turn_all(h, "ffn_tr")
            pe.wait_ge(sem("ffn_xlo"), DK)

            def up_turn(j):
                pe.wait_ge(sem("up_dve"), j + 1)
                at_least(pe, sem("up_cpA"), j)
                at_least(pe, sem("up_cpD"), j)
                turn_blocks(s0, 4).then_inc(sem("up_tr"), 1)

            def up(i):
                at_least(pe, sem("up_act"), i)
                for u in range(16):
                    if u == 8:
                        at_least(pe, sem("up_dve"), i)
                    unit(UNITS["up"] + u, i, 16, u // 8, 2 * (u % 8), 99)
                    if u == 3 and not (isinstance(i, int) and i == 0):
                        up_turn(i - 1)
            repeat(pe, 11, up)
            up_turn(10)
            pe.wait_ge(sem("up_cpA"), 11)
            pe.wait_ge(sem("up_cpD"), 11)
            rows("down", 44, osh2, osl2)

            pe.wait_ge(sem("ffn_done"), 2)
            turn_all(h, "a_tr")
            pe.wait_ge(sem("a_xlo"), 8)

            def a_turn(c):
                pe.wait_ge(sem("a_rot"), c + 1)
                at_least(pe, sem("a_cpA"), c)
                at_least(pe, sem("a_cpD"), c)
                turn_blocks(s1, 4).then_inc(sem("a_ctr"), 1)

            def a_q(i):
                for c in range(2):
                    at_least(pe, sem("a_evA"), i * 2 + c - 1)
                    at_least(pe, sem("a_evD"), i * 2 + c - 1)
                    for u in range(8):
                        unit(UNITS["aqkv"] + 8 * c + u, i, 16, c, 2 * u, 99)
                        if u == 7 and not (isinstance(i, int) and i == 0 and c == 0):
                            a_turn(i * 2 + c - 1)
            repeat(pe, 2, a_q)
            for c in range(4, 6):
                pe.wait_ge(sem("a_evA"), c - 1)
                pe.wait_ge(sem("a_evD"), c - 1)
                for u in range(8):
                    unit(UNITS["aqkv"] + 8 * c + u, 0, 8, c % 2, 2 * u, 99)
                    if u == 7:
                        a_turn(c - 1)
            pe.wait_ge(sem("a_evA"), 6)
            pe.wait_ge(sem("a_evD"), 6)
            pe.wait_ge(sem("a_cpA"), 5)
            pe.wait_ge(sem("a_cpD"), 5)

            def ag_logits(n, e):
                pe.wait_ge(sem("ag_q"), n + 1)
                at_least(pe, sem("ag_exp"), n - 1)
                for t in range(T):
                    tok = slice(t * P, (t + 1) * P)
                    last = three(aux[:, e % 2, t * TOK:(t + 1) * TOK], aqh[:, e % 2, tok], aql[:, e % 2, tok],
                                 kvh[:, 0], kvl[:, 0], True, False)
                last.then_inc(sem("ag_s"), 1)

            def ag_ptr(n, e):
                pe.wait_ge(sem("ag_exp"), n + 1)
                at_least(pe, sem("ag_pl"), n)
                for kt in range(T):
                    for t in range(T):
                        last = pe.transpose(aux[:, 2, kt * TOK + t * P:kt * TOK + (t + 1) * P],
                                            ap_[:, e % 2, t, kt * P:(kt + 1) * P], ident[:])
                last.then_inc(sem("ag_ptr"), 1)

            def ag_values(n, e):
                pe.wait_ge(sem("ag_pl"), n + 1)
                at_least(pe, sem("ag_o"), n)
                for t in range(T):
                    tok = slice(t * P, (t + 1) * P)
                    for kt in range(T):
                        last = three(aux[:, 3, t * P:(t + 1) * P], aph[:, kt, tok], apl[:, kt, tok],
                                     kvh[:, 1, kt * P:(kt + 1) * P], kvl[:, 1, kt * P:(kt + 1) * P], kt == 0, False)
                last.then_inc(sem("ag_v"), 1)

            def ag_turn(j):
                pe.wait_ge(sem("ag_gated"), j + 1)
                pe.wait_ge(sem("ag_exp"), j * 4 + 4)
                turn_blocks(s1, 4).then_inc(sem("ag_ctr"), 1)

            def ag(i):
                at_least(pe, sem("ag_silu"), i)
                for u in range(8):
                    unit(UNITS["ag"] + u, i, 8, 0, 2 * u, 99)
                    if u == 0 and not (isinstance(i, int) and i == 0):
                        ag_turn(i - 1)
                        pe.wait_ge(sem("ag_cpA"), i)
                        pe.wait_ge(sem("ag_cpD"), i)
                    if u % 2 == 0:
                        ag_logits(i * 4 + u // 2, u // 2)
                        if u:
                            ag_values(i * 4 + u // 2 - 1, u // 2 - 1)
                    else:
                        ag_ptr(i * 4 + u // 2, u // 2)
                ag_values(i * 4 + 3, 3)
            repeat(pe, 4, ag)
            ag_turn(3)
            pe.wait_ge(sem("ag_cpA"), 4)
            pe.wait_ge(sem("ag_cpD"), 4)
            rows("aout", DK, osh3, osl3)
            pe.wait_ge(sem("attn_done"), 2)
            turn_all(h, "r_tr")
            pe.wait_ge(sem("r_xlo"), 8)

            def r_turn(n):
                pe.wait_ge(sem("r_rot"), n + 1)
                at_least(pe, sem("r_qlo"), 2 * n)
                turn_blocks(s1, 4).then_inc(sem("r_ctr"), 1)

            def r_scores(n, hh):
                pe.wait_ge(sem("r_qlo"), n - hh * 0 + 0 if False else n)
                for jt in range(T):
                    keys = slice(jt * P, (jt + 1) * P)
                    for kt in range(2):
                        last = three(aux[:, 2 + hh, jt * TOK:(jt + 1) * TOK], rqh[:, 1, 2 * hh + kt, keys],
                                     rql[:, 1, 2 * hh + kt, keys], rqh[:, 0, 2 * hh + kt], rql[:, 0, 2 * hh + kt],
                                     kt == 0, False)
                last.then_inc(sem("r_s"), 1)

            def r_out(i, hh):
                pe.wait_ge(sem("r_pl"), i * 2 + hh + 1)
                pe.wait_ge(sem("r_evD"), i * 6 + hh + 3)
                for t in range(T):
                    tok = slice(t * P, (t + 1) * P)
                    for jt in range(T):
                        last = three(aux[:, 2 * hh + t], pth[:, hh, jt, tok], ptl[:, hh, jt, tok],
                                     rvh[:, hh, jt], rvl[:, hh, jt], jt == 0, False)
                last.then_inc(sem("r_o"), 1)

            def r_gturn(i, hh):
                pe.wait_ge(sem("r_evD"), i * 6 + hh + 5)
                turn_blocks(s0, 4).then_inc(sem("r_gtr"), 1)

            def ret(i):
                first = isinstance(i, int) and i == 0
                for c in range(6):
                    at_least(pe, sem("r_evA"), i * 6 + c - 1)
                    at_least(pe, sem("r_evD"), i * 6 + c - 1)
                    for u in range(8):
                        unit(UNITS["ret"] + 8 * c + u, i, 48, c % 2, 2 * u, 99)
                        if c == 0 and u == 3 and not first:
                            r_gturn(i - 1, 1)
                        if c == 1 and u == 4:
                            at_least(pe, sem("r_gcpA"), i * 2)
                            at_least(pe, sem("r_gcpD"), i * 2)
                            r_turn(i * 2)
                        if c == 2 and u == 4:
                            r_turn(i * 2 + 1)
                        if c == 3 and u in (0, 1):
                            r_scores(i * 4 + 4, u)
                        if c == 4 and u == 2:
                            r_out(i, 0)
                        if c == 4 and u == 5:
                            pe.wait_ge(sem("r_pl"), i * 2 + 2)
                            r_out(i, 1)
                        if c == 5 and u == 4:
                            pe.wait_ge(sem("r_norm"), i * 2 + 1)
                            r_gturn(i, 0)
            repeat(pe, 4, ret)
            pe.wait_ge(sem("r_gcpA"), 7)
            pe.wait_ge(sem("r_gcpD"), 7)
            r_gturn(3, 1)
            pe.wait_ge(sem("r_gcpA"), 8)
            pe.wait_ge(sem("r_gcpD"), 8)
            rows("rout", 32, osh4, osl4)

        @block.scalar
        def _(act):
            own = Own(act, act_own)
            A = nc.scalar.activation

            def split(base, i, per):
                slot, turn, n = slot_of(base + R, i, per)
                if isinstance(n, int) and n >= N_UNITS:
                    return
                act.wait_ge(landed[slot], 16 * (turn + 1))
                at_least(act, used, n - R + 1)
                A(whi[:, slot], raw[:, slot], ACT.Copy).then_inc(hi_done, 1)

            def rows(name, n_kt, src, sh):
                base = UNITS[name]

                def stage(kt, k):
                    at_least(act, used, base + 2 * kt - 2)
                    A(sh[:, k], src[:, kt] if isinstance(kt, int) else src[:, ds(kt, 1)].squeeze(1),
                      ACT.Copy).then_inc(sem(name + "_sthi"), 1)
                stage(0, 0)
                stage(1, 1)

                def body(i):
                    final = isinstance(i, int) and i == n_kt // 2 - 1
                    for k in range(2):
                        for half in range(2):
                            split(base + 2 * k + half, i, 4)
                        if not final:
                            stage(i * 2 + k + 2, k)
                repeat(act, n_kt // 2, body, last=True)

            for s in range(R):
                split(s - R, 0, R)
            act.wait_ge(sem("x_in"), 48)
            for k in range(DK):
                A(xh[:, k], xT_raw[:, k], ACT.Copy, scale=gpre_c[:, k:k + 1]).then_inc(sem("x_hi"), 1)
            for t in range(T):
                own.step(A(whole[1], x_tok[:, t], ACT.Square, accum_out=ssum[:, t:t + 1]))
            act.wait_ge(consts, 80)
            A(ident_r[:], ident[:], ACT.Copy).then_inc(sem("act_stage"), 1)
            act.wait_ge(sem("masks"), 64)
            A(ntri[:], s1[:, 0, 0:P], ACT.Copy)
            A(nones[:], s1[:, 0, P:2 * P], ACT.Copy)
            A(mask_sb[:], s1[:, 1, 0:384], ACT.Copy)
            own.step(A(mask_mla[:], s0[:, 0], ACT.Copy))
            act.wait_ge(sem("dve_stage"), DVE_STAGE["ang"])
            own.step(A(kk[:], ang[:], ACT.Sin))
            A(ang[:], angc[:], ACT.Sin).then_inc(sem("act_stage"), 1)

            act.wait_ge(sem("dve_stage"), DVE_STAGE["r1"])

            def ev(name, c, pair, base, dst, scale, src=None):
                act.wait_ge(used, base)
                A(dst, acc[:, pair, 0] if src is None else src, ACT.Copy, scale=scale).then_inc(sem(name), 1)

            def cp(name, dst, src, c):
                act.wait_ge(sem(name + "_tr"), c + 1)
                A(dst, src, ACT.Copy).then_inc(sem(name + "_cpA"), 1)

            def flat(x_):
                return x_.rearrange("p a b -> p (a b)")

            def qkv(i):
                for c in range(2):
                    for u in range(8):
                        split(UNITS["qkv"] + 8 * c + u, i, 16)
                        if u == 4 and not (isinstance(i, int) and i == 0 and c == 0):
                            cp("qkv", flat(qkT[:, ds(i * 8 + c * 4 - 4, 2)]), aux[:, 0], i * 2 + c - 1)
                    ev("qkv_evA", 0, c, i * 16 + 8 * (c + 1) + UNITS["qkv"], s0[:, 0], r1[:, 0:1])
            repeat(act, 2, qkv)
            for c in range(2):
                for u in range(8):
                    split(UNITS["qkv"] + 32 + 8 * c + u, 0, 8)
                    if u == 4 and c == 0:
                        cp("qkv", flat(qkT[:, 12:14]), aux[:, 0], 3)
                ev("qkv_evA", 0, c, UNITS["qkv"] + 32 + 8 * (c + 1), v_sb[:, 0, c * CW:(c + 1) * CW], r1[:, 0:1])
            for c in range(3):
                for u in range(8):
                    split(UNITS["lat"] + 8 * c + u, 0, 8)
                ev("qkv_evA", 0, 0, UNITS["lat"] + 8 * (c + 1), lat[:, 0, c * 448:(c + 1) * 448], r1[:, 0:1],
                   acc[:, c % 2, 0, 0:448])
            act.wait_ge(sem("qkv_evA"), 9)
            act.wait_ge(sem("qkv_evD"), 9)
            for t in range(T):
                own.step(A(s0[:, 0], lat[:, t, 0:CW], ACT.Square, accum_out=ssum[:, t:t + 1]))
                own.step(A(s0[:, 0, 0:256], lat[:, t, CW:Q_RANK], ACT.Square, accum_out=ssum[:, 2 + t:3 + t]))
                own.step(A(s0[:, 0], lat[:, t, Q_RANK:Q_RANK + KV_RANK], ACT.Square, accum_out=ssum[:, 4 + t:5 + t]))
            A(s0[:, 0, 0:1], s0[:, 0, 0:1], ACT.Copy).then_inc(sem("act_stage"), 1)
            for b in range(10):
                act.wait_ge(sem("lat_tr"), b // 2 + 1)
                A(latTh[:, b], aux[:, b // 2 % 4, (b % 2) * TOK:(b % 2 + 1) * TOK], ACT.Copy,
                  scale=glat_c[:, b:b + 1]).then_inc(sem("lat_hi"), 1)
            act.wait_ge(sem("kr_tr"), 1)
            A(krh[:], aux[:, 1, 0:TOK], ACT.Copy).then_inc(sem("act_stage"), 1)
            act.wait_ge(sem("dve_stage"), DVE_STAGE["rlat"])
            for c in range(4):
                for u in range(3):
                    split(UNITS["uq"] + 3 * c + u, 0, 4)
                    if u == 2 and c:
                        cp("uq", flat(qnT[:, 2 * c - 2:2 * c]), aux[:, 0], c - 1)
                ev("uq_evA", 0, 0, UNITS["uq"] + 3 * (c + 1), s0[:, 0, 0:384], rlat[:, 0:1], acc[:, c % 2, 0, 0:384])
            for c in range(4):
                for u in range(2):
                    split(UNITS["ukv"] + 2 * c + u, 0, 4)
                    if u == 1 and c == 0:
                        cp("uq", flat(qnT[:, 6:8]), aux[:, 0], 3)
                    if u == 1 and c:
                        cp("ukv", flat(knT[:, 2 * c - 2:2 * c]), aux[:, 2], c - 1)
                act.wait_ge(used, UNITS["ukv"] + 2 * (c + 1))
                src = acc[:, c % 2, 0].rearrange("p (h v d) -> p h v d", h=2, v=2)
                A(s0[:, 0, 0:256].rearrange("p (h d) -> p h d", h=2), src[:, :, 0], ACT.Copy, scale=rlat[:, 2:3])
                A(vm[:, 0, 2 * c:2 * c + 2], src[:, :, 1], ACT.Copy, scale=rlat[:, 2:3]).then_inc(sem("ukv_evA"), 1)
            cp("ukv", flat(knT[:, 6:8]), aux[:, 2], 3)

            act.wait_ge(sem("ukv_evA"), 4)

            def at(t_, n):
                return t_[:, n] if isinstance(n, int) else t_[:, ds(n, 1)].squeeze(1)

            def sb_stage(n, hh):
                at_least(act, sem("sb_v"), n - 1)
                A(sth[:, hh, 0], at(qkT, n), ACT.Copy, scale=HD ** -0.5)
                A(sth[:, hh, 1], at(qkT, n + 8), ACT.Copy)
                A(sth[:, hh, 2].rearrange("p (t d) -> p t d", t=T), v_sb[:, :, ds(n * HD, HD)],
                  ACT.Copy).then_inc(sem("sb_sthi"), 1)

            def sb_middle(n, hh):
                act.wait_ge(sem("sb_z"), n + 1)
                own.step(A(sbt[:], aux[:, hh, 0:384], ACT.Abs))
                own.step(A(sbt[:], sbt[:], ACT.Exp, scale=-1.0))
                A(sbt[:], sbt[:], ACT.Ln, bias=1.0).then_inc(sem("sb_ln"), 1)
                act.wait_ge(sem("sb_L"), n + 1)
                at_least(act, sem("sb_v"), n)
                A(sbh[:], sbL[:], ACT.Copy).then_inc(sem("sb_hi"), 1)

            def sb_weights(n, hh):
                act.wait_ge(sem("sb_s"), n + 1)
                own.step(A(sbt[:], aux[:, hh, 0:384], ACT.Exp))
                A(sbh[:], sbt[:], ACT.Copy).then_inc(sem("sb_w"), 1)

            def sb_out(n, hh):
                act.wait_ge(sem("sb_v"), n + 1)
                A(at(yTh, n), aux[:, 2 + hh, 0:TOK], ACT.Copy).then_inc(sem("sb_yh"), 1)

            def gate_bias(i):
                act.dma_start(bias_t[:], b_gate[ds(i * CW, CW)].partition_broadcast(P)).then_inc(sem("bias_in"), 16)

            def sigmoid(i):
                act.wait_ge(sem("gate_dve"), i + 1)
                A(s0[:], s0[:], ACT.Sigmoid).then_inc(sem("gate_act"), 1)
                act.wait_ge(sem("gate_act"), i + 1)
                act.dma_start(gates_dram[:, ds(i * CW, CW)].rearrange("(t p) n -> p t n", p=P),
                              s0[:]).then_inc(sem("gate_out"), 16)

            def gates_sb(i):
                gate_bias(i)
                sb_stage(i * 2, 0)
                sb_stage(i * 2 + 1, 1)
                for u in range(8):
                    split(UNITS["gate"] + u, i, 8)
                    for hh in range(2):
                        if u == 3 * hh + 1:
                            sb_middle(i * 2 + hh, hh)
                        if u == 3 * hh + 2:
                            sb_weights(i * 2 + hh, hh)
                        if u == 3 * hh + 4:
                            sb_out(i * 2 + hh, hh)
                sigmoid(i)
            repeat(act, 4, gates_sb, own)
            act.wait_ge(sem("sb_y"), 8)

            def mla_stage(n, hh, i):
                at_least(act, sem("mla_v"), n)
                A(mqh[:, 0], at(qnT, n), ACT.Copy)
                A(mqh[:, 1], at(qrT, i), ACT.Copy)
                A(mqh[:, 2], at(knT, n), ACT.Copy)
                A(mqh[:, 3].rearrange("p (t d) -> p t d", t=T), vm[:, :, ds(n, 1)].squeeze(2) if not isinstance(n, int) else vm[:, :, n],
                  ACT.Copy).then_inc(sem("mla_sthi"), 1)

            def mla_exp(n):
                act.wait_ge(sem("mla_max"), n + 1)
                for t in range(T):
                    last = A(mp[:, t], aux[:, 0, t * TOK:(t + 1) * TOK], ACT.Exp, bias=nmax[:, 0, t:t + 1],
                             accum_out=psum_[:, 0, t:t + 1])
                last.then_inc(sem("mla_exp"), 1)

            def mla_ph(n):
                act.wait_ge(sem("mla_tr"), n + 1)
                at_least(act, sem("mla_v"), n)
                A(flat(mph[:]), aux[:, 1], ACT.Copy).then_inc(sem("mla_ph"), 1)

            def mla_out(n):
                act.wait_ge(sem("mla_v"), n + 1)
                A(at(yTh, n + 8), aux[:, 2, 0:TOK], ACT.Copy).then_inc(sem("mla_yh"), 1)

            def gates_mla(i):
                gate_bias(i + 4)
                mla_stage(i * 2, 0, i)
                for u in range(8):
                    split(UNITS["gate"] + 32 + u, i, 8)
                    for hh in range(2):
                        if u == 3 * hh:
                            mla_exp(i * 2 + hh)
                        if u == 3 * hh + 1:
                            mla_ph(i * 2 + hh)
                        if u == 3 * hh + 2:
                            mla_out(i * 2 + hh)
                            if hh == 0:
                                mla_stage(i * 2 + 1, 1, i)
                sigmoid(i + 4)
            repeat(act, 4, gates_mla, own)

            def mix_cp(j):
                act.wait_ge(sem("mix_tr"), j + 1)
                A(flat(mixT[:, ds(j * 4, 2)]), aux[:, 0], ACT.Copy).then_inc(sem("mix_cpA"), 1)

            def mix(i):
                for u in range(8):
                    split(UNITS["mix"] + u, i, 8)
                    if u == 3:
                        at_least(act, sem("mix_dve"), i)
                        for b in range(2):
                            src = gates_dram[:, ds(i * CW + b * D, CW)].rearrange("(t p) n -> p t n", p=P)
                            act.dma_start(gt[:, b], src).then_inc(sem(f"gt_in{b}"), 16)
                    if u == 4 and not (isinstance(i, int) and i == 0):
                        mix_cp(i - 1)
            act.wait_ge(sem("mla_y"), 8)
            act.wait_ge(sem("gate_out"), 16 * 8)
            repeat(act, 4, mix)
            mix_cp(3)
            act.wait_ge(sem("mix_cpA"), 4)
            act.wait_ge(sem("mix_cpD"), 4)
            rows("out", DK, mixT, osh1)

            def squares_of_banks(done):
                act.wait_ge(used, done)
                for t in range(T):
                    A(xh_as_f32(t), whole[t], ACT.Square, accum_out=ssum[:, t:t + 1]).then_inc(sem("ss_banks"), 1)

            def xh_as_f32(t):
                return xl[:, 8 * t:8 * t + 8].rearrange("p a b -> p (a b)")

            squares_of_banks(UNITS["up"])
            for t in range(T):
                act.wait_ge(sem("mixer_done"), t + 1)
                A(xh_as_f32(t), h[:, t], ACT.Square, accum_out=ssum[:, 4 + t:5 + t]).then_inc(sem("ss_ffn"), 1)
            for b in range(8):
                act.wait_ge(sem("ffn_tr"), b + 1)
                for k in range(2):
                    A(xh[:, 2 * b + k], banks[b][:, k * TOK:(k + 1) * TOK], ACT.Copy,
                      scale=gffn_c[:, 2 * b + k:2 * b + k + 1]).then_inc(sem("ffn_xhi"), 1)
            act.wait_ge(sem("dve_stage"), DVE_STAGE["r2"])

            def up_cp(j):
                act.wait_ge(sem("up_tr"), j + 1)
                A(flat(actT[:, ds(j * 4, 2)]), aux[:, 0], ACT.Copy).then_inc(sem("up_cpA"), 1)

            def up(i):
                for u in range(16):
                    split(UNITS["up"] + u, i, 16)
                    if u == 4 and not (isinstance(i, int) and i == 0):
                        up_cp(i - 1)
                    if u == 7:
                        act.wait_ge(used, i * 16 + UNITS["up"] + 8)
                        for t in range(T):
                            last = A(s0[:, t], acc[:, 0, t], ACT.Silu, scale=r2[:, t:t + 1])
                        last.then_inc(sem("up_act"), 1)
            repeat(act, 11, up)
            up_cp(10)
            act.wait_ge(sem("up_cpA"), 11)
            act.wait_ge(sem("up_cpD"), 11)
            rows("down", 44, actT, osh2)
            squares_of_banks(UNITS["aqkv"])

            def hi_of_banks(name):
                for b in range(8):
                    act.wait_ge(sem(name + "_tr"), b + 1)
                    A(flat(xh[:, 2 * b:2 * b + 2]), banks[b], ACT.Copy).then_inc(sem(name + "_xhi"), 1)
            hi_of_banks("a")

            def a_ev(c, pair, done):
                act.wait_ge(used, done)
                at_least(act, sem("a_rot"), c)
                A(s0[:, 0], acc[:, pair, 0], ACT.Copy).then_inc(sem("a_evA"), 1)

            def a_sq(c):
                act.wait_ge(sem("a_evA"), c + 1)
                act.wait_ge(sem("a_evD"), c + 1)
                A(sqt[:], s0[:], ACT.Square).then_inc(sem("a_sq"), 1)

            def a_cp(c):
                act.wait_ge(sem("a_ctr"), c + 1)
                A(flat(aqT[:, ds(c * 4, 2)]), aux[:, 0], ACT.Copy).then_inc(sem("a_cpA"), 1)

            def a_q(i):
                for c in range(2):
                    for u in range(8):
                        split(UNITS["aqkv"] + 8 * c + u, i, 16)
                    if not (isinstance(i, int) and i == 0 and c == 0):
                        a_cp(i * 2 + c - 1)
                    a_ev(i * 2 + c, c, i * 16 + 8 * (c + 1) + UNITS["aqkv"])
                    a_sq(i * 2 + c)
            repeat(act, 2, a_q)
            for c in range(4, 6):
                for u in range(8):
                    split(UNITS["aqkv"] + 8 * c + u, 0, 8)
                a_cp(c - 1)
                if c == 4:
                    a_ev(c, 0, UNITS["aqkv"] + 40)
                    a_sq(c)
                else:
                    act.wait_ge(used, UNITS["aqkv"] + 48)
                    A(av[:, 0], acc[:, 1, 0], ACT.Copy).then_inc(sem("a_evA"), 1)
            act.wait_ge(sem("a_evA"), 6)
            act.wait_ge(sem("a_evD"), 6)
            act.wait_ge(sem("a_cpA"), 5)
            act.wait_ge(sem("a_cpD"), 5)

            def ag_q(n, e):
                at_least(act, sem("ag_s"), n - 1)
                A(aqh[:, e % 2], at(aqT, n), ACT.Copy).then_inc(sem("ag_qh"), 1)

            def ag_exp(n, e):
                act.wait_ge(sem("ag_max"), n + 1)
                at_least(act, sem("ag_ptr"), n - 1)
                for t in range(T):
                    last = A(ap_[:, e % 2, t], aux[:, e % 2, t * TOK:(t + 1) * TOK], ACT.Exp,
                             bias=nmax[:, e, t:t + 1], accum_out=psum_[:, e, t:t + 1])
                last.then_inc(sem("ag_exp"), 1)

            def ag_ph(n):
                act.wait_ge(sem("ag_ptr"), n + 1)
                at_least(act, sem("ag_v"), n)
                A(flat(aph[:]), aux[:, 2], ACT.Copy).then_inc(sem("ag_ph"), 1)

            def ag_cp(j):
                act.wait_ge(sem("ag_ctr"), j + 1)
                A(flat(agT[:, ds(j * 4, 2)]), aux[:, 0], ACT.Copy).then_inc(sem("ag_cpA"), 1)

            def ag(i):
                at_least(act, sem("ag_v"), i * 4)
                A(kvh[:, 0], at(aqT, i + 16), ACT.Copy)
                A(kvh[:, 1].rearrange("p (t d) -> p t d", t=T), av[:, :, ds(i * HD, HD)], ACT.Copy).then_inc(sem("ag_kvh"), 1)
                ag_q(i * 4, 0)
                ag_q(i * 4 + 1, 1)
                for u in range(8):
                    split(UNITS["ag"] + u, i, 8)
                    if u == 0 and not (isinstance(i, int) and i == 0):
                        ag_cp(i - 1)
                    if u % 2 == 0:
                        ag_exp(i * 4 + u // 2, u // 2)
                    else:
                        ag_ph(i * 4 + u // 2)
                        if u < 5:
                            ag_q(i * 4 + u // 2 + 2, u // 2 + 2)
                act.wait_ge(used, i * 8 + UNITS["ag"] + 8)
                A(s0[:], acc[:, 0], ACT.Silu).then_inc(sem("ag_silu"), 1)
            repeat(act, 4, ag)
            ag_cp(3)
            act.wait_ge(sem("ag_cpA"), 4)
            act.wait_ge(sem("ag_cpD"), 4)
            rows("aout", DK, agT, osh3)
            hi_of_banks("r")

            act.wait_ge(sem("tables_in"), 144)
            own.step(A(lg[:], lg[:], ACT.Exp, scale=-float(np.log(2.0))))
            act.wait_ge(act_own, own.base + own.k)
            A(lg[:], lg[:], ACT.Ln, scale=-1.0, bias=1.0).then_inc(sem("act_stage"), 1)

            def r_ev(i, c):
                act.wait_ge(used, i * 48 + 8 * (c + 1) + UNITS["ret"])
                if c == 0:
                    A(s0[:, 0], acc[:, 0, 0], ACT.Copy).then_inc(sem("r_evA"), 1)
                elif c == 1:
                    at_least(act, sem("r_rot"), i * 2 + 1)
                    A(s0[:, 0], acc[:, 1, 0], ACT.Copy, scale=R_QK ** -0.5).then_inc(sem("r_evA"), 1)
                elif c < 4:
                    at_least(act, sem("r_o"), i * 2 + c - 4 + 0 if not (isinstance(i, int) and i == 0) else 0)
                    A(rvh[:, c - 2], acc[:, c % 2], ACT.Copy).then_inc(sem("r_evA"), 1)
                else:
                    if c == 5:
                        act.wait_ge(sem("r_gtr"), i * 2 + 1)
                    A(s0[:], acc[:, c % 2], ACT.Silu).then_inc(sem("r_evA"), 1)

            def r_qhi(n, which):
                act.wait_ge(sem("r_ctr"), n + 1)
                for b in range(2):
                    A(flat(rqh[:, which, 2 * b:2 * b + 2]), aux[:, b], ACT.Copy).then_inc(sem("r_qhi"), 1)

            def r_decay_exp(n, hh):
                act.wait_ge(sem("r_dexp"), n + 1)
                A(dmat[:, hh], dmat[:, hh], ACT.Exp).then_inc(sem("r_d"), 1)

            def r_phi(n, hh):
                act.wait_ge(sem("r_p"), n + 1)
                A(pth[:, hh], dmat[:, hh], ACT.Copy).then_inc(sem("r_ph"), 1)

            def r_gcp(n):
                act.wait_ge(sem("r_gtr"), n + 1)
                A(flat(rgT[:, ds(n * 4, 2)]), aux[:, 0], ACT.Copy).then_inc(sem("r_gcpA"), 1)

            def ret(i):
                first = isinstance(i, int) and i == 0
                for c in range(6):
                    for u in range(8):
                        split(UNITS["ret"] + 8 * c + u, i, 48)
                        if c == 0 and u == 4 and not first:
                            r_gcp(i * 2 - 1)
                        if c == 1 and u == 2:
                            r_decay_exp(i * 2, 0)
                            r_decay_exp(i * 2 + 1, 1)
                        if c == 1 and u == 5:
                            r_qhi(i * 2, 0)
                        if c == 2 and u == 5:
                            r_qhi(i * 2 + 1, 1)
                        if c == 3 and u == 3:
                            r_phi(i * 2, 0)
                            r_phi(i * 2 + 1, 1)
                        if c == 5 and u == 5:
                            r_gcp(i * 2)
                    r_ev(i, c)
            repeat(act, 4, ret)
            r_gcp(7)
            act.wait_ge(sem("r_gcpA"), 8)
            act.wait_ge(sem("r_gcpD"), 8)
            rows("rout", 32, rgT, osh4)

        @block.vector
        def _(dve):
            own = Own(dve, dve_own)
            V = nc.vector

            def f32(x_):
                return x_.bitcast(F32)

            def flat(x_):
                return x_.rearrange("p a b -> p (a b)")

            def at(t_, n):
                return t_[:, n] if isinstance(n, int) else t_[:, ds(n, 1)].squeeze(1)

            def split(base, i, per):
                slot, turn, n = slot_of(base + R, i, per)
                if isinstance(n, int) and n >= N_UNITS:
                    return
                dve.wait_ge(hi_done, n + 1)
                at_least(dve, used, n - R + 1)
                V.tensor_tensor(wlo[:, slot], raw[:, slot], f32(whi[:, slot]), ALU.subtract).then_inc(lo_done, 1)

            def rows(name, n_kt, src, sh, sl):
                base = UNITS[name]

                def stage(kt, k):
                    dve.wait_ge(sem(name + "_sthi"), kt + 1)
                    at_least(dve, used, base + 2 * kt - 2)
                    V.tensor_tensor(sl[:, k], at(src, kt), f32(sh[:, k]), ALU.subtract).then_inc(sem(name + "_stage"), 1)
                stage(0, 0)
                stage(1, 1)

                def body(i):
                    final = isinstance(i, int) and i == n_kt // 2 - 1
                    for k in range(2):
                        for half in range(2):
                            split(base + 2 * k + half, i, 4)
                        if not final:
                            stage(i * 2 + k + 2, k)
                repeat(dve, n_kt // 2, body, last=True)

            def rsqrt(n):
                v, y, t_, ti = rs_v[:, 0:n], rs_y[:, 0:n], rs_t[:, 0:n], rs_i[:, 0:n]
                own.step(V.tensor_scalar(ti, v.bitcast(I32), 1, None, ALU.logical_shift_right))
                own.step(V.tensor_scalar(y.bitcast(I32), ti, -1.0, RSQRT_SEED, ALU.mult, ALU.add))
                for _ in range(3):
                    own.step(V.tensor_tensor(t_, y, y, ALU.mult))
                    own.step(V.scalar_tensor_tensor(t_, t_, -0.5, v, ALU.mult, ALU.mult))
                    own.step(V.scalar_tensor_tensor(y, t_, 1.5, y, ALU.add, ALU.mult))

            for s in range(R):
                split(s - R, 0, R)
            for k in range(DK):
                dve.wait_ge(sem("x_hi"), k + 1)
                V.scalar_tensor_tensor(xl[:, k], xT_raw[:, k], gpre_c[:, k:k + 1], f32(xh[:, k]),
                                       ALU.mult, ALU.subtract).then_inc(sem("x_split"), 1)
            dve.wait_ge(sem("act_stage"), ACT_STAGE["ss_x"])
            own.step(V.tensor_scalar(rs_v[:, 0:2], ssum[:, 0:2], 1.0 / D, EPS, ALU.mult, ALU.add))
            rsqrt(2)
            V.tensor_copy(r1[:], rs_y[:, 0:2]).then_inc(sem("dve_stage"), 1)
            dve.wait_ge(consts, 80)
            own.step(V.tensor_copy(pos_f[:], pos_i[:]))
            for t in range(T):
                own.mark(V.tensor_scalar(ang[:, t], invf[:], pos_f[:, t:t + 1], None, ALU.mult))
            own.wait()
            own.step(V.tensor_scalar(kk[:], ang[:], float(1 / (2 * np.pi)), ROUND, ALU.mult, ALU.add))
            own.step(V.tensor_scalar(kk[:], kk[:], -ROUND, None, ALU.add))
            rest = 2 * np.pi
            for bits in (5, 14, 23, 40):
                part = np.floor(rest * 2.0 ** bits) / 2.0 ** bits
                rest -= part
                own.step(V.scalar_tensor_tensor(ang[:], kk[:], float(-part), ang[:], ALU.mult, ALU.add))
            own.step(V.tensor_scalar(angc[:], ang[:], float(np.pi / 2), None, ALU.add))
            own.step(V.tensor_scalar(kk[:], angc[:], float(np.pi), float(-2 * np.pi), ALU.is_gt, ALU.mult))
            own.step(V.tensor_tensor(angc[:], angc[:], kk[:], ALU.add))
            own.step(V.tensor_scalar(angc[:], angc[:], PI_F, -PI_F, ALU.min, ALU.max))
            V.tensor_scalar(ang[:], ang[:], PI_F, -PI_F, ALU.min, ALU.max).then_inc(sem("dve_stage"), 1)
            dve.wait_ge(sem("act_stage"), ACT_STAGE["sines"])
            for half in range(2):
                cols = slice(half * 32, half * 32 + 32)
                own.mark(V.tensor_copy(cos_m[:, :, cols], ang[:]))
                own.mark(V.tensor_scalar(sin_m[:, :, cols], kk[:], -1.0 if half == 0 else 1.0, None, ALU.mult))
            own.wait()

            def ev(name, dst, src, scale, done):
                dve.wait_ge(used, done)
                V.tensor_scalar(dst, src, scale, None, ALU.mult).then_inc(sem(name), 1)

            def cp(name, dst, src, c):
                dve.wait_ge(sem(name + "_tr"), c + 1)
                V.tensor_copy(dst, src).then_inc(sem(name + "_cpD"), 1)

            dve.wait_ge(act_own, 3)

            def qkv(i):
                for c in range(2):
                    for u in range(8):
                        split(UNITS["qkv"] + 8 * c + u, i, 16)
                        if u == 4 and not (isinstance(i, int) and i == 0 and c == 0):
                            cp("qkv", flat(qkT[:, ds(i * 8 + c * 4 - 2, 2)]), aux[:, 1], i * 2 + c - 1)
                    ev("qkv_evD", s0[:, 1], acc[:, c, 1], r1[:, 1:2], i * 16 + 8 * (c + 1) + UNITS["qkv"])
            repeat(dve, 2, qkv)
            for c in range(2):
                for u in range(8):
                    split(UNITS["qkv"] + 32 + 8 * c + u, 0, 8)
                    if u == 4 and c == 0:
                        cp("qkv", flat(qkT[:, 14:16]), aux[:, 1], 3)
                ev("qkv_evD", v_sb[:, 1, c * CW:(c + 1) * CW], acc[:, c, 1], r1[:, 1:2], UNITS["qkv"] + 32 + 8 * (c + 1))
            for c in range(3):
                for u in range(8):
                    split(UNITS["lat"] + 8 * c + u, 0, 8)
                ev("qkv_evD", lat[:, 1, c * 448:(c + 1) * 448], acc[:, c % 2, 1, 0:448], r1[:, 1:2],
                   UNITS["lat"] + 8 * (c + 1))
            dve.wait_ge(sem("qkv_evA"), 9)
            dve.wait_ge(sem("qkv_evD"), 9)

            def rotate(dst, tmp, src, cos, sin, half):
                own.mark(V.tensor_tensor(dst, src, cos, ALU.mult))
                own.mark(V.tensor_tensor(tmp[:, :, 0:half], src[:, :, half:2 * half], sin[:, :, 0:half], ALU.mult))
                own.step(V.tensor_tensor(tmp[:, :, half:2 * half], src[:, :, 0:half], sin[:, :, half:2 * half], ALU.mult))
                return V.tensor_tensor(dst, dst, tmp, ALU.add)

            own.step(rotate(rtm2[:, :, 0:ROPE], rtmp[:, :, 0:ROPE], lat[:, :, 1280:1344], cos_m[:], sin_m[:], 32))
            V.tensor_copy(krot[:, :, 0:ROPE], rtm2[:, :, 0:ROPE])
            V.tensor_copy(krot[:, :, ROPE:P], rtm2[:, :, 0:ROPE]).then_inc(sem("dve_stage"), 1)
            dve.wait_ge(sem("act_stage"), ACT_STAGE["ss_lat"])
            own.step(V.tensor_tensor(ssum[:, 0:2], ssum[:, 0:2], ssum[:, 2:4], ALU.add))
            own.mark(V.tensor_scalar(rs_v[:, 0:2], ssum[:, 0:2], 1.0 / Q_RANK, EPS, ALU.mult, ALU.add))
            own.step(V.tensor_scalar(rs_v[:, 2:4], ssum[:, 4:6], 1.0 / KV_RANK, EPS, ALU.mult, ALU.add))
            rsqrt(4)
            own.mark(V.tensor_scalar(rlat[:, 0:2], rs_y[:, 0:2], QK_DIM ** -0.5, None, ALU.mult))
            own.step(V.tensor_copy(rlat[:, 2:4], rs_y[:, 2:4]))
            V.tensor_copy(mark[:], rs_y[:, 0:1]).then_inc(sem("dve_stage"), 1)
            for b in range(10):
                dve.wait_ge(sem("lat_hi"), b // 2 * 2 + 2)
                V.scalar_tensor_tensor(latTl[:, b], aux[:, b // 2 % 4, (b % 2) * TOK:(b % 2 + 1) * TOK],
                                       glat_c[:, b:b + 1], f32(latTh[:, b]), ALU.mult, ALU.subtract).then_inc(sem("lat_lo"), 1)
            dve.wait_ge(sem("act_stage"), ACT_STAGE["kr_hi"])
            V.tensor_tensor(krl[:], aux[:, 1, 0:TOK], f32(krh[:]), ALU.subtract).then_inc(sem("kr_lo"), 1)

            for c in range(4):
                for u in range(3):
                    split(UNITS["uq"] + 3 * c + u, 0, 4)
                    if u == 2 and c:
                        cp("uq", at(qrT, c - 1), aux[:, 1, 0:TOK], c - 1)
                ev("uq_evD", s0[:, 1, 0:384], acc[:, c % 2, 1, 0:384], rlat[:, 1:2], UNITS["uq"] + 3 * (c + 1))
                dve.wait_ge(sem("uq_evA"), c + 1)
                dve.wait_ge(sem("uq_evD"), c + 1)
                for t in range(T):
                    src = s0[:, t, 0:384].rearrange("p (h d) -> p h d", h=2)[:, :, HD:QK_DIM]
                    last = rotate(s1[:, t, 0:P].rearrange("p (h d) -> p h d", h=2),
                                  rtmp[:, t].rearrange("p (h d) -> p h d", h=2), src,
                                  cos_m[:, t:t + 1].broadcast_to([P, 2, ROPE]), sin_m[:, t:t + 1].broadcast_to([P, 2, ROPE]), 32)
                last.then_inc(sem("uq_rope"), 1)
            for c in range(4):
                for u in range(2):
                    split(UNITS["ukv"] + 2 * c + u, 0, 4)
                    if u == 1 and c == 0:
                        cp("uq", at(qrT, 3), aux[:, 1, 0:TOK], 3)
                dve.wait_ge(used, UNITS["ukv"] + 2 * (c + 1))
                at_least(dve, sem("ukv_tr"), c)
                src = acc[:, c % 2, 1].rearrange("p (h v d) -> p h v d", h=2, v=2)
                V.tensor_scalar(s0[:, 1, 0:256].rearrange("p (h d) -> p h d", h=2), src[:, :, 0], rlat[:, 3:4], None, ALU.mult)
                V.tensor_scalar(vm[:, 1, 2 * c:2 * c + 2], src[:, :, 1], rlat[:, 3:4], None, ALU.mult).then_inc(sem("ukv_evD"), 1)

            dve.wait_ge(sem("ukv_evD"), 4)

            def sb_stage(n, hh):
                dve.wait_ge(sem("sb_sthi"), n + 1)
                V.scalar_tensor_tensor(stl[:, hh, 0], at(qkT, n), HD ** -0.5, f32(sth[:, hh, 0]), ALU.mult, ALU.subtract)
                V.tensor_tensor(stl[:, hh, 1], at(qkT, n + 8), f32(sth[:, hh, 1]), ALU.subtract)
                V.tensor_tensor(stl[:, hh, 2].rearrange("p (t d) -> p t d", t=T), v_sb[:, :, ds(n * HD, HD)],
                                f32(sth[:, hh, 2]).rearrange("p (t d) -> p t d", t=T), ALU.subtract).then_inc(sem("sb_stage"), 1)

            def sb_middle(n, hh):
                z = aux[:, hh, 0:384]
                dve.wait_ge(sem("sb_ln"), n + 1)
                V.scalar_tensor_tensor(sbL[:], z, 0.0, sbt[:], ALU.max, ALU.add).then_inc(sem("sb_L"), 1)
                dve.wait_ge(sem("sb_hi"), n + 1)
                V.tensor_tensor(sbl[:], sbL[:], f32(sbh[:]), ALU.subtract).then_inc(sem("sb_split"), 1)

            def sb_weights(n, hh):
                dve.wait_ge(sem("sb_w"), n + 1)
                V.tensor_tensor(sbl[:], sbt[:], f32(sbh[:]), ALU.subtract).then_inc(sem("sb_split"), 1)

            def sb_out(n, hh):
                dve.wait_ge(sem("sb_yh"), n + 1)
                V.tensor_tensor(at(yTl, n), aux[:, 2 + hh, 0:TOK], f32(at(yTh, n)), ALU.subtract).then_inc(sem("sb_y"), 1)

            def gate_ev(i, done):
                dve.wait_ge(sem("bias_in"), 16 * (i + 1) if isinstance(i, int) else i * 16 + 16)
                at_least(dve, sem("gate_out"), i * 16)
                dve.wait_ge(used, done)
                for t in range(T):
                    last = V.scalar_tensor_tensor(s0[:, t], acc[:, 0, t], r1[:, t:t + 1], bias_t[:], ALU.mult, ALU.add)
                last.then_inc(sem("gate_dve"), 1)

            def gates_sb(i):
                sb_stage(i * 2, 0)
                sb_stage(i * 2 + 1, 1)
                for u in range(8):
                    split(UNITS["gate"] + u, i, 8)
                    for hh in range(2):
                        if u == 3 * hh + 1:
                            sb_middle(i * 2 + hh, hh)
                        if u == 3 * hh + 2:
                            sb_weights(i * 2 + hh, hh)
                        if u == 3 * hh + 4:
                            sb_out(i * 2 + hh, hh)
                gate_ev(i, i * 8 + UNITS["gate"] + 8)
            repeat(dve, 4, gates_sb)
            dve.wait_ge(sem("sb_y"), 8)

            def mla_stage(n, hh, i):
                dve.wait_ge(sem("mla_sthi"), n + 1)
                V.tensor_tensor(mql[:, 0], at(qnT, n), f32(mqh[:, 0]), ALU.subtract)
                V.tensor_tensor(mql[:, 1], at(qrT, i), f32(mqh[:, 1]), ALU.subtract)
                V.tensor_tensor(mql[:, 2], at(knT, n), f32(mqh[:, 2]), ALU.subtract)
                V.tensor_tensor(mql[:, 3].rearrange("p (t d) -> p t d", t=T),
                                vm[:, :, ds(n, 1)].squeeze(2) if not isinstance(n, int) else vm[:, :, n],
                                f32(mqh[:, 3]).rearrange("p (t d) -> p t d", t=T), ALU.subtract).then_inc(sem("mla_stage"), 1)

            def mla_softmax(n):
                dve.wait_ge(sem("mla_s"), n + 1)
                V.tensor_reduce(nmax[:, 0], aux[:, 0].rearrange("p (t k) -> p t k", t=T), AX.X, ALU.max,
                                negate=True).then_inc(sem("mla_max"), 1)
                dve.wait_ge(sem("mla_exp"), n + 1)
                own.step(V.reciprocal(prec[:, 0], psum_[:, 0]))
                for t in range(T):
                    last = V.tensor_scalar(mp[:, t], mp[:, t], prec[:, 0, t:t + 1], None, ALU.mult)
                last.then_inc(sem("mla_norm"), 1)

            def mla_pl(n):
                dve.wait_ge(sem("mla_ph"), n + 1)
                V.tensor_tensor(flat(mpl[:]), aux[:, 1], f32(flat(mph[:])), ALU.subtract).then_inc(sem("mla_pl"), 1)

            def mla_out(n):
                dve.wait_ge(sem("mla_yh"), n + 1)
                V.tensor_tensor(at(yTl, n + 8), aux[:, 2, 0:TOK], f32(at(yTh, n + 8)), ALU.subtract).then_inc(sem("mla_y"), 1)

            def gates_mla(i):
                mla_stage(i * 2, 0, i)
                for u in range(8):
                    split(UNITS["gate"] + 32 + u, i, 8)
                    for hh in range(2):
                        if u == 3 * hh:
                            mla_softmax(i * 2 + hh)
                        if u == 3 * hh + 1:
                            mla_pl(i * 2 + hh)
                        if u == 3 * hh + 2:
                            mla_out(i * 2 + hh)
                            if hh == 0:
                                mla_stage(i * 2 + 1, 1, i)
                gate_ev(i + 4, i * 8 + UNITS["gate"] + 40)
            repeat(dve, 4, gates_mla, own)
            dve.wait_ge(sem("mla_y"), 8)
            V.tensor_copy(mark[:], rs_y[:, 0:1]).then_inc(sem("dve_stage"), 1)

            def mix_cp(j):
                dve.wait_ge(sem("mix_tr"), j + 1)
                V.tensor_copy(flat(mixT[:, ds(j * 4 + 2, 2)]), aux[:, 1]).then_inc(sem("mix_cpD"), 1)

            def mix(i):
                for u in range(8):
                    split(UNITS["mix"] + u, i, 8)
                    if u == 4 and not (isinstance(i, int) and i == 0):
                        mix_cp(i - 1)
                for b in range(2):
                    dve.wait_ge(sem(f"gt_in{b}"), i * 16 + 16)
                dve.wait_ge(used, i * 8 + UNITS["mix"] + 8)
                at_least(dve, sem("gate_out"), 16 * 8)
                for t in range(T):
                    own.mark(V.tensor_tensor(s0[:, t], acc[:, 0, t], gt[:, 0, t], ALU.mult))
                    own.mark(V.tensor_tensor(s1[:, t], acc[:, 1, t], gt[:, 1, t], ALU.mult))
                own.wait()
                V.tensor_tensor(s0[:], s0[:], s1[:], ALU.add).then_inc(sem("mix_dve"), 1)
            repeat(dve, 4, mix, own)
            mix_cp(3)
            dve.wait_ge(sem("mix_cpA"), 4)
            dve.wait_ge(sem("mix_cpD"), 4)
            rows("out", DK, mixT, osh1, osl1)

            def add_normed(n_before, gain, tmp, done):
                for t in range(T):
                    dve.wait_ge(sem("ss_banks"), n_before + t + 1)
                    own.step(V.tensor_scalar(rs_v[:, 0:1], ssum[:, t:t + 1], 1.0 / D, EPS, ALU.mult, ALU.add))
                    rsqrt(1)
                    own.step(V.scalar_tensor_tensor(tmp[:], whole[t], rs_y[:, 0:1], gain[:], ALU.mult, ALU.mult))
                    V.tensor_tensor(h[:, t], h[:, t], tmp[:], ALU.add).then_inc(sem(done), 1)

            dve.wait_ge(sem("x_again"), 16)
            dve.wait_ge(sem("gains_in"), 16)
            add_normed(0, gbc1, tmp1, "mixer_done")
            for b in range(DK):
                dve.wait_ge(sem("ffn_xhi"), b // 2 * 2 + 2)
                dve.wait_ge(sem("ss_ffn"), 2)
                V.scalar_tensor_tensor(xl[:, b], banks[b // 2][:, (b % 2) * TOK:(b % 2 + 1) * TOK], gffn_c[:, b:b + 1],
                                       f32(xh[:, b]), ALU.mult, ALU.subtract).then_inc(sem("ffn_xlo"), 1)
            own.step(V.tensor_scalar(rs_v[:, 0:2], ssum[:, 4:6], 1.0 / D, EPS, ALU.mult, ALU.add))
            rsqrt(2)
            own.step(V.tensor_copy(r2[:], rs_y[:, 0:2]))
            V.tensor_copy(mark[:], rs_y[:, 0:1]).then_inc(sem("dve_stage"), 1)

            def up_cp(j):
                dve.wait_ge(sem("up_tr"), j + 1)
                V.tensor_copy(flat(actT[:, ds(j * 4 + 2, 2)]), aux[:, 1]).then_inc(sem("up_cpD"), 1)

            def up(i):
                for u in range(16):
                    split(UNITS["up"] + u, i, 16)
                    if u == 4 and not (isinstance(i, int) and i == 0):
                        up_cp(i - 1)
                dve.wait_ge(used, i * 16 + UNITS["up"] + 16)
                dve.wait_ge(sem("up_act"), i + 1)
                for t in range(T):
                    last = V.scalar_tensor_tensor(s0[:, t], acc[:, 1, t], r2[:, t:t + 1], s0[:, t], ALU.mult, ALU.mult)
                last.then_inc(sem("up_dve"), 1)
            repeat(dve, 11, up)
            up_cp(10)
            dve.wait_ge(sem("up_cpA"), 11)
            dve.wait_ge(sem("up_cpD"), 11)
            rows("down", 44, actT, osh2, osl2)
            dve.wait_ge(sem("gains_in"), 32)
            add_normed(2, gbc2, tmp2, "ffn_done")

            def lo_of_banks(name):
                for b in range(8):
                    dve.wait_ge(sem(name + "_xhi"), b + 1)
                    V.tensor_tensor(flat(xl[:, 2 * b:2 * b + 2]), banks[b], f32(flat(xh[:, 2 * b:2 * b + 2])),
                                    ALU.subtract).then_inc(sem(name + "_xlo"), 1)
            lo_of_banks("a")

            dve.wait_ge(sem("tables_in"), 64)
            for w in range(2):
                gain = gtab[:, w:w + 1]
                own.mark(V.tensor_tensor(cgs[:, 2 * w], ctab[:, 0], gain.broadcast_to([P, T, HD]), ALU.mult))
                for q in range(4):
                    other = q ^ 1
                    own.mark(V.tensor_tensor(cgs[:, 2 * w + 1, :, 32 * q:32 * q + 32], ctab[:, 1, :, 32 * q:32 * q + 32],
                                             gain[:, :, 32 * other:32 * other + 32].broadcast_to([P, T, 32]), ALU.mult))
            own.wait()

            def a_ev(c, pair, done):
                dve.wait_ge(used, done)
                V.tensor_copy(s0[:, 1], acc[:, pair, 1]).then_inc(sem("a_evD"), 1)

            def heads_rotate(dst, tmp, src, cos, sin, heads, quarter):
                n = 4 * quarter
                dv, sv = (x_.rearrange("p (h d) -> p h d", h=heads) for x_ in (dst, src))
                tv = tmp.rearrange("p (h d) -> p h d", h=heads)
                own.mark(V.tensor_tensor(dv, sv, cos.broadcast_to([P, heads, n]), ALU.mult))
                for q in range(4):
                    other = (q ^ 1) * quarter
                    own.mark(V.tensor_tensor(tv[:, :, q * quarter:(q + 1) * quarter], sv[:, :, other:other + quarter],
                                             sin[:, :, q * quarter:(q + 1) * quarter].broadcast_to([P, heads, quarter]),
                                             ALU.mult))
                own.wait()
                return V.tensor_tensor(dst, dst, tmp, ALU.add)

            def a_norm_rotate(c, w):
                dve.wait_ge(sem("a_sq"), c + 1)
                at_least(dve, sem("a_ctr"), c)
                own.step(V.tensor_reduce(ssum[:, 0:8].rearrange("p (t h) -> p t h", t=T),
                                         sqt[:].rearrange("p t (h d) -> p t h d", h=4), AX.X, ALU.add))
                own.step(V.tensor_scalar(rs_v[:, 0:8], ssum[:, 0:8], 1.0 / HD, EPS, ALU.mult, ALU.add))
                rsqrt(8)
                if w == 0:
                    own.step(V.tensor_scalar(rs_y[:, 0:8], rs_y[:, 0:8], HD ** -0.5, None, ALU.mult))
                for t in range(T):
                    own.step(heads_rotate(s1[:, t], sqt[:, t], s0[:, t], cgs[:, 2 * w, t:t + 1], cgs[:, 2 * w + 1, t:t + 1], 4, 32))
                    v = s1[:, t].rearrange("p (h d) -> p h d", h=4)
                    last = V.tensor_tensor(v, v, rs_y[:, 4 * t:4 * t + 4].unsqueeze(2).broadcast_to([P, 4, HD]), ALU.mult)
                last.then_inc(sem("a_rot"), 1)

            def a_cp(c):
                dve.wait_ge(sem("a_ctr"), c + 1)
                V.tensor_copy(flat(aqT[:, ds(c * 4 + 2, 2)]), aux[:, 1]).then_inc(sem("a_cpD"), 1)

            def a_part(base, i, per, c, skip_cp, w):
                for u in range(8):
                    split(base + u, i, per)
                    if u == 0 and not skip_cp:
                        a_norm_rotate(c - 1, w)
                if not skip_cp:
                    a_cp(c - 1)

            def a_q(i):
                for c in range(2):
                    n = i * 2 + c
                    if c == 0 and isinstance(i, int) and i == 0:
                        for u in range(8):
                            split(UNITS["aqkv"] + u, 0, 16)
                    else:
                        a_part(UNITS["aqkv"] + 8 * c, i, 16, n, False, 0)
                    a_ev(n, c, i * 16 + 8 * (c + 1) + UNITS["aqkv"])
            for i in range(2):
                a_q(i)
            a_part(UNITS["aqkv"] + 32, 0, 8, 4, False, 0)
            a_ev(4, 0, UNITS["aqkv"] + 40)
            a_part(UNITS["aqkv"] + 40, 0, 8, 5, False, 1)
            dve.wait_ge(used, UNITS["aqkv"] + 48)
            V.tensor_copy(av[:, 1], acc[:, 1, 1]).then_inc(sem("a_evD"), 1)
            dve.wait_ge(sem("a_evA"), 6)
            dve.wait_ge(sem("a_evD"), 6)
            dve.wait_ge(sem("a_cpA"), 5)
            dve.wait_ge(sem("a_cpD"), 5)

            def ag_q(n, e):
                dve.wait_ge(sem("ag_qh"), n + 1)
                V.tensor_tensor(aql[:, e % 2], at(aqT, n), f32(aqh[:, e % 2]), ALU.subtract).then_inc(sem("ag_q"), 1)

            def ag_max(n, e):
                dve.wait_ge(sem("ag_s"), n + 1)
                V.tensor_reduce(nmax[:, e], aux[:, e % 2].rearrange("p (t k) -> p t k", t=T), AX.X, ALU.max,
                                negate=True).then_inc(sem("ag_max"), 1)
                dve.wait_ge(sem("ag_exp"), n + 1)
                V.reciprocal(prec[:, e], psum_[:, e])

            def ag_pl(n):
                dve.wait_ge(sem("ag_ph"), n + 1)
                V.tensor_tensor(flat(apl[:]), aux[:, 2], f32(flat(aph[:])), ALU.subtract).then_inc(sem("ag_pl"), 1)

            def ag_out(n, e):
                dve.wait_ge(sem("ag_v"), n + 1)
                own.wait()
                for t in range(T):
                    last = V.tensor_scalar(obuf[:, t, e * HD:(e + 1) * HD], aux[:, 3, t * P:(t + 1) * P],
                                           prec[:, e, t:t + 1], None, ALU.mult)
                last.then_inc(sem("ag_o"), 1)

            def ag_cp(j):
                dve.wait_ge(sem("ag_ctr"), j + 1)
                V.tensor_copy(flat(agT[:, ds(j * 4 + 2, 2)]), aux[:, 1]).then_inc(sem("ag_cpD"), 1)

            def ag(i):
                dve.wait_ge(sem("ag_kvh"), i + 1)
                V.tensor_tensor(kvl[:, 0], at(aqT, i + 16), f32(kvh[:, 0]), ALU.subtract)
                V.tensor_tensor(kvl[:, 1].rearrange("p (t d) -> p t d", t=T), av[:, :, ds(i * HD, HD)],
                                f32(kvh[:, 1]).rearrange("p (t d) -> p t d", t=T), ALU.subtract)
                ag_q(i * 4, 0)
                ag_q(i * 4 + 1, 1)
                for u in range(8):
                    split(UNITS["ag"] + u, i, 8)
                    if u == 0 and not (isinstance(i, int) and i == 0):
                        ag_cp(i - 1)
                    if u % 2 == 0:
                        ag_max(i * 4 + u // 2, u // 2)
                        if u:
                            ag_out(i * 4 + u // 2 - 1, u // 2 - 1)
                    else:
                        ag_pl(i * 4 + u // 2)
                        if u < 5:
                            ag_q(i * 4 + u // 2 + 2, u // 2 + 2)
                ag_out(i * 4 + 3, 3)
                dve.wait_ge(sem("ag_o"), i * 4 + 4)
                dve.wait_ge(sem("ag_silu"), i + 1)
                V.tensor_tensor(s1[:], s0[:], obuf[:], ALU.mult).then_inc(sem("ag_gated"), 1)
            repeat(dve, 4, ag)
            ag_cp(3)
            V.tensor_copy(mark[:], rs_y[:, 0:1]).then_inc(sem("dve_stage"), 1)
            dve.wait_ge(sem("ag_cpA"), 4)
            dve.wait_ge(sem("ag_cpD"), 4)
            rows("aout", DK, agT, osh3, osl3)

            def add_layer_norm(done_units, tab, done):
                dve.wait_ge(used, done_units)
                for t in range(T):
                    own.step(V.scalar_tensor_tensor(h[:, t], h[:, t], float(ALPHA), whole[t], ALU.mult, ALU.add))
                    for b in range(4):
                        own.mark(V.bn_stats(stats[:, 0, b], h[:, t, b * CW:(b + 1) * CW]))
                    own.wait()
                    own.step(V.bn_aggr(mv[:, 0], stats[:, 0].rearrange("p a b -> p (a b)")))
                    own.step(V.tensor_scalar(rs_v[:, 0:1], mv[:, 0, 1:2], LN_EPS, None, ALU.add))
                    rsqrt(1)
                    own.step(V.tensor_scalar(h[:, t], h[:, t], mv[:, 0, 0:1], rs_y[:, 0:1], ALU.subtract, ALU.mult))
                    own.step(V.tensor_tensor(h[:, t], h[:, t], tab[:, 0], ALU.mult))
                    V.tensor_tensor(h[:, t], h[:, t], tab[:, 1], ALU.add).then_inc(sem(done), 1)

            dve.wait_ge(sem("gains_in"), 64)
            add_layer_norm(UNITS["ret"], lng1, "attn_done")
            lo_of_banks("r")

            dve.wait_ge(sem("tables_in"), 144)
            dve.wait_ge(sem("act_stage"), ACT_STAGE["lg"])

            def r_ev(i, c):
                dve.wait_ge(used, i * 48 + 8 * (c + 1) + UNITS["ret"])
                if c == 0:
                    at_least(dve, sem("r_gtr"), i * 2)
                    V.tensor_copy(s0[:, 1], acc[:, 0, 1]).then_inc(sem("r_evD"), 1)
                elif c == 1:
                    V.tensor_scalar(s0[:, 1], acc[:, 1, 1], R_QK ** -0.5, None, ALU.mult).then_inc(sem("r_evD"), 1)
                elif c < 4:
                    dve.wait_ge(sem("r_evA"), i * 6 + c + 1)
                    V.tensor_tensor(rvl[:, c - 2], acc[:, c % 2], f32(rvh[:, c - 2]), ALU.subtract).then_inc(sem("r_evD"), 1)
                else:
                    dve.wait_ge(sem("r_evA"), i * 6 + c + 1)
                    dve.wait_ge(sem("r_norm"), i * 2 + c - 3)
                    V.tensor_tensor(s0[:], s0[:], onorm[:, c - 4], ALU.mult).then_inc(sem("r_evD"), 1)

            def r_rotate(n):
                dve.wait_ge(sem("r_evA"), 1)
                for t in range(T):
                    last = heads_rotate(s1[:, t], rt[:], s0[:, t], rcs[:, 0, t:t + 1], rcs[:, 1, t:t + 1], 2, 64)
                    if t == 0:
                        own.step(last)
                last.then_inc(sem("r_rot"), 1)

            def r_decay_arg(n, hh):
                head = n
                own.step(V.tensor_scalar(dmat[:, hh], dist[:, 0], at2(lg, head), None, ALU.mult))
                V.scalar_tensor_tensor(dmat[:, hh], dist[:, 1], at2(lg, head + 8), dmat[:, hh], ALU.mult,
                                       ALU.add).then_inc(sem("r_dexp"), 1)

            def at2(t_, n):
                return t_[:, n:n + 1] if isinstance(n, int) else t_[:, ds(n, 1)]

            def r_qlo(n, which):
                for b in range(2):
                    dve.wait_ge(sem("r_qhi"), n * 2 + b + 1)
                    V.tensor_tensor(flat(rql[:, which, 2 * b:2 * b + 2]), aux[:, b],
                                    f32(flat(rqh[:, which, 2 * b:2 * b + 2])), ALU.subtract).then_inc(sem("r_qlo"), 1)

            def r_decayed(n, hh):
                dve.wait_ge(sem("r_s"), n + 1)
                dve.wait_ge(sem("r_d"), n + 1)
                V.tensor_tensor(flat(dmat[:, hh]), aux[:, 2 + hh], flat(dmat[:, hh]), ALU.mult).then_inc(sem("r_p"), 1)

            def r_plo(n, hh):
                dve.wait_ge(sem("r_ph"), n + 1)
                V.tensor_tensor(ptl[:, hh], dmat[:, hh], f32(pth[:, hh]), ALU.subtract).then_inc(sem("r_pl"), 1)

            def r_norm(n, hh):
                dve.wait_ge(sem("r_o"), n + 1)
                for t in range(T):
                    own.mark(V.bn_stats(stats[:, t, 0], aux[:, 2 * hh + t]))
                own.wait()
                V.tensor_copy(rs_t[:, 0:1], rs_y[:, 0:1])
                for t in range(T):
                    own.mark(V.bn_aggr(mv[:, t], stats[:, t, 0]))
                own.wait()
                own.step(V.tensor_scalar(rs_v[:, 0:2], mv[:, :, 1], LN_EPS, None, ALU.add))
                rsqrt(2)
                for t in range(T):
                    last = V.tensor_scalar(onorm[:, hh, t], aux[:, 2 * hh + t], mv[:, t, 0:1], rs_y[:, t:t + 1],
                                           ALU.subtract, ALU.mult)
                last.then_inc(sem("r_norm"), 1)

            def r_gcp(n):
                dve.wait_ge(sem("r_gtr"), n + 1)
                V.tensor_copy(flat(rgT[:, ds(n * 4 + 2, 2)]), aux[:, 1]).then_inc(sem("r_gcpD"), 1)

            def ret(i):
                first = isinstance(i, int) and i == 0
                for c in range(6):
                    for u in range(8):
                        split(UNITS["ret"] + 8 * c + u, i, 48)
                        if c == 0 and u == 4 and not first:
                            r_gcp(i * 2 - 1)
                        if c == 1 and u == 0:
                            dve.wait_ge(sem("r_evA"), i * 6 + 1)
                            dve.wait_ge(sem("r_evD"), i * 6 + 1)
                            r_rotate(i * 2)
                            r_decay_arg(i * 2, 0)
                            r_decay_arg(i * 2 + 1, 1)
                        if c == 1 and u == 5:
                            r_qlo(i * 2, 0)
                        if c == 2 and u == 0:
                            dve.wait_ge(sem("r_evA"), i * 6 + 2)
                            dve.wait_ge(sem("r_evD"), i * 6 + 2)
                            r_rotate(i * 2 + 1)
                        if c == 2 and u == 5:
                            r_qlo(i * 2 + 1, 1)
                        if c == 3 and u == 2:
                            r_decayed(i * 2, 0)
                            r_decayed(i * 2 + 1, 1)
                        if c == 3 and u == 4:
                            r_plo(i * 2, 0)
                            r_plo(i * 2 + 1, 1)
                        if c == 4 and u == 4:
                            r_norm(i * 2, 0)
                        if c == 4 and u == 6:
                            r_norm(i * 2 + 1, 1)
                        if c == 5 and u == 5:
                            r_gcp(i * 2)
                    r_ev(i, c)
            repeat(dve, 4, ret, own)
            r_gcp(7)
            V.tensor_copy(mark[:], rs_y[:, 0:1]).then_inc(sem("dve_stage"), 1)
            dve.wait_ge(sem("r_gcpA"), 8)
            dve.wait_ge(sem("r_gcpD"), 8)
            rows("rout", 32, rgT, osh4, osl4)
            dve.wait_ge(sem("gains_in"), 96)
            add_layer_norm(N_UNITS, lng2, "result")


def constants():
    f = np.float32
    j, q = np.arange(P)[:, None], np.arange(P)[None, :]
    mask_sb = np.zeros((P, 3 * P), f)
    mask_sb[:, 0:P] = np.where(j >= q, BIG, 0)
    mask_sb[:, 2 * P:] = np.where(j >= q, BIG, 0)
    mask_mla = np.zeros((P, T, TOK), f)
    for t in range(T):
        rows, keys = t * P + np.arange(P)[:, None], np.arange(TOK)[None, :]
        mask_mla[:, t] = np.where(keys // 64 <= rows // 64, 0, BIG)
    half = ROPE // 2
    invf = (10000.0 ** (-np.arange(half) / half)).astype(f)

    def axial(dim):
        row = np.repeat(np.arange(TOK // 64, dtype=f), 64)
        col = np.tile(np.arange(64, dtype=f), TOK // 64)
        hf = dim // 2
        inv = (10000.0 ** (-np.arange(0, hf, 2) / hf)).astype(f)
        ar, ac = row[:, None] * inv, col[:, None] * inv
        sign = np.concatenate([-np.ones(dim // 4), np.ones(dim // 4)] * 2).astype(f)
        a = np.concatenate([ar, ar, ac, ac], axis=-1).astype(np.float64)
        return np.cos(a).astype(f), (np.sin(a) * sign).astype(f)

    cos_a, sin_a = axial(HD)
    cos_r, sin_r = axial(R_QK)
    keys, qs = np.arange(TOK)[:, None], np.arange(TOK)[None, :]
    return {
        "c_ident": np.eye(P, dtype=f), "c_ntri": -(j >= q).astype(f), "c_nones": -np.ones((P, P), f),
        "c_mask_sb": mask_sb, "c_mask_mla": mask_mla.reshape(P, T * TOK), "c_invf": invf,
        "c_cos_a": cos_a, "c_sin_a": sin_a, "c_cos_r": cos_r, "c_sin_r": sin_r,
        "c_dist_f": np.maximum(qs - keys, 0).astype(f), "c_dist_b": np.maximum(keys - qs, 0).astype(f),
    }


def kernel(**inputs):
    import concourse.bacc as bacc
    from concourse.bass_utils import run_bass_kernel_spmd

    a = {k: np.asarray(v) for k, v in inputs.items()}

    def columns(v):
        return v.reshape(-1, P).T

    arrays = {
        "x": a["x"][0], "xT": a["x"][0].T, "positions": columns(a["positions"][0]),
        "g_pre": columns(a["norm_pre_mix"][0]), "w_in": a["w_in"][0], "b_gate": a["b_gate"][0],
        "g_lat": columns(np.concatenate([a["q_norm"][0], a["kv_norm"][0]])),
        "w_uq": a["w_uq"][0], "w_ukv": a["w_ukv"][0], "w_o_sb": a["w_o_sb"][0], "w_o_mla": a["w_o_mla"][0],
        "w_out": a["w_out"][0], "g_post_mix": a["norm_post_mix"][0], "g_ffn": columns(a["norm_pre_ffn"][0]),
        "w_gate_up": a["w_gate_up"][0], "w_down": a["w_down"][0], "g_post_ffn": a["norm_post_ffn"][0],
        "a_w_in": a["attn_w_in_2"][0], "a_q_gain": a["attn_q_gain_2"][0], "a_k_gain": a["attn_k_gain_2"][0],
        "a_w_out": a["attn_w_out_2"][0], "r_w_in": a["ret_w_in_2"][0],
        "r_decay": a["ret_decay_exp_2"][0].reshape(-1), "r_w_out": a["ret_w_out_2"][0],
        "ln_gain": a["ln_gain_2"], "ln_bias": a["ln_bias_2"],
    }
    arrays.update(constants())
    arrays = {k: np.ascontiguousarray(v) for k, v in arrays.items()}
    nc = bacc.Bacc("TRN2", target_bir_lowering=False, num_devices=1)
    args = {k: nc.dram_tensor(k, v.shape, mybir.dt.from_np(v.dtype), kind="ExternalInput").ap() for k, v in arrays.items()}
    args["out"] = nc.dram_tensor("out", (TOK, D), F32, kind="ExternalOutput").ap()
    build(nc, **args)
    r = run_bass_kernel_spmd(nc, [arrays], core_ids=[0])
    return r.results[0]["out"].reshape(1, TOK, D)
```

```python
from contextlib import ExitStack

import numpy as np

import concourse.bass as bass
from concourse import mybir

F32, F32R, I32 = mybir.dt.float32, mybir.dt.float32r, mybir.dt.int32
ALU = mybir.AluOpType
ACT = mybir.ActivationFunctionType
AX = mybir.AxisListType
ds = bass.ds

P = 128
T = 2
TOK = T * P
D = 2048
DK = D // P
SB_H, HD = 8, 128
MLA_H, ROPE, QK_DIM = 8, 64, 192
Q_RANK, KV_RANK = 768, 512
D_FF = 5632
A_H, A_KV = 16, 4
R_H, R_QK, R_V = 8, 256, 512
EPS, LN_EPS = 1e-6, 1e-5
ALPHA = (2.0 * 2) ** 0.25
BIG = -1e30
RSQRT_SEED = float(0x5F3759DF)
ROUND = 12582912.0
PI_F = 3.1415925

R = 4
UE = 1024
CW = 512

UNITS = {}
_n = 0
for _name, _u in [("qk", 4 * 8), ("lat", 3 * 8), ("v", 2 * 8), ("uq", 4 * 3), ("ukv", 4 * 2), ("gate", 8 * 8), ("mix", 4 * 8),
                  ("out", 2 * DK), ("up", 11 * 16), ("down", 2 * D_FF // P), ("aqkv", 6 * 8), ("ag", 4 * 8),
                  ("aout", 2 * DK), ("ret", 4 * 48), ("rout", 2 * 32)]:
    UNITS[_name] = _n
    _n += _u
N_UNITS = _n
BANKED = {"out": 0, "down": 7, "aout": 14, "rout": 21}
DVE_STAGE = {name: i + 1 for i, name in enumerate(('r1', 'ang', 'krot_done', 'rlat', 'mla_end', 'r2', 'attn_end', 'ret_end'))}
ACT_STAGE = {name: i + 1 for i, name in enumerate(('ss_x', 'sines', 'ss_lat', 'kr_hi', 'lg'))}


def at_least(eng, sem, value):
    if not (isinstance(value, int) and value <= 0):
        eng.wait_ge(sem, value)


def repeat(eng, n, body, own=None, last=False):
    if own:
        own.enter()
    body(0)
    if own:
        own.measured()
    end = n - 1 if last else n
    if end > 1:
        with eng.Fori(1, end) as i:
            if own:
                own.at(i)
            body(i)
    if last:
        if own:
            own.at(n - 1)
        body(n - 1)
    if own:
        own.leave(n)


class Own:

    def __init__(self, eng, sem):
        self.eng, self.sem = eng, sem
        self.base, self.k, self.i, self.per = 0, 0, 0, 0

    def mark(self, instruction):
        instruction.then_inc(self.sem, 1)
        self.k += 1

    def now(self):
        assert not self.per
        return self.base + self.k

    def wait(self):
        at_least(self.eng, self.sem, self.base + self.i * self.per + self.k)

    def step(self, instruction):
        self.mark(instruction)
        self.wait()

    def enter(self):
        self.base, self.k, self.i, self.per = self.base + self.k, 0, 0, 0

    def measured(self):
        self.per = self.k

    def at(self, i):
        assert self.k == self.per or not self.i, (self.k, self.per)
        self.k, self.i = 0, i

    def leave(self, n):
        assert self.k == self.per, (self.k, self.per)
        self.base, self.k, self.i, self.per = self.base + n * self.per, 0, 0, 0


def slot_of(base, i, per):
    return base % R, base // R + i * (per // R), base + i * per


def build(nc, x, xT, positions, g_pre, w_in, b_gate, g_lat, w_uq, w_ukv, w_o_sb, w_o_mla, w_out, g_post_mix,
          g_ffn, w_gate_up, w_down, g_post_ffn, a_w_in, a_q_gain, a_k_gain, a_w_out, r_w_in, r_decay, r_w_out,
          ln_gain, ln_bias, c_ident, c_ntri, c_nones, c_mask_sb, c_mask_mla, c_invf, c_cos_a, c_sin_a,
          c_cos_r, c_sin_r, c_dist_f, c_dist_b, out):
    gates_dram = nc.dram_tensor("gates_scratch", (TOK, 2 * D), F32, kind="Internal").ap()
    with ExitStack() as ctx:
        lo_end = -(-nc.sbuf_base // 64) * 64
        top = [lo_end]
        size = nc.sbuf_usable_end - lo_end

        def place(name, shape, dt, offset):
            n = 4
            for s in shape[1:]:
                n *= s
            assert offset + n <= lo_end + size, (name, offset + n - lo_end, size)
            return nc.alloc_sbuf_tensor_at(name, shape, dt, offset=offset)

        def put(name, shape, dt):
            t = place(name, shape, dt, top[0])
            n = 4
            for s in shape[1:]:
                n *= s
            top[0] += -(-n // 32) * 32
            return t

        raw = put("raw", [P, R, UE], F32)
        whi = put("whi", [P, R, UE], F32R)
        wlo = put("wlo", [P, R, UE], F32R)
        xh = put("xh", [P, DK, TOK], F32R)
        xl = put("xl", [P, DK, TOK], F32R)
        s0 = put("s0", [P, T, CW], F32)
        s1 = put("s1", [P, T, CW], F32)
        ident = put("ident", [P, P], F32)
        ident_r = put("ident_r", [P, P], F32R)
        ntri = put("ntri", [P, P], F32R)
        nones = put("nones", [P, P], F32R)
        mask_sb = put("mask_sb", [P, 3 * P], F32R)
        mask_mla = put("mask_mla", [P, T * TOK], F32R)
        gpre_c = put("gpre_c", [P, DK], F32)
        gffn_c = put("gffn_c", [P, DK], F32)
        glat_c = put("glat_c", [P, 10], F32)
        cos_m = put("cos_m", [P, T, ROPE], F32)
        sin_m = put("sin_m", [P, T, ROPE], F32)
        r1 = put("r1", [P, 2], F32)
        rlat = put("rlat", [P, 4], F32)
        r2 = put("r2", [P, 2], F32)
        ssum = put("ssum", [P, 16], F32)
        rs_v = put("rs_v", [P, 16], F32)
        rs_y = put("rs_y", [P, 16], F32)
        rs_t = put("rs_t", [P, 16], F32)
        shift = put("shift", [P, 1], F32)
        warm = put("warm", [P, 2], F32)
        mark = put("mark", [P, 1], F32)
        rs_i = put("rs_i", [P, 16], I32)
        rs_h = put("rs_h", [P, 16], F32)
        nmax = put("nmax", [P, 4, 2], F32)
        psum_ = put("psum_", [P, 4, 2], F32)
        prec = put("prec", [P, 4, 2], F32)
        stats = put("stats", [P, 2, 4, 6], F32)
        mv = put("mv", [P, 2, 2], F32)
        lg = put("lg", [P, 16], F32)
        h0 = top[0]
        h = place("h", [P, T, D], F32, h0)
        K = 1024
        qkT = place("qkT", [P, 16, TOK], F32, h0)
        v_sb = place("v_sb", [P, T, 1024], F32, h0 + 16 * K)
        qnT = place("qnT", [P, MLA_H, TOK], F32, h0 + 24 * K)
        qrT = place("qrT", [P, MLA_H // 2, TOK], F32, h0 + 32 * K)
        knT = place("knT", [P, MLA_H, TOK], F32, h0 + 36 * K)
        krh = place("krh", [P, TOK], F32R, h0 + 44 * K)
        krl = place("krl", [P, TOK], F32R, h0 + 45 * K)
        vm = place("vm", [P, T, MLA_H, HD], F32, h0 + 46 * K)
        yTh = place("yTh", [P, 16, TOK], F32R, h0 + 54 * K)
        yTl = place("yTl", [P, 16, TOK], F32R, h0 + 70 * K)
        latTh = place("latTh", [P, 10, TOK], F32R, h0 + 54 * K)
        latTl = place("latTl", [P, 10, TOK], F32R, h0 + 64 * K)
        lat = place("lat", [P, T, 1344], F32, h0 + 74 * K)
        x_tok = place("x_tok", [P, T, D], F32, h0 + 54 * K)
        xT_raw = place("xT_raw", [P, DK, TOK], F32, h0 + 70 * K)
        W = h0 + 86 * K
        sth = place("sth", [P, 2, 3, TOK], F32R, W)
        stl = place("stl", [P, 2, 3, TOK], F32R, W + 6 * K)
        sbt = place("sbt", [P, 2, 384], F32, W + 12 * K)
        sbh = place("sbh", [P, 2, 384], F32R, W + 15 * K)
        sbl = place("sbl", [P, 2, 384], F32R, W + 18 * K)
        mqh = place("mqh", [P, 2, 4, TOK], F32R, W)
        mql = place("mql", [P, 2, 4, TOK], F32R, W + 8 * K)
        mp = place("mp", [P, T, TOK], F32, W + 16 * K)
        mph = place("mph", [P, T, TOK], F32R, W + 18 * K)
        mpl = place("mpl", [P, T, TOK], F32R, W + 20 * K)
        bias_t = place("bias_t", [P, CW], F32, W + 22 * K)
        pos_i = place("pos_i", [P, T], I32, W)
        pos_f = place("pos_f", [P, T], F32, W + 64)
        invf = place("invf", [P, 32], F32, W + 128)
        ang = place("ang", [P, T, 32], F32, W + 512)
        kk = place("kk", [P, T, 32], F32, W + 1024)
        angc = place("angc", [P, T, 32], F32, W + 1536)
        mask_raw = place("mask_raw", [P, 9 * P], F32, W + 8 * K)
        krot = place("krot", [P, T, P], F32, W + 2 * K)
        rtmp = place("rtmp", [P, T, P], F32, W + 4 * K)
        rtm2 = place("rtm2", [P, T, P], F32, W + 5 * K)
        gt = place("gt", [P, 2, T, CW], F32, h0 + 16 * K)
        mixT = place("mixT", [P, DK, TOK], F32, h0 + 24 * K)
        osh1 = place("osh1", [P, 4, TOK], F32R, h0 + 40 * K)
        osl1 = place("osl1", [P, 4, TOK], F32R, h0 + 44 * K)
        gbc1 = place("gbc1", [P, D], F32, W)
        tmp1 = place("tmp1", [P, D], F32, W + 8 * K)
        actT = place("actT", [P, 44, TOK], F32, h0 + 16 * K)
        osh2 = place("osh2", [P, 4, TOK], F32R, h0 + 60 * K)
        osl2 = place("osl2", [P, 4, TOK], F32R, h0 + 64 * K)
        gbc2 = place("gbc2", [P, D], F32, h0 + 68 * K)
        tmp2 = place("tmp2", [P, D], F32, h0 + 76 * K)
        aqT = place("aqT", [P, A_H + A_KV, TOK], F32, h0 + 16 * K)
        av = place("av", [P, T, CW], F32, h0 + 36 * K)
        agT = place("agT", [P, DK, TOK], F32, h0 + 40 * K)
        osh3 = place("osh3", [P, 4, TOK], F32R, h0 + 56 * K)
        osl3 = place("osl3", [P, 4, TOK], F32R, h0 + 60 * K)
        cgs = place("cgs", [P, 4, T, HD], F32, h0 + 60 * K)
        kvh = place("kvh", [P, 2, 2, TOK], F32R, h0 + 64 * K)
        kvl = place("kvl", [P, 2, 2, TOK], F32R, h0 + 68 * K)
        aqh = place("aqh", [P, 2, TOK], F32R, h0 + 72 * K)
        aql = place("aql", [P, 2, TOK], F32R, h0 + 74 * K)
        ap_ = place("ap_", [P, 2, T, TOK], F32, h0 + 76 * K)
        aph = place("aph", [P, T, TOK], F32R, h0 + 80 * K)
        apl = place("apl", [P, T, TOK], F32R, h0 + 82 * K)
        obuf = place("obuf", [P, T, CW], F32, h0 + 84 * K)
        sqt = place("sqt", [P, T, CW], F32, h0 + 88 * K)
        gtab = place("gtab", [P, 2, HD], F32, h0 + 92 * K)
        ctab = place("ctab", [P, 2, T, HD], F32, h0 + 93 * K)
        lng1 = place("lng1", [P, 2, D], F32, h0 + 64 * K)
        rqh = place("rqh", [P, 2, 4, TOK], F32R, h0 + 16 * K)
        rql = place("rql", [P, 2, 4, TOK], F32R, h0 + 24 * K)
        pth = place("pth", [P, 2, T, TOK], F32R, h0 + 32 * K)
        ptl = place("ptl", [P, 2, T, TOK], F32R, h0 + 36 * K)
        rvh = place("rvh", [P, 2, T, R_V], F32R, h0 + 40 * K)
        rvl = place("rvl", [P, 2, T, R_V], F32R, h0 + 48 * K)
        rcs = place("rcs", [P, 2, T, R_QK], F32, h0 + 56 * K)
        dist = place("dist", [P, 2, T, TOK], F32, h0 + 60 * K)
        dmat = place("dmat", [P, 2, T, TOK], F32, h0 + 64 * K)
        onorm = place("onorm", [P, 2, T, R_V], F32, h0 + 68 * K)
        rgT = place("rgT", [P, 32, TOK], F32, h0 + 76 * K)
        rt = place("rt", [P, CW], F32, h0 + 108 * K)
        osh4 = place("osh4", [P, 4, TOK], F32R, h0 + 16 * K)
        osl4 = place("osl4", [P, 4, TOK], F32R, h0 + 20 * K)
        lng2 = place("lng2", [P, 2, D], F32, h0 + 32 * K)

        acc = ctx.enter_context(nc.psum_tensor("acc", [P, 2, T, CW], F32))
        aux = ctx.enter_context(nc.psum_tensor("aux", [P, 4, CW], F32))
        banks = [acc[:, 0, 0], acc[:, 0, 1], acc[:, 1, 0], acc[:, 1, 1], aux[:, 0], aux[:, 1], aux[:, 2], aux[:, 3]]
        whole = [acc[:].rearrange("p a b c -> p (a b c)"), aux[:].rearrange("p a c -> p (a c)")]

        names = {}

        def sem(name):
            if name not in names:
                names[name] = ctx.enter_context(nc.semaphore(name))
            return names[name]

        landed = [sem(f"weights_landed{s}") for s in range(R)]
        hi_done, lo_done, used = sem("hi_done"), sem("lo_done"), sem("unit_used")
        consts, act_own, dve_own = sem("consts"), sem("act_own"), sem("dve_own")

        block = ctx.enter_context(nc.Block())

        @block.sync
        def _(sp):
            def load(base, i, per, src, width):
                slot, turn, n = slot_of(base, i, per)
                at_least(sp, lo_done, n - R + 1)
                if width == UE:
                    dst = raw[:, slot]
                else:
                    dst = raw[:, slot, 0:2 * width].rearrange("p (k n) -> p k n", k=2)
                sp.dma_start(dst, src).then_inc(landed[slot], 16)

            def chunk(base, i, per, w, units, col, width=CW, row0=0):
                for u in range(units):
                    src = w[row0 + u * 2 * P:row0 + (u + 1) * 2 * P, ds(col, width)].rearrange("(k p) n -> p k n", p=P)
                    load(base + u, i, per, src, width)

            def rows(name, n_kt, w):
                def body(i):
                    for k in range(2):
                        for half in range(2):
                            load(UNITS[name] + 2 * k + half, i, 4,
                                 w[ds(i * 2 * P + k * P, P), half * UE:(half + 1) * UE], UE)
                repeat(sp, n_kt // 2, body)

            repeat(sp, 4, lambda i: chunk(UNITS["qk"], i, 8, w_in, 8, i * CW))
            for c in range(3):
                chunk(UNITS["lat"] + 8 * c, 0, 8, w_in, 8, 3072 + c * 448, 448)
            for c in range(2):
                chunk(UNITS["v"] + 8 * c, 0, 8, w_in, 8, 2048 + c * CW)
            for c in range(4):
                chunk(UNITS["uq"] + 3 * c, 0, 4, w_uq, 3, c * 384, 384)
            for c in range(4):
                chunk(UNITS["ukv"] + 2 * c, 0, 4, w_ukv, 2, c * CW)

            def gate(i):
                chunk(UNITS["gate"], i, 8, w_in, 8, i * CW + 4416)
            repeat(sp, 8, gate)

            def mix(i):
                chunk(UNITS["mix"], i, 8, w_o_sb, 4, i * CW)
                chunk(UNITS["mix"] + 4, i, 8, w_o_mla, 4, i * CW)
            repeat(sp, 4, mix)
            rows("out", DK, w_out)

            def up(i):
                chunk(UNITS["up"], i, 16, w_gate_up, 8, i * CW)
                chunk(UNITS["up"] + 8, i, 16, w_gate_up, 8, i * CW + D_FF)
            repeat(sp, 11, up)
            rows("down", 44, w_down)
            repeat(sp, 3, lambda i: [chunk(UNITS["aqkv"] + 8 * c, i, 16, a_w_in, 8, i * 1024 + c * CW) for c in range(2)])
            repeat(sp, 4, lambda i: chunk(UNITS["ag"], i, 8, a_w_in, 8, i * CW + 3072))
            rows("aout", DK, a_w_out)

            def ret(i):
                cols = [i * CW, i * CW + 2048, i * 1024 + 4096, i * 1024 + 4608, i * 1024 + 8192, i * 1024 + 8704]
                for c, col in enumerate(cols):
                    chunk(UNITS["ret"] + 8 * c, i, 48, r_w_in, 8, col)
            repeat(sp, 4, ret)
            rows("rout", 32, r_w_out)
            for n in range(4 * T):
                t, cols = n // 4, slice(n % 4 * CW, (n % 4 + 1) * CW)
                sp.wait_ge(sem("result" if t else "result0"), n % 4 + 1)
                sp.dma_start(out[t * P:(t + 1) * P, cols], h[:, t, cols]).then_inc(sem("stored"), 16)
            sp.wait_ge(sem("stored"), 16 * 4 * T)

        @block.gpsimd
        def _(pool):
            def bring(name, pairs):
                for dst, src in pairs:
                    pool.dma_start(dst, src).then_inc(sem(name), 16)

            bring("gain_in", [(gpre_c[:], g_pre)])
            bring("consts", [(ident[:], c_ident), (gffn_c[:], g_ffn), (glat_c[:], g_lat),
                             (pos_i[:], positions), (invf[:], c_invf.partition_broadcast(P))])
            bring("masks", [(mask_raw[:, 0:P], c_ntri), (mask_raw[:, P:2 * P], c_nones),
                            (mask_raw[:, 2 * P:5 * P], c_mask_sb), (mask_raw[:, 5 * P:9 * P], c_mask_mla)])

            pool.wait_ge(sem("dve_stage"), DVE_STAGE["mla_end"])
            pool.dma_start(h[:], x.rearrange("(t p) n -> p t n", p=P)).then_inc(sem("x_again"), 16)

            bring("gains_in", [(gbc1[:], g_post_mix.partition_broadcast(P))])
            def lo_between(phase):
                for u in range(4):
                    slot, turn, n = slot_of(UNITS[phase] + u, 0, R)
                    pool.wait_ge(hi_done, n + 1)
                    nc.gpsimd.tensor_tensor(wlo[:, slot], raw[:, slot], whi[:, slot].bitcast(F32),
                                            ALU.subtract).then_inc(lo_done, 1)
            lo_between("up")
            bring("gains_in", [(gbc2[:], g_post_ffn.partition_broadcast(P))])
            lo_between("aqkv")
            bring("tables_in", [(gtab[:, 0], a_q_gain.partition_broadcast(P)), (gtab[:, 1], a_k_gain.partition_broadcast(P)),
                              (ctab[:, 0], c_cos_a.rearrange("(t p) n -> p t n", p=P)),
                              (ctab[:, 1], c_sin_a.rearrange("(t p) n -> p t n", p=P))])
            pool.wait_ge(sem("dve_stage"), DVE_STAGE["attn_end"])
            bring("gains_in", [(lng1[:, 0], ln_gain[0].partition_broadcast(P)), (lng1[:, 1], ln_bias[0].partition_broadcast(P))])
            lo_between("ret")
            pool.wait_ge(sem("attn_done"), 5)
            bring("tables_in", [(rcs[:, 0], c_cos_r.rearrange("(t p) n -> p t n", p=P)),
                              (rcs[:, 1], c_sin_r.rearrange("(t p) n -> p t n", p=P)),
                              (dist[:, 0], c_dist_f.rearrange("(t p) n -> p t n", p=P)),
                              (dist[:, 1], c_dist_b.rearrange("(t p) n -> p t n", p=P)),
                              (lg[:], r_decay.partition_broadcast(P))])
            pool.wait_ge(sem("dve_stage"), DVE_STAGE["ret_end"])
            bring("gains_in", [(lng2[:, 0], ln_gain[1].partition_broadcast(P)), (lng2[:, 1], ln_bias[1].partition_broadcast(P))])

            pool.wait_ge(sem("gains_in"), 96)
            for b in range(4):
                cols = slice(b * CW, (b + 1) * CW)
                pool.wait_ge(sem("scaled"), b + 1)
                nc.gpsimd.tensor_tensor(h[:, 0, cols], h[:, 0, cols], lng2[:, 0, cols], ALU.mult).then_inc(sem("gained"), 1)
                pool.wait_ge(sem("gained"), b + 1)
                nc.gpsimd.tensor_tensor(h[:, 0, cols], h[:, 0, cols], lng2[:, 1, cols], ALU.add).then_inc(sem("result0"), 1)

        @block.tensor
        def _(pe):
            def three(dst, lh, ll, rh, rl, start, stop):
                pe.matmul(dst, lh, rh, start=start, stop=False, skip_group_check=True)
                pe.matmul(dst, lh, rl, start=False, stop=False, skip_group_check=True)
                return pe.matmul(dst, ll, rh, start=False, stop=stop, skip_group_check=True)

            def unit(base, i, per, pair, kt0, restart=None, sh=xh, sl=xl, width=CW):
                slot, turn, n = slot_of(base, i, per)
                pe.wait_ge(lo_done, n + 1)
                for k in range(2):
                    for t in range(T):
                        tok = slice(t * P, (t + 1) * P)
                        last = three(acc[:, pair, t, 0:width], sh[:, kt0 + k, tok], sl[:, kt0 + k, tok],
                                     whi[:, slot, k * width:(k + 1) * width], wlo[:, slot, k * width:(k + 1) * width],
                                     start=k == 0 and kt0 in (0, restart), stop=False)
                last.then_inc(used, 1)

            def turn_blocks(src, blocks, bank0=0):
                for b in range(blocks):
                    for t in range(T):
                        last = pe.transpose(aux[:, bank0 + b // 2, (b % 2) * TOK + t * P:(b % 2) * TOK + (t + 1) * P],
                                            src[:, t, b * P:(b + 1) * P], ident[:])
                return last

            def rows(name, n_kt, sh, sl, free, turned):
                def by_tile(i):
                    for t in range(T):
                        tok = slice(t * P, (t + 1) * P)
                        for half in range(2):
                            if i == 0 and t == 0:
                                free(half)
                            for c in range(2):
                                cols = slice(c * CW, (c + 1) * CW)
                                for k in range(2):
                                    slot, turn, n = slot_of(UNITS[name] + 4 * i + 2 * k + half, 0, 4)
                                    if t == 0 and c == 0:
                                        pe.wait_ge(sem(name + "_stage"), i * 2 + k + 1)
                                        pe.wait_ge(lo_done, n + 1)
                                    buf = (2 * i + k) % 4
                                    last = three(banks[4 * t + 2 * half + c], sh[:, buf, tok], sl[:, buf, tok],
                                                 whi[:, slot, cols], wlo[:, slot, cols], start=i == 0 and k == 0, stop=False)
                                    if t == 1 and c == 1 and k == 0:
                                        last.then_inc(used, half + 1)
                                if (t, half, c) == (1, 1, 1):
                                    last.then_inc(used, 1)
                                elif i:
                                    last.then_inc(sem("bank_done"), 1)
                        if i == 0 and t == 0:
                            turned()

                def body(i):
                    for k in range(4):
                        pe.wait_ge(sem(name + "_stage"), i * 4 + k + 3)
                        for half in range(2):
                            slot, turn, n = slot_of(UNITS[name] + 4 + 2 * k + half, i, 8)
                            pe.wait_ge(lo_done, n + 1)
                            for c in range(2):
                                for t in range(T):
                                    tok = slice(t * P, (t + 1) * P)
                                    cols = slice(c * CW, (c + 1) * CW)
                                    buf = (k + 2) % 4
                                    last = three(banks[4 * t + 2 * half + c], sh[:, buf, tok], sl[:, buf, tok],
                                                 whi[:, slot, cols], wlo[:, slot, cols], start=False, stop=False)
                            last.then_inc(used, 1)
                by_tile(0)
                repeat(pe, (n_kt - 4) // 4, body)
                by_tile(n_kt // 2 - 1)


            def turned(name, c):
                pe.wait_ge(sem(name + "_evA"), c + 1)
                pe.wait_ge(sem(name + "_evD"), c + 1)
                at_least(pe, sem(name + "_cpA"), c)
                at_least(pe, sem(name + "_cpD"), c)

            def qkv(i):
                for c in range(2):
                    at_least(pe, sem("qkv_evA"), i * 2 + c - 1)
                    at_least(pe, sem("qkv_evD"), i * 2 + c - 1)
                    first = isinstance(i, int) and i == 0
                    if first and c == 1:
                        pe.wait_ge(consts, 16 * 5)
                    for u in range(8):
                        if first and c == 0:
                            pe.wait_ge(sem("x_split"), 2 * u + 2)
                        unit(UNITS["qk"] + 8 * c + u, i, 16, 1 - c, 2 * u)
                        if (c == 1 and u == 7) if first else u == 3:
                            turned("qkv", i * 2 + c - 1)
                            turn_blocks(s0, 4).then_inc(sem("qkv_tr"), 1)
            repeat(pe, 2, qkv)
            for c in range(3):
                pe.wait_ge(sem("qkv_evA"), 4 + c - 1)
                pe.wait_ge(sem("qkv_evD"), 4 + c - 1)
                for u in range(8):
                    unit(UNITS["lat"] + 8 * c + u, 0, 8, 1 - c % 2, 2 * u, width=448)
                    if u == 3 and c == 0:
                        turned("qkv", 3)
                        turn_blocks(s0, 4).then_inc(sem("qkv_tr"), 1)

            def lat_turn(blocks):
                for b in blocks:
                    if b >= 8:
                        pe.wait_ge(sem("lat_lo"), 2)
                    for t in range(T):
                        last = pe.transpose(aux[:, b // 2 % 4, (b % 2) * TOK + t * P:(b % 2) * TOK + (t + 1) * P],
                                            lat[:, t, b * P:(b + 1) * P], ident[:])
                    if b % 2 == 1:
                        last.then_inc(sem("lat_tr"), 1)
            for c in range(2):
                pe.wait_ge(sem("qkv_evA"), 7 + c - 1)
                pe.wait_ge(sem("qkv_evD"), 7 + c - 1)
                for u in range(8):
                    unit(UNITS["v"] + 8 * c + u, 0, 8, c, 2 * u)
                    if c == 0 and u == 2:
                        pe.wait_ge(sem("qkv_evA"), 7)
                        pe.wait_ge(sem("qkv_evD"), 7)
                        pe.wait_ge(sem("qkv_cpA"), 4)
                        pe.wait_ge(sem("qkv_cpD"), 4)
                        lat_turn(range(8))
                    if c == 0 and u == 6:
                        lat_turn(range(8, 10))
                        pe.wait_ge(sem("dve_stage"), DVE_STAGE["krot_done"])
                        pe.wait_ge(sem("lat_lo"), 4)
                        for t in range(T):
                            last = pe.transpose(aux[:, 1, t * P:(t + 1) * P], krot[:, t], ident[:])
                        last.then_inc(sem("kr_tr"), 1)
            pe.wait_ge(sem("qkv_evA"), 8)
            pe.wait_ge(sem("qkv_evD"), 8)
            pe.wait_ge(sem("lat_lo"), 10)
            pe.wait_ge(sem("kr_lo"), 1)

            def uq_turn(c):
                pe.wait_ge(sem("uq_evA"), c + 1)
                pe.wait_ge(sem("uq_rope"), c + 1)
                at_least(pe, sem("uq_cpA"), c)
                at_least(pe, sem("uq_cpD"), c)
                for hh in range(2):
                    for t in range(T):
                        pe.transpose(aux[:, 0, hh * TOK + t * P:hh * TOK + (t + 1) * P],
                                     s0[:, t, hh * QK_DIM:hh * QK_DIM + HD], ident[:])
                for t in range(T):
                    last = pe.transpose(aux[:, 1, t * P:(t + 1) * P], s1[:, t, 0:P], ident[:])
                last.then_inc(sem("uq_tr"), 1)
            for c in range(4):
                if c == 1:
                    pe.wait_ge(sem("qkv_evA"), 9)
                    pe.wait_ge(sem("qkv_evD"), 9)
                at_least(pe, sem("uq_evA"), c - 1)
                at_least(pe, sem("uq_evD"), c - 1)
                for u in range(3):
                    unit(UNITS["uq"] + 3 * c + u, 0, 4, c % 2, 2 * u, None, latTh, latTl, 384)
                    if u == 2 and c:
                        uq_turn(c - 1)

            def ukv_turn(c):
                pe.wait_ge(sem("ukv_evA"), c + 1)
                pe.wait_ge(sem("ukv_evD"), c + 1)
                at_least(pe, sem("ukv_cpA"), c)
                turn_blocks(s0, 2, 2).then_inc(sem("ukv_tr"), 1)
            for c in range(4):
                if c < 2:
                    pe.wait_ge(sem("uq_evA"), 3 + c)
                    pe.wait_ge(sem("uq_evD"), 3 + c)
                else:
                    pe.wait_ge(sem("ukv_evA"), c - 1)
                    pe.wait_ge(sem("ukv_evD"), c - 1)
                for u in range(2):
                    slot, turn, n = slot_of(UNITS["ukv"] + 2 * c + u, 0, 4)
                    pe.wait_ge(lo_done, n + 1)
                    for k in range(2):
                        for t in range(T):
                            tok = slice(t * P, (t + 1) * P)
                            last = three(acc[:, c % 2, t], latTh[:, 6 + 2 * u + k, tok], latTl[:, 6 + 2 * u + k, tok],
                                         whi[:, slot, k * CW:(k + 1) * CW], wlo[:, slot, k * CW:(k + 1) * CW],
                                         start=u == 0 and k == 0, stop=False)
                    last.then_inc(used, 1)
                    if u == 1 and c == 0:
                        uq_turn(3)
                    if u == 1 and c:
                        ukv_turn(c - 1)
            pe.wait_ge(sem("ukv_evA"), 3)
            pe.wait_ge(sem("ukv_evD"), 3)

            def sb_logits(n):
                pe.wait_ge(sem("sb_stage"), n + 1)
                for hh in range(2):
                    z = aux[:, hh]
                    pe.matmul(z[:, 0:384], ident_r[:], mask_sb[:], start=True, stop=False, skip_group_check=True)
                    three(z[:, 0:TOK], sth[:, hh, 1, 0:P], stl[:, hh, 1, 0:P], sth[:, hh, 0], stl[:, hh, 0], False, False)
                    last = three(z[:, TOK:384], sth[:, hh, 1, P:TOK], stl[:, hh, 1, P:TOK], sth[:, hh, 0, P:TOK],
                                 stl[:, hh, 0, P:TOK], False, False)
                last.then_inc(sem("sb_z"), 1)

            def sb_sums(n):
                pe.wait_ge(sem("sb_split"), 2 * n + 1)
                for hh in range(2):
                    z = aux[:, hh]
                    for part in (sbh[:, hh], sbl[:, hh]):
                        pe.matmul(z[:, 0:384], ntri[:], part, start=False, stop=False, skip_group_check=True)
                        last = pe.matmul(z[:, P:TOK], nones[:], part[:, TOK:384], start=False, stop=False,
                                         skip_group_check=True)
                last.then_inc(sem("sb_s"), 1)

            def sb_values(n):
                pe.wait_ge(sem("sb_split"), 2 * n + 2)
                if isinstance(n, int) and n == 0:
                    pe.wait_ge(sem("ukv_cpA"), 4)
                at_least(pe, sem("sb_y"), n)
                for hh in range(2):
                    y = aux[:, 2 + hh]
                    three(y[:, 0:TOK], sth[:, hh, 2, 0:P], stl[:, hh, 2, 0:P], sbh[:, hh, 0:TOK], sbl[:, hh, 0:TOK], True, False)
                    last = three(y[:, P:TOK], sth[:, hh, 2, P:TOK], stl[:, hh, 2, P:TOK], sbh[:, hh, TOK:384],
                                 sbl[:, hh, TOK:384], False, False)
                last.then_inc(sem("sb_v"), 1)

            def gates_sb(i):
                for c in range(2):
                    n = i * 2 + c
                    if c == 1 and isinstance(i, int) and i == 0:
                        pe.wait_ge(sem("ukv_cpA"), 4)
                    at_least(pe, sem("gate_dve"), n - 1)
                    for u in range(8):
                        unit(UNITS["gate"] + 8 * c + u, i, 16, c, 2 * u)
                        if u == 1 and c == 0 and isinstance(i, int) and i == 0:
                            ukv_turn(3)
                            pe.wait_ge(sem("uq_cpD"), 4)
                        if u == 1:
                            sb_logits(n)
                        if u == 5:
                            sb_sums(n)
                        if u == 7:
                            sb_values(n)
            repeat(pe, 2, gates_sb)
            def mla_logits(n, hh):
                pe.wait_ge(sem("mla_stage"), n + 1)
                at_least(pe, sem("mla_exp"), n)
                half = slice(hh * ROPE, (hh + 1) * ROPE)
                s = aux[:, 0]
                pe.matmul(s, ident_r[:], mask_mla[:], start=True, stop=False, skip_group_check=True)
                for t in range(T):
                    tok, keys = slice(t * P, (t + 1) * P), slice(0, (t + 1) * P)
                    cols = slice(t * TOK, t * TOK + (t + 1) * P)
                    three(s[:, cols], mqh[:, hh, 0, tok], mql[:, hh, 0, tok], mqh[:, hh, 2, keys], mql[:, hh, 2, keys],
                          False, False)
                    last = three(s[:, cols], mqh[half, hh, 1, tok], mql[half, hh, 1, tok], krh[half, keys], krl[half, keys],
                                 False, False)
                last.then_inc(sem("mla_s"), 1)

            def mla_turn(n):
                pe.wait_ge(sem("mla_norm"), n + 1)
                at_least(pe, sem("mla_pl"), n)
                for kt in range(T):
                    for t in range(T):
                        last = pe.transpose(aux[:, 1, kt * TOK + t * P:kt * TOK + (t + 1) * P],
                                            mp[:, t, kt * P:(kt + 1) * P], ident[:])
                last.then_inc(sem("mla_tr"), 1)

            def mla_values(n, hh):
                pe.wait_ge(sem("mla_pl"), n + 1)
                if isinstance(n, int) and n == 0:
                    pe.wait_ge(sem("sb_y"), 4)
                at_least(pe, sem("mla_y"), n)
                for kt in range(T):
                    rows_ = slice(kt * P, (kt + 1) * P)
                    last = three(aux[:, 2, kt * P:TOK], mqh[:, hh, 3, rows_], mql[:, hh, 3, rows_],
                                 mph[:, kt, kt * P:TOK], mpl[:, kt, kt * P:TOK], kt == 0, False)
                last.then_inc(sem("mla_v"), 1)

            def gates_mla(i):
                for c in range(2):
                    n = i * 2 + c
                    pe.wait_ge(sem("gate_dve"), n + 3)
                    for u in range(8):
                        unit(UNITS["gate"] + 32 + 8 * c + u, i, 16, c, 2 * u)
                        for hh in range(2):
                            if u == 3 * hh + 1:
                                mla_logits(n * 2 + hh, hh)
                            if u == 3 * hh + 3:
                                mla_turn(n * 2 + hh)
                            if u == 3 * hh + 4:
                                mla_values(n * 2 + hh, hh)
            repeat(pe, 2, gates_mla)
            pe.wait_ge(sem("gate_dve"), 7)

            def mix_turn(j):
                pe.wait_ge(sem("mix_dve"), j + 1)
                at_least(pe, sem("mix_cpA"), j)
                at_least(pe, sem("mix_cpD"), j)
                turn_blocks(s0, 4).then_inc(sem("mix_tr"), 1)

            def mix(i):
                for u in range(8):
                    if u % 4 == 0:
                        if u == 4 and isinstance(i, int) and i == 0:
                            pe.wait_ge(sem("gate_dve"), 8)
                            pe.wait_ge(sem("mla_y"), 8)
                        at_least(pe, sem(f"mix_free{u // 4}"), i)
                    unit(UNITS["mix"] + u, i, 8, u // 4, 2 * u, MLA_H, yTh, yTl)
                    if u == 3 and not (isinstance(i, int) and i == 0):
                        mix_turn(i - 1)
            repeat(pe, 4, mix)

            def mix_turned():
                mix_turn(3)
                pe.wait_ge(sem("mix_cpA"), 4)
                pe.wait_ge(sem("mix_cpD"), 4)
            rows("out", DK, osh1, osl1, lambda half: pe.wait_ge(sem(f"mix_free{half}"), 4), mix_turned)

            def turn_tile(t, done, name):
                for b in range(4):
                    pe.wait_ge(sem(done), 4 * t + b + 1)
                    for j in range(4):
                        last = pe.transpose(banks[4 * t + b][:, j * P:(j + 1) * P],
                                            h[:, t, (4 * b + j) * P:(4 * b + j + 1) * P], ident[:])
                    last.then_inc(sem(name + "_tr"), 1)

            def first_units(name, phase, done):
                turn_tile(0, done, name)
                for t in range(T):
                    if t == 1:
                        turn_tile(1, done, name)
                    tok = slice(t * P, (t + 1) * P)
                    for u in range(4):
                        slot, turn, n = slot_of(UNITS[phase] + u, 0, 4)
                        if t == 0:
                            pe.wait_ge(lo_done, n + 1)
                        if u % 2 == 0:
                            pe.wait_ge(sem(name + "_xlo"), 4 * t + u // 2 + 1)
                        for k in range(2):
                            last = three(acc[:, 0, t], xh[:, 2 * u + k, tok], xl[:, 2 * u + k, tok],
                                         whi[:, slot, k * CW:(k + 1) * CW], wlo[:, slot, k * CW:(k + 1) * CW],
                                         start=u == 0 and k == 0, stop=False)
                        if t == 1:
                            last.then_inc(used, 1)

            def up_turn(j):
                pe.wait_ge(sem("up_dve"), j + 1)
                at_least(pe, sem("up_cpA"), j)
                at_least(pe, sem("up_cpD"), j)
                turn_blocks(s0, 4).then_inc(sem("up_tr"), 1)

            first_units("ffn", "up", "mixer_done")

            def up(i):
                first = isinstance(i, int) and i == 0
                at_least(pe, sem("up_act"), i)
                for u in range(4 if first else 0, 16):
                    if first and u in (4, 6):
                        pe.wait_ge(sem("ffn_xlo"), u // 2 + 5)
                    if u == 8:
                        at_least(pe, sem("up_dve"), i)
                    unit(UNITS["up"] + u, i, 16, u // 8, 2 * (u % 8))
                    if u == 3 and not (isinstance(i, int) and i == 0):
                        up_turn(i - 1)
            repeat(pe, 11, up)

            def up_turned():
                up_turn(10)
                pe.wait_ge(sem("up_cpA"), 11)
                pe.wait_ge(sem("up_cpD"), 11)
            rows("down", 44, osh2, osl2, lambda half: pe.wait_ge(sem("up_dve" if half else "up_act"), 11), up_turned)

            first_units("a", "aqkv", "ffn_done")

            def a_turn(c):
                pe.wait_ge(sem("a_rot"), c + 1)
                at_least(pe, sem("a_cpA"), c)
                at_least(pe, sem("a_cpD"), c)
                turn_blocks(s1, 4).then_inc(sem("a_ctr"), 1)

            def a_q(i):
                for c in range(2):
                    at_least(pe, sem("a_evA"), i * 2 + c - 1)
                    at_least(pe, sem("a_evD"), i * 2 + c - 1)
                    first = isinstance(i, int) and i == 0 and c == 0
                    for u in range(4 if first else 0, 8):
                        if first and u in (4, 6):
                            pe.wait_ge(sem("a_xlo"), u // 2 + 5)
                        unit(UNITS["aqkv"] + 8 * c + u, i, 16, c, 2 * u)
                        if u == 7 and not (isinstance(i, int) and i == 0 and c == 0):
                            a_turn(i * 2 + c - 1)
            repeat(pe, 2, a_q)
            for c in range(4, 6):
                pe.wait_ge(sem("a_evA"), c - 1)
                pe.wait_ge(sem("a_evD"), c - 1)
                for u in range(8):
                    unit(UNITS["aqkv"] + 8 * c + u, 0, 8, c % 2, 2 * u)
                    if u == 7:
                        a_turn(c - 1)

            def ag_logits(n, e, kv):
                pe.wait_ge(sem("ag_q"), n + 1)
                at_least(pe, sem("ag_exp"), n - 1)
                for t in range(T):
                    tok = slice(t * P, (t + 1) * P)
                    last = three(aux[:, e % 2, t * TOK:(t + 1) * TOK], aqh[:, e % 2, tok], aql[:, e % 2, tok],
                                 kvh[:, kv, 0], kvl[:, kv, 0], True, False)
                last.then_inc(sem("ag_s"), 1)

            def ag_ptr(n, e):
                pe.wait_ge(sem("ag_exp"), n + 1)
                at_least(pe, sem("ag_pl"), n)
                for kt in range(T):
                    for t in range(T):
                        last = pe.transpose(aux[:, 2, kt * TOK + t * P:kt * TOK + (t + 1) * P],
                                            ap_[:, e % 2, t, kt * P:(kt + 1) * P], ident[:])
                last.then_inc(sem("ag_ptr"), 1)

            def ag_values(n, kv):
                pe.wait_ge(sem("ag_pl"), n + 1)
                at_least(pe, sem("ag_o"), n)
                for t in range(T):
                    tok = slice(t * P, (t + 1) * P)
                    for kt in range(T):
                        last = three(aux[:, 3, t * P:(t + 1) * P], aph[:, kt, tok], apl[:, kt, tok],
                                     kvh[:, kv, 1, kt * P:(kt + 1) * P], kvl[:, kv, 1, kt * P:(kt + 1) * P], kt == 0, False)
                last.then_inc(sem("ag_v"), 1)

            def ag_turn(j, dst):
                pe.wait_ge(sem("ag_gated"), j + 1)
                for b in range(4):
                    for t in range(T):
                        last = pe.transpose(dst[:, b // 2, (b % 2) * TOK + t * P:(b % 2) * TOK + (t + 1) * P],
                                            s1[:, t, b * P:(b + 1) * P], ident[:])
                last.then_inc(sem("ag_ctr"), 1)

            def ag(i):
                for c in range(2):
                    g = i * 2 + c
                    first = isinstance(g, int) and g == 0
                    if isinstance(i, int) and i == 0:
                        pe.wait_ge(sem("a_evA"), 5 + c)
                        pe.wait_ge(sem("a_evD"), 5 + c)
                    at_least(pe, sem("ag_cpA"), g - 1)
                    at_least(pe, sem("ag_cpD"), g - 1)
                    for u in range(8):
                        unit(UNITS["ag"] + 8 * c + u, i, 16, c, 2 * u)
                        if u == 0 and first:
                            pe.wait_ge(sem("a_cpA"), 5)
                            pe.wait_ge(sem("a_cpD"), 5)
                        if u == 0 and not first:
                            ag_values(g * 4 - 1, 1 - c)
                        if u == 0:
                            pe.wait_ge(sem("ag_kv"), g + 1)
                        if u % 2 == 0:
                            ag_logits(g * 4 + u // 2, u // 2, c)
                            if u:
                                ag_values(g * 4 + u // 2 - 1, c)
                        else:
                            ag_ptr(g * 4 + u // 2, u // 2)
                        if u == 3 and not first:
                            ag_turn(g - 1, acc[:, 1 - c])
            repeat(pe, 2, ag)

            def ag_free(half):
                if half == 0:
                    pe.wait_ge(sem("ag_cpA"), 3)
                    pe.wait_ge(sem("ag_cpD"), 3)
                else:
                    pe.wait_ge(sem("ag_silu"), 4)
                    ag_values(15, 1)

            def ag_turned():
                pe.wait_ge(sem("ag_exp"), 16)
                ag_turn(3, aux)
                pe.wait_ge(sem("ag_cpA"), 4)
                pe.wait_ge(sem("ag_cpD"), 4)
            rows("aout", DK, osh3, osl3, ag_free, ag_turned)
            first_units("r", "ret", "attn_done")

            def r_turn(n):
                pe.wait_ge(sem("r_rot"), n + 1)
                at_least(pe, sem("r_qlo"), 2 * n)
                turn_blocks(s1, 4).then_inc(sem("r_ctr"), 1)

            def r_scores(n, hh):
                pe.wait_ge(sem("r_qlo"), n)
                for jt in range(T):
                    keys = slice(jt * P, (jt + 1) * P)
                    for kt in range(2):
                        last = three(aux[:, 2 + hh, jt * TOK:(jt + 1) * TOK], rqh[:, 1, 2 * hh + kt, keys],
                                     rql[:, 1, 2 * hh + kt, keys], rqh[:, 0, 2 * hh + kt], rql[:, 0, 2 * hh + kt],
                                     kt == 0, False)
                last.then_inc(sem("r_s"), 1)

            def r_out(i, hh):
                pe.wait_ge(sem("r_pl"), i * 2 + hh + 1)
                pe.wait_ge(sem("r_evD"), i * 6 + hh + 3)
                for t in range(T):
                    tok = slice(t * P, (t + 1) * P)
                    for jt in range(T):
                        last = three(aux[:, 2 * hh + t], pth[:, hh, jt, tok], ptl[:, hh, jt, tok],
                                     rvh[:, hh, jt], rvl[:, hh, jt], jt == 0, False)
                last.then_inc(sem("r_o"), 1)

            def r_gturn(i, hh):
                pe.wait_ge(sem("r_evD"), i * 6 + hh + 5)
                turn_blocks(s0, 4).then_inc(sem("r_gtr"), 1)

            def ret(i):
                first = isinstance(i, int) and i == 0
                for c in range(6):
                    at_least(pe, sem("r_evA"), i * 6 + c - 1)
                    at_least(pe, sem("r_evD"), i * 6 + c - 1)
                    for u in range(4 if first and c == 0 else 0, 8):
                        if first and c == 0 and u in (4, 6):
                            pe.wait_ge(sem("r_xlo"), u // 2 + 5)
                        unit(UNITS["ret"] + 8 * c + u, i, 48, c % 2, 2 * u)
                        if c == 0 and u == 3 and not first:
                            r_gturn(i - 1, 1)
                        if c == 1 and u == 4:
                            at_least(pe, sem("r_gcpA"), i * 2)
                            at_least(pe, sem("r_gcpD"), i * 2)
                            r_turn(i * 2)
                        if c == 2 and u == 4:
                            r_turn(i * 2 + 1)
                        if c == 3 and u in (0, 1):
                            r_scores(i * 4 + 4, u)
                        if c == 4 and u == 2:
                            r_out(i, 0)
                        if c == 4 and u == 5:
                            pe.wait_ge(sem("r_pl"), i * 2 + 2)
                            r_out(i, 1)
                        if c == 5 and u == 4:
                            pe.wait_ge(sem("r_norm"), i * 2 + 1)
                            r_gturn(i, 0)
            repeat(pe, 4, ret)

            def r_free(half):
                pe.wait_ge(sem("r_evA"), 23 + half)
                pe.wait_ge(sem("r_evD"), 23 + half)

            def r_turned():
                pe.wait_ge(sem("r_gcpA"), 7)
                pe.wait_ge(sem("r_gcpD"), 7)
                r_gturn(3, 1)
                pe.wait_ge(sem("r_gcpA"), 8)
                pe.wait_ge(sem("r_gcpD"), 8)
            rows("rout", 32, osh4, osl4, r_free, r_turned)

        @block.scalar
        def _(act):
            own = Own(act, act_own)
            A = nc.scalar.activation

            def split(base, i, per):
                slot, turn, n = slot_of(base + R, i, per)
                if isinstance(n, int) and n >= N_UNITS:
                    return
                act.wait_ge(landed[slot], 16 * (turn + 1))
                at_least(act, used, n - R + 1)
                A(whi[:, slot], raw[:, slot], ACT.Copy).then_inc(hi_done, 1)

            def stage(name, src, sh, kt0, i=0):
                kt = i * 4 + kt0
                if kt0 >= 4:
                    act.wait_ge(used, i * 8 + UNITS[name] + 2 * kt0 - 6)
                else:
                    act.wait_ge(used, UNITS[name] - 8)
                A(sh[:, kt0 % 4], src[:, kt] if isinstance(kt, int) else src[:, ds(kt, 1)].squeeze(1),
                      ACT.Copy).then_inc(sem(name + "_sthi"), 1)

            def rows(name, n_kt, src, sh, turned):
                base = UNITS[name]
                turned()
                for u in range(4):
                    split(base + u, 0, 4)
                for kt in (4, 5):
                    stage(name, src, sh, kt)

                def body(i, more=True):
                    for k in range(4):
                        for half in range(2):
                            split(base + 4 + 2 * k + half, i, 8)
                        if more or k < 2:
                            stage(name, src, sh, 6 + k, i)
                repeat(act, (n_kt - 4) // 4 - 1, body)
                body((n_kt - 4) // 4 - 1, more=False)

            pieces = [0, 2, 4, 8, 12, DK]

            def bring_piece(n):
                k0, k1 = pieces[n], pieces[n + 1]
                act.dma_start(xT_raw[:, k0:k1], xT[k0 * P:k1 * P].rearrange("(k p) t -> p k t", p=P)).then_inc(
                    sem(f"x_in{n}"), 16)
            bring_piece(0)
            bring_piece(1)
            act.wait_ge(dve_own, 1)
            A(warm[:, 1:2], warm[:, 0:1], ACT.Copy)
            act.wait_ge(sem("gain_in"), 16)

            def x_hi(k):
                if k in pieces:
                    act.wait_ge(sem(f"x_in{pieces.index(k)}"), 16)
                A(xh[:, k], xT_raw[:, k], ACT.Copy, scale=gpre_c[:, k:k + 1]).then_inc(sem("x_hi"), 1)
            for u in range(R):
                split(u - R, 0, R)
                x_hi(2 * u)
                x_hi(2 * u + 1)
                if u < 3:
                    bring_piece(u + 2)

            def x_squares():
                act.wait_ge(sem("x_tok_in"), 16)
                for t in range(T):
                    own.step(A(whole[1], x_tok[:, t], ACT.Square, accum_out=ssum[:, t:t + 1]))
                act.wait_ge(consts, 80)
                A(ident_r[:], ident[:], ACT.Copy).then_inc(sem("act_stage"), 1)


            def ev(name, c, pair, base, dst, scale, src=None):
                act.wait_ge(used, base)
                A(dst, acc[:, pair, 0] if src is None else src, ACT.Copy, scale=scale).then_inc(sem(name), 1)

            def cp(name, dst, src, c):
                act.wait_ge(sem(name + "_tr"), c + 1)
                A(dst, src, ACT.Copy).then_inc(sem(name + "_cpA"), 1)

            def flat(x_):
                return x_.rearrange("p a b -> p (a b)")

            def qkv(i):
                for c in range(2):
                    for u in range(8):
                        if c == 0 and u < 4 and isinstance(i, int) and i == 0:
                            x_hi(2 * (R + u))
                            x_hi(2 * (R + u) + 1)
                        split(UNITS["qk"] + 8 * c + u, i, 16)
                        first = isinstance(i, int) and i == 0
                        if u == 4 and not first:
                            cp("qkv", flat(qkT[:, ds(i * 8 + c * 4 - 4, 2)]), aux[:, 0], i * 2 + c - 1)
                        if c == 0 and u == 5 and first:
                            act.dma_start(x_tok[:], x.rearrange("(t p) n -> p t n", p=P)).then_inc(sem("x_tok_in"), 16)
                        if c == 1 and u == 3 and first:
                            x_squares()
                        if c == 1 and u == 5 and first:
                            act.wait_ge(sem("dve_stage"), DVE_STAGE["r1"])
                            ev("qkv_evA", 0, 1, UNITS["qk"] + 8, s0[:, 0], r1[:, 0:1])
                        if c == 1 and u == 7 and first:
                            cp("qkv", flat(qkT[:, 0:2]), aux[:, 0], 0)
                    if c == 1 or not first:
                        ev("qkv_evA", 0, 1 - c, i * 16 + 8 * (c + 1) + UNITS["qk"], s0[:, 0], r1[:, 0:1])
            repeat(act, 2, qkv)
            act.wait_ge(sem("masks"), 64)
            A(ntri[:], mask_raw[:, 0:P], ACT.Copy)
            A(nones[:], mask_raw[:, P:2 * P], ACT.Copy)
            A(mask_sb[:], mask_raw[:, 2 * P:5 * P], ACT.Copy)
            own.step(A(mask_mla[:], mask_raw[:, 5 * P:9 * P], ACT.Copy))
            act.wait_ge(sem("dve_stage"), DVE_STAGE["ang"])
            own.step(A(kk[:], ang[:], ACT.Sin))
            A(ang[:], angc[:], ACT.Sin).then_inc(sem("act_stage"), 1)
            for c in range(3):
                for u in range(8):
                    split(UNITS["lat"] + 8 * c + u, 0, 8)
                    if u == 4 and c == 0:
                        cp("qkv", flat(qkT[:, 12:14]), aux[:, 0], 3)
                ev("qkv_evA", 0, 0, UNITS["lat"] + 8 * (c + 1), lat[:, 0, c * 448:(c + 1) * 448], r1[:, 0:1],
                   acc[:, 1 - c % 2, 0, 0:448])

            def lat_hi(blocks):
                for b in blocks:
                    act.wait_ge(sem("lat_tr"), b // 2 + 1)
                    A(latTh[:, b], aux[:, b // 2 % 4, (b % 2) * TOK:(b % 2 + 1) * TOK], ACT.Copy,
                      scale=glat_c[:, b:b + 1]).then_inc(sem("lat_hi"), 1)

            def lat_squares():
                act.wait_ge(sem("qkv_evA"), 7)
                act.wait_ge(sem("qkv_evD"), 7)
                for t in range(T):
                    own.step(A(s0[:, 0], lat[:, t, 0:CW], ACT.Square, accum_out=ssum[:, t:t + 1]))
                    own.step(A(s0[:, 0, 0:256], lat[:, t, CW:Q_RANK], ACT.Square, accum_out=ssum[:, 2 + t:3 + t]))
                    own.step(A(s0[:, 0], lat[:, t, Q_RANK:Q_RANK + KV_RANK], ACT.Square, accum_out=ssum[:, 4 + t:5 + t]))
                A(s0[:, 0, 0:1], s0[:, 0, 0:1], ACT.Copy).then_inc(sem("act_stage"), 1)
            for c in range(2):
                for u in range(8):
                    split(UNITS["v"] + 8 * c + u, 0, 8)
                    if c == 0 and u == 3:
                        lat_hi(range(8))
                    if c == 0 and u == 5:
                        lat_squares()
                    if c == 0 and u == 7:
                        lat_hi(range(8, 10))
                        act.wait_ge(sem("kr_tr"), 1)
                        A(krh[:], aux[:, 1, 0:TOK], ACT.Copy).then_inc(sem("act_stage"), 1)
                ev("qkv_evA", 0, c, UNITS["v"] + 8 * (c + 1), v_sb[:, 0, c * CW:(c + 1) * CW], r1[:, 0:1])
            act.wait_ge(sem("dve_stage"), DVE_STAGE["rlat"])
            for c in range(4):
                for u in range(3):
                    split(UNITS["uq"] + 3 * c + u, 0, 4)
                    if u == 2 and c:
                        cp("uq", flat(qnT[:, 2 * c - 2:2 * c]), aux[:, 0], c - 1)
                ev("uq_evA", 0, 0, UNITS["uq"] + 3 * (c + 1), s0[:, 0, 0:384], rlat[:, 0:1], acc[:, c % 2, 0, 0:384])
            for c in range(4):
                for u in range(2):
                    split(UNITS["ukv"] + 2 * c + u, 0, 4)
                    if u == 1 and c == 0:
                        cp("uq", flat(qnT[:, 6:8]), aux[:, 0], 3)
                    if u == 1 and c:
                        cp("ukv", flat(knT[:, 2 * c - 2:2 * c]), aux[:, 2], c - 1)
                act.wait_ge(used, UNITS["ukv"] + 2 * (c + 1))
                src = acc[:, c % 2, 0].rearrange("p (h v d) -> p h v d", h=2, v=2)
                A(s0[:, 0, 0:256].rearrange("p (h d) -> p h d", h=2), src[:, :, 0], ACT.Copy, scale=rlat[:, 2:3])
                A(vm[:, 0, 2 * c:2 * c + 2], src[:, :, 1], ACT.Copy, scale=rlat[:, 2:3]).then_inc(sem("ukv_evA"), 1)
            act.wait_ge(sem("ukv_evA"), 4)

            def at(t_, n):
                return t_[:, n] if isinstance(n, int) else t_[:, ds(n, 1)].squeeze(1)

            def two(t_, n):
                return t_[:, n:n + 2] if isinstance(n, int) else t_[:, ds(n, 2)]

            def sb_stage(n):
                at_least(act, sem("sb_v"), n)
                A(sth[:, :, 0], two(qkT, n * 2), ACT.Copy, scale=HD ** -0.5)
                A(sth[:, :, 1], two(qkT, n * 2 + 8), ACT.Copy)
                for t in range(T):
                    last = A(sth[:, :, 2, t * P:(t + 1) * P],
                             v_sb[:, t, ds(n * 2 * HD, 2 * HD)].rearrange("p (h d) -> p h d", h=2), ACT.Copy)
                last.then_inc(sem("sb_sthi"), 1)

            def sb_softplus(n):
                act.wait_ge(sem("sb_z"), n + 1)
                own.step(A(sbt[:], aux[:, 0:2, 0:384], ACT.Abs))
                own.step(A(sbt[:], sbt[:], ACT.Exp, scale=-1.0))
                A(sbt[:], sbt[:], ACT.Ln, bias=1.0).then_inc(sem("sb_ln"), 1)

            def sb_rounded(n):
                act.wait_ge(sem("sb_L"), n + 1)
                A(sbh[:], sbt[:], ACT.Copy).then_inc(sem("sb_hi"), 1)

            def sb_weights(n):
                act.wait_ge(sem("sb_s"), n + 1)
                own.step(A(sbt[:], aux[:, 0:2, 0:384], ACT.Exp))
                A(sbh[:], sbt[:], ACT.Copy).then_inc(sem("sb_w"), 1)

            def sb_out(n):
                act.wait_ge(sem("sb_v"), n + 1)
                A(two(yTh, n * 2), aux[:, 2:4, 0:TOK], ACT.Copy).then_inc(sem("sb_yh"), 1)

            def gate_bias(i):
                act.dma_start(bias_t[:], b_gate[ds(i * CW, CW)].partition_broadcast(P)).then_inc(sem("bias_in"), 16)

            def sigmoid(i):
                act.wait_ge(sem("gate_dve"), i + 1)
                A(s0[:], s0[:], ACT.Sigmoid).then_inc(sem("gate_act"), 1)
                act.wait_ge(sem("gate_act"), i + 1)
                act.dma_start(gates_dram[:, ds(i * CW, CW)].rearrange("(t p) n -> p t n", p=P),
                              s0[:]).then_inc(sem("gate_out"), 16)

            def gates_sb(i):
                for c in range(2):
                    n = i * 2 + c
                    first = isinstance(n, int) and n == 0
                    if not first:
                        sb_out(n - 1)
                    sb_stage(n)
                    for u in range(8):
                        split(UNITS["gate"] + 8 * c + u, i, 16)
                        if u == 1:
                            if first:
                                cp("ukv", flat(knT[:, 6:8]), aux[:, 2], 3)
                            sb_softplus(n)
                        if u == 3:
                            sb_rounded(n)
                        if u == 5:
                            sb_weights(n)
                        if u == 6 and not first:
                            sigmoid(n - 1)
                        if u == 6:
                            gate_bias(n)
            repeat(act, 2, gates_sb, own)
            sb_out(3)
            act.wait_ge(sem("sb_y"), 4)

            def mla_stage(n, hh, i):
                at_least(act, sem("mla_v"), n - 1)
                A(mqh[:, hh, 0], at(qnT, n), ACT.Copy)
                A(mqh[:, hh, 1], at(qrT, i), ACT.Copy)
                A(mqh[:, hh, 2], at(knT, n), ACT.Copy)
                A(mqh[:, hh, 3].rearrange("p (t d) -> p t d", t=T), vm[:, :, ds(n, 1)].squeeze(2) if not isinstance(n, int) else vm[:, :, n],
                  ACT.Copy).then_inc(sem("mla_sthi"), 1)

            def mla_exp(n):
                act.wait_ge(sem("mla_max"), n + 1)
                for t in range(T):
                    last = A(mp[:, t], aux[:, 0, t * TOK:(t + 1) * TOK], ACT.Exp, bias=nmax[:, 0, t:t + 1],
                             accum_out=psum_[:, 0, t:t + 1])
                last.then_inc(sem("mla_exp"), 1)

            def mla_ph(n):
                act.wait_ge(sem("mla_tr"), n + 1)
                at_least(act, sem("mla_v"), n)
                A(flat(mph[:]), aux[:, 1], ACT.Copy).then_inc(sem("mla_ph"), 1)

            def mla_out(n):
                act.wait_ge(sem("mla_v"), n + 1)
                A(at(yTh, n + 8), aux[:, 2, 0:TOK], ACT.Copy).then_inc(sem("mla_yh"), 1)

            def gates_mla(i):
                for c in range(2):
                    n = i * 2 + c
                    mla_stage(n * 2, 0, n)
                    for u in range(8):
                        split(UNITS["gate"] + 32 + 8 * c + u, i, 16)
                        for hh in range(2):
                            if u == 3 * hh + 1:
                                mla_exp(n * 2 + hh)
                            if u == 3 * hh + 3:
                                mla_ph(n * 2 + hh)
                            if u == 3 * hh + 4:
                                mla_out(n * 2 + hh)
                        if u == 0:
                            mla_stage(n * 2 + 1, 1, n)
                        if u == 6:
                            sigmoid(n + 3)
                            gate_bias(n + 4)
            repeat(act, 2, gates_mla, own)

            def mix_cp(j):
                act.wait_ge(sem("mix_tr"), j + 1)
                A(flat(mixT[:, ds(j * 4, 2)]), aux[:, 0], ACT.Copy).then_inc(sem("mix_cpA"), 1)

            def mix(i):
                first = isinstance(i, int) and i == 0
                for u in range(8):
                    split(UNITS["mix"] + u, i, 8)
                    if u == 6 and isinstance(i, int) and i == 3:
                        for kt in range(4):
                            stage("out", mixT, osh1, kt)
                    if u == 0:
                        act.wait_ge(sem("gate_out"), 16 * (7 if first else 8))
                        at_least(act, sem("mix_dve"), i)
                        for b in range(2):
                            src = gates_dram[:, ds(i * CW + b * D, CW)].rearrange("(t p) n -> p t n", p=P)
                            act.dma_start(gt[:, b], src).then_inc(sem(f"gt_in{b}"), 16)
                        if first:
                            sigmoid(7)
                    if u == 4 and not (isinstance(i, int) and i == 0):
                        mix_cp(i - 1)
            act.wait_ge(sem("mla_y"), 8)
            repeat(act, 4, mix, last=True)

            def mix_turned():
                mix_cp(3)
                act.wait_ge(sem("mix_cpA"), 4)
                act.wait_ge(sem("mix_cpD"), 4)
            rows("out", DK, mixT, osh1, mix_turned)

            def bank_ready(name, end, b):
                if b < 7:
                    act.wait_ge(sem("bank_done"), BANKED[name] + b + 1)
                else:
                    act.wait_ge(used, end)

            def squares(name, end, b):
                bank_ready(name, end, b)
                if b >= 4:
                    act.wait_ge(sem("ss_banks"), BANKED[name] // 7 * 8 + b - 3)
                A((s0, s1)[b % 4 // 2][:, b % 2], banks[b], ACT.Square,
                  accum_out=ssum[:, b:b + 1]).then_inc(sem("ss_banks"), 1)

            def hi_of_tile(name, t, b, gain=None):
                act.wait_ge(sem(name + "_tr"), 4 * t + b + 1)
                src, dst = banks[4 * t + b], xh[:, 4 * b:4 * b + 4, t * P:(t + 1) * P]
                if gain is None:
                    last = A(dst, src.rearrange("p (k n) -> p k n", k=4), ACT.Copy)
                else:
                    for k in range(4):
                        last = A(dst[:, k], src[:, k * P:(k + 1) * P], ACT.Copy, scale=gain[:, 4 * b + k:4 * b + k + 1])
                last.then_inc(sem(name + "_xhi"), 1)

            def between(product, name, phase, gain=None, normed=True):
                for b in range(8 if normed else 0):
                    squares(product, UNITS[phase], b)
                    if b == 5:
                        split(UNITS[phase] - R, 0, R)
                if not normed:
                    split(UNITS[phase] - R, 0, R)
                split(UNITS[phase] - R + 1, 0, R)
                for b in range(4):
                    hi_of_tile(name, 0, b, gain)
                    if b < 2:
                        split(UNITS[phase] - R + b + 2, 0, R)
                for b in range(4):
                    hi_of_tile(name, 1, b, gain)

            between("out", "ffn", "up", gffn_c)

            def h_squares():
                for t in range(T):
                    act.wait_ge(sem("mixer_done"), 4 * t + 4)
                    act.wait_ge(sem("ss_ffn") if t else sem("ss_banks"), 2 if t else 8)
                    for half in range(2):
                        A((s0, s1)[half][:].rearrange("p a b -> p (a b)"), h[:, t, half * 1024:(half + 1) * 1024], ACT.Square,
                          accum_out=ssum[:, 8 + 2 * t + half:9 + 2 * t + half]).then_inc(sem("ss_ffn"), 1)

            def up_cp(j):
                act.wait_ge(sem("up_tr"), j + 1)
                A(flat(actT[:, ds(j * 4, 2)]), aux[:, 0], ACT.Copy).then_inc(sem("up_cpA"), 1)

            def up(i):
                for u in range(16):
                    split(UNITS["up"] + u, i, 16)
                    if u == 14 and isinstance(i, int) and i == 10:
                        for kt in range(4):
                            stage("down", actT, osh2, kt)
                    if u == 4 and not (isinstance(i, int) and i == 0):
                        up_cp(i - 1)
                    if u == 1 and isinstance(i, int) and i == 0:
                        h_squares()
                    if u == 7:
                        if isinstance(i, int) and i == 0:
                            act.wait_ge(sem("dve_stage"), DVE_STAGE["r2"])
                        act.wait_ge(used, i * 16 + UNITS["up"] + 8)
                        for t in range(T):
                            last = A(s0[:, t], acc[:, 0, t], ACT.Silu, scale=r2[:, t:t + 1])
                        last.then_inc(sem("up_act"), 1)
            repeat(act, 11, up, last=True)

            def up_turned():
                up_cp(10)
                act.wait_ge(sem("up_cpA"), 11)
                act.wait_ge(sem("up_cpD"), 11)
            rows("down", 44, actT, osh2, up_turned)
            between("down", "a", "aqkv")

            def a_ev(c, pair, done):
                act.wait_ge(used, done)
                at_least(act, sem("a_rot"), c)
                A(s0[:, 0], acc[:, pair, 0], ACT.Copy).then_inc(sem("a_evA"), 1)

            def a_sq(c):
                act.wait_ge(sem("a_evA"), c + 1)
                act.wait_ge(sem("a_evD"), c + 1)
                A(sqt[:], s0[:], ACT.Square).then_inc(sem("a_sq"), 1)

            def a_cp(c):
                act.wait_ge(sem("a_ctr"), c + 1)
                A(flat(aqT[:, ds(c * 4, 2)]), aux[:, 0], ACT.Copy).then_inc(sem("a_cpA"), 1)

            def a_q(i):
                for c in range(2):
                    for u in range(8):
                        split(UNITS["aqkv"] + 8 * c + u, i, 16)
                    if not (isinstance(i, int) and i == 0 and c == 0):
                        a_cp(i * 2 + c - 1)
                    a_ev(i * 2 + c, c, i * 16 + 8 * (c + 1) + UNITS["aqkv"])
                    a_sq(i * 2 + c)
            repeat(act, 2, a_q)
            for c in range(4, 6):
                for u in range(8):
                    split(UNITS["aqkv"] + 8 * c + u, 0, 8)
                a_cp(c - 1)
                if c == 4:
                    a_ev(c, 0, UNITS["aqkv"] + 40)
                    a_sq(c)
                else:
                    act.wait_ge(used, UNITS["aqkv"] + 48)
                    A(av[:, 0], acc[:, 1, 0], ACT.Copy).then_inc(sem("a_evA"), 1)

            def ag_q(n, e):
                at_least(act, sem("ag_s"), n - 1)
                A(aqh[:, e % 2], at(aqT, n), ACT.Copy).then_inc(sem("ag_qh"), 1)

            def ag_exp(n, e):
                act.wait_ge(sem("ag_max"), n + 1)
                at_least(act, sem("ag_ptr"), n - 1)
                for t in range(T):
                    last = A(ap_[:, e % 2, t], aux[:, e % 2, t * TOK:(t + 1) * TOK], ACT.Exp,
                             bias=nmax[:, e, t:t + 1], accum_out=psum_[:, e, t:t + 1])
                last.then_inc(sem("ag_exp"), 1)

            def ag_ph(n):
                act.wait_ge(sem("ag_ptr"), n + 1)
                at_least(act, sem("ag_v"), n)
                A(flat(aph[:]), aux[:, 2], ACT.Copy).then_inc(sem("ag_ph"), 1)

            def ag_cp(j, src):
                act.wait_ge(sem("ag_ctr"), j + 1)
                A(flat(agT[:, ds(j * 4, 2)]), src, ACT.Copy).then_inc(sem("ag_cpA"), 1)

            def ag_silu(g, pair):
                act.wait_ge(used, g * 8 + UNITS["ag"] + 8)
                at_least(act, sem("ag_gated"), g)
                A(s0[:], acc[:, pair], ACT.Silu).then_inc(sem("ag_silu"), 1)

            def ag(i):
                for c in range(2):
                    g = i * 2 + c
                    first = isinstance(g, int) and g == 0
                    if first:
                        act.wait_ge(sem("a_cpA"), 4)
                        act.wait_ge(sem("a_cpD"), 4)
                    ag_q(g * 4, 0)
                    ag_q(g * 4 + 1, 1)
                    if first:
                        act.wait_ge(sem("a_cpA"), 5)
                        act.wait_ge(sem("a_cpD"), 5)
                        act.wait_ge(sem("a_evA"), 6)
                        act.wait_ge(sem("a_evD"), 6)
                    at_least(act, sem("ag_v"), g * 4 - 4)
                    A(kvh[:, c, 0], at(aqT, g + 16), ACT.Copy)
                    A(kvh[:, c, 1].rearrange("p (t d) -> p t d", t=T), av[:, :, ds(g * HD, HD)],
                      ACT.Copy).then_inc(sem("ag_kvh"), 1)
                    for u in range(8):
                        split(UNITS["ag"] + 8 * c + u, i, 16)
                        if c == 1 and u == 6 and isinstance(i, int) and i == 1:
                            for kt in range(4):
                                stage("aout", agT, osh3, kt)
                        if u % 2 == 0:
                            ag_exp(g * 4 + u // 2, u // 2)
                        else:
                            ag_ph(g * 4 + u // 2)
                            if u < 5:
                                ag_q(g * 4 + u // 2 + 2, u // 2 + 2)
                        if u == 0 and not first:
                            ag_silu(g - 1, 1 - c)
                        if u == 4 and not first:
                            ag_cp(g - 1, acc[:, 1 - c, 0])
            repeat(act, 2, ag, last=True)
            ag_silu(3, 1)

            def ag_turned():
                ag_cp(3, aux[:, 0])
                act.wait_ge(sem("ag_cpA"), 4)
                act.wait_ge(sem("ag_cpD"), 4)
            rows("aout", DK, agT, osh3, ag_turned)
            between("aout", "r", "ret", normed=False)

            def log_decays():
                act.wait_ge(sem("tables_in"), 144)
                own.step(A(lg[:], lg[:], ACT.Exp, scale=-float(np.log(2.0))))
                A(lg[:], lg[:], ACT.Ln, scale=-1.0, bias=1.0).then_inc(sem("act_stage"), 1)

            def r_ev(i, c):
                act.wait_ge(used, i * 48 + 8 * (c + 1) + UNITS["ret"])
                if c == 0:
                    A(s0[:, 0], acc[:, 0, 0], ACT.Copy).then_inc(sem("r_evA"), 1)
                elif c == 1:
                    at_least(act, sem("r_rot"), i * 2 + 1)
                    A(s0[:, 0], acc[:, 1, 0], ACT.Copy, scale=R_QK ** -0.5).then_inc(sem("r_evA"), 1)
                elif c < 4:
                    if not (isinstance(i, int) and i == 0):
                        act.wait_ge(sem("r_o"), i * 2 + c - 3)
                    A(rvh[:, c - 2], acc[:, c % 2], ACT.Copy).then_inc(sem("r_evA"), 1)
                else:
                    if c == 5:
                        act.wait_ge(sem("r_gtr"), i * 2 + 1)
                    A(s0[:], acc[:, c % 2], ACT.Silu).then_inc(sem("r_evA"), 1)

            def r_qhi(n, which):
                act.wait_ge(sem("r_ctr"), n + 1)
                for b in range(2):
                    A(flat(rqh[:, which, 2 * b:2 * b + 2]), aux[:, b], ACT.Copy).then_inc(sem("r_qhi"), 1)

            def r_decay_exp(n, hh):
                act.wait_ge(sem("r_dexp"), n + 1)
                A(dmat[:, hh], dmat[:, hh], ACT.Exp).then_inc(sem("r_d"), 1)

            def r_phi(n, hh):
                act.wait_ge(sem("r_p"), n + 1)
                A(pth[:, hh], dmat[:, hh], ACT.Copy).then_inc(sem("r_ph"), 1)

            def r_gcp(n):
                act.wait_ge(sem("r_gtr"), n + 1)
                A(flat(rgT[:, ds(n * 4, 2)]), aux[:, 0], ACT.Copy).then_inc(sem("r_gcpA"), 1)

            def ret(i):
                first = isinstance(i, int) and i == 0
                for c in range(6):
                    for u in range(8):
                        split(UNITS["ret"] + 8 * c + u, i, 48)
                        if c == 5 and u == 6 and isinstance(i, int) and i == 3:
                            for kt in range(4):
                                stage("rout", rgT, osh4, kt)
                        if c == 0 and u == 4 and not first:
                            r_gcp(i * 2 - 1)
                        if c == 0 and u == 5 and first:
                            log_decays()
                        if c == 1 and u == 2:
                            r_decay_exp(i * 2, 0)
                            r_decay_exp(i * 2 + 1, 1)
                        if c == 1 and u == 5:
                            r_qhi(i * 2, 0)
                        if c == 2 and u == 5:
                            r_qhi(i * 2 + 1, 1)
                        if c == 3 and u == 3:
                            r_phi(i * 2, 0)
                            r_phi(i * 2 + 1, 1)
                        if c == 5 and u == 5:
                            r_gcp(i * 2)
                    r_ev(i, c)
            repeat(act, 4, ret, last=True)

            def r_turned():
                r_gcp(7)
                act.wait_ge(sem("r_gcpA"), 8)
                act.wait_ge(sem("r_gcpD"), 8)
            rows("rout", 32, rgT, osh4, r_turned)

            act.wait_ge(sem("shift_in"), 1)
            for b in range(4):
                cols = slice(b * CW, (b + 1) * CW)
                A(h[:, 0, cols], h[:, 0, cols], ACT.Identity, scale=rs_y[:, 0:1], bias=shift[:, 0:1]).then_inc(sem("scaled"), 1)

        @block.vector
        def _(dve):
            own = Own(dve, dve_own)
            V = nc.vector

            def f32(x_):
                return x_.bitcast(F32)

            def flat(x_):
                return x_.rearrange("p a b -> p (a b)")

            def at(t_, n):
                return t_[:, n] if isinstance(n, int) else t_[:, ds(n, 1)].squeeze(1)

            def split(base, i, per):
                slot, turn, n = slot_of(base + R, i, per)
                if isinstance(n, int) and n >= N_UNITS:
                    return
                dve.wait_ge(hi_done, n + 1)
                at_least(dve, used, n - R + 1)
                V.tensor_tensor(wlo[:, slot], raw[:, slot], f32(whi[:, slot]), ALU.subtract).then_inc(lo_done, 1)

            def stage(name, src, sh, sl, kt0, i=0):
                kt = i * 4 + kt0
                dve.wait_ge(sem(name + "_sthi"), kt + 1)
                if kt0 >= 4:
                    dve.wait_ge(used, i * 8 + UNITS[name] + 2 * kt0 - 6)
                else:
                    dve.wait_ge(used, UNITS[name] - 8)
                V.tensor_tensor(sl[:, kt0 % 4], at(src, kt), f32(sh[:, kt0 % 4]), ALU.subtract).then_inc(sem(name + "_stage"), 1)

            def rows(name, n_kt, src, sh, sl, turned):
                base = UNITS[name]
                turned()
                for u in range(4):
                    split(base + u, 0, 4)
                for kt in (4, 5):
                    stage(name, src, sh, sl, kt)

                def body(i, more=True):
                    for k in range(4):
                        for half in range(2):
                            split(base + 4 + 2 * k + half, i, 8)
                        if more or k < 2:
                            stage(name, src, sh, sl, 6 + k, i)
                repeat(dve, (n_kt - 4) // 4 - 1, body)
                body((n_kt - 4) // 4 - 1, more=False)

            def rsqrt(n):
                v, y, t_, ti = rs_v[:, 0:n], rs_y[:, 0:n], rs_t[:, 0:n], rs_i[:, 0:n]
                own.step(V.tensor_scalar(ti, v.bitcast(I32), 1, None, ALU.logical_shift_right))
                own.step(V.tensor_scalar(y.bitcast(I32), ti, -1.0, RSQRT_SEED, ALU.mult, ALU.add))
                for _ in range(3):
                    own.step(V.tensor_tensor(t_, y, y, ALU.mult))
                    own.step(V.scalar_tensor_tensor(t_, t_, -0.5, v, ALU.mult, ALU.mult))
                    own.step(V.scalar_tensor_tensor(y, t_, 1.5, y, ALU.add, ALU.mult))

            def rsqrt_one(c, meanwhile):
                v, y, t_, ti, vh = (x_[:, c:c + 1] for x_ in (rs_v, rs_y, rs_t, rs_i, rs_h))
                own.mark(V.tensor_scalar(ti, v.bitcast(I32), 1, None, ALU.logical_shift_right))
                own.step(V.tensor_scalar(vh, v, -0.5, None, ALU.mult))
                seeded = V.tensor_scalar(y.bitcast(I32), ti, -1.0, RSQRT_SEED, ALU.mult, ALU.add)
                for n in range(3):
                    own.mark(seeded if n == 0 else V.scalar_tensor_tensor(y, t_, 1.5, y, ALU.add, ALU.mult))
                    ready = own.now()
                    meanwhile(n)
                    dve.wait_ge(dve_own, ready)
                    own.step(V.scalar_tensor_tensor(t_, y, vh, y, ALU.mult, ALU.mult))
                own.mark(V.scalar_tensor_tensor(y, t_, 1.5, y, ALU.add, ALU.mult))
                meanwhile(3)
                own.wait()

            own.step(V.memset(warm[:], 0.0))

            def x_lo(k):
                dve.wait_ge(sem("x_hi"), k + 1)
                V.scalar_tensor_tensor(xl[:, k], xT_raw[:, k], gpre_c[:, k:k + 1], f32(xh[:, k]),
                                       ALU.mult, ALU.subtract).then_inc(sem("x_split"), 1)
            for u in range(R):
                split(u - R, 0, R)
                x_lo(2 * u)
                x_lo(2 * u + 1)

            def first_norm():
                dve.wait_ge(sem("act_stage"), ACT_STAGE["ss_x"])
                own.step(V.tensor_scalar(rs_v[:, 0:2], ssum[:, 0:2], 1.0 / D, EPS, ALU.mult, ALU.add))
                rsqrt(2)
                V.tensor_copy(r1[:], rs_y[:, 0:2]).then_inc(sem("dve_stage"), 1)
                dve.wait_ge(sem("dve_stage"), DVE_STAGE["r1"])

            def ev(name, dst, src, scale, done):
                dve.wait_ge(used, done)
                V.tensor_scalar(dst, src, scale, None, ALU.mult).then_inc(sem(name), 1)

            def cp(name, dst, src, c):
                dve.wait_ge(sem(name + "_tr"), c + 1)
                V.tensor_copy(dst, src).then_inc(sem(name + "_cpD"), 1)

            def qkv(i):
                for c in range(2):
                    for u in range(8):
                        if c == 0 and u < 4 and isinstance(i, int) and i == 0:
                            x_lo(2 * (R + u))
                            x_lo(2 * (R + u) + 1)
                        split(UNITS["qk"] + 8 * c + u, i, 16)
                        first = isinstance(i, int) and i == 0
                        if u == 4 and not first:
                            cp("qkv", flat(qkT[:, ds(i * 8 + c * 4 - 2, 2)]), aux[:, 1], i * 2 + c - 1)
                        if c == 1 and u == 4 and first:
                            first_norm()
                        if c == 1 and u == 5 and first:
                            ev("qkv_evD", s0[:, 1], acc[:, 1, 1], r1[:, 1:2], UNITS["qk"] + 8)
                        if c == 1 and u == 7 and first:
                            cp("qkv", flat(qkT[:, 2:4]), aux[:, 1], 0)
                    if c == 1 or not first:
                        ev("qkv_evD", s0[:, 1], acc[:, 1 - c, 1], r1[:, 1:2], i * 16 + 8 * (c + 1) + UNITS["qk"])
            repeat(dve, 2, qkv)
            dve.wait_ge(consts, 80)
            own.step(V.tensor_copy(pos_f[:], pos_i[:]))
            for t in range(T):
                own.mark(V.tensor_scalar(ang[:, t], invf[:], pos_f[:, t:t + 1], None, ALU.mult))
            own.wait()
            own.step(V.tensor_scalar(kk[:], ang[:], float(1 / (2 * np.pi)), ROUND, ALU.mult, ALU.add))
            own.step(V.tensor_scalar(kk[:], kk[:], -ROUND, None, ALU.add))
            rest = 2 * np.pi
            for bits in (5, 14, 23, 40):
                part = np.floor(rest * 2.0 ** bits) / 2.0 ** bits
                rest -= part
                own.step(V.scalar_tensor_tensor(ang[:], kk[:], float(-part), ang[:], ALU.mult, ALU.add))
            own.step(V.tensor_scalar(angc[:], ang[:], float(np.pi / 2), None, ALU.add))
            own.step(V.tensor_scalar(kk[:], angc[:], float(np.pi), float(-2 * np.pi), ALU.is_gt, ALU.mult))
            own.step(V.tensor_tensor(angc[:], angc[:], kk[:], ALU.add))
            own.step(V.tensor_scalar(angc[:], angc[:], PI_F, -PI_F, ALU.min, ALU.max))
            V.tensor_scalar(ang[:], ang[:], PI_F, -PI_F, ALU.min, ALU.max).then_inc(sem("dve_stage"), 1)
            dve.wait_ge(sem("act_stage"), ACT_STAGE["sines"])
            for half in range(2):
                cols = slice(half * 32, half * 32 + 32)
                own.mark(V.tensor_copy(cos_m[:, :, cols], ang[:]))
                own.mark(V.tensor_scalar(sin_m[:, :, cols], kk[:], -1.0 if half == 0 else 1.0, None, ALU.mult))
            own.wait()

            for c in range(3):
                for u in range(8):
                    split(UNITS["lat"] + 8 * c + u, 0, 8)
                    if u == 4 and c == 0:
                        cp("qkv", flat(qkT[:, 14:16]), aux[:, 1], 3)
                ev("qkv_evD", lat[:, 1, c * 448:(c + 1) * 448], acc[:, 1 - c % 2, 1, 0:448], r1[:, 1:2],
                   UNITS["lat"] + 8 * (c + 1))

            def rotate(dst, tmp, src, cos, sin, half):
                own.mark(V.tensor_tensor(dst, src, cos, ALU.mult))
                own.mark(V.tensor_tensor(tmp[:, :, 0:half], src[:, :, half:2 * half], sin[:, :, 0:half], ALU.mult))
                own.step(V.tensor_tensor(tmp[:, :, half:2 * half], src[:, :, 0:half], sin[:, :, half:2 * half], ALU.mult))
                return V.tensor_tensor(dst, dst, tmp, ALU.add)

            def k_rope():
                dve.wait_ge(sem("qkv_evA"), 7)
                dve.wait_ge(sem("qkv_evD"), 7)
                own.step(rotate(rtm2[:, :, 0:ROPE], rtmp[:, :, 0:ROPE], lat[:, :, 1280:1344], cos_m[:], sin_m[:], 32))
                V.tensor_copy(krot[:, :, 0:ROPE], rtm2[:, :, 0:ROPE])
                V.tensor_copy(krot[:, :, ROPE:P], rtm2[:, :, 0:ROPE]).then_inc(sem("dve_stage"), 1)

            def lat_norms():
                dve.wait_ge(sem("act_stage"), ACT_STAGE["ss_lat"])
                own.step(V.tensor_tensor(ssum[:, 0:2], ssum[:, 0:2], ssum[:, 2:4], ALU.add))
                own.mark(V.tensor_scalar(rs_v[:, 0:2], ssum[:, 0:2], 1.0 / Q_RANK, EPS, ALU.mult, ALU.add))
                own.step(V.tensor_scalar(rs_v[:, 2:4], ssum[:, 4:6], 1.0 / KV_RANK, EPS, ALU.mult, ALU.add))
                rsqrt(4)
                own.mark(V.tensor_scalar(rlat[:, 0:2], rs_y[:, 0:2], QK_DIM ** -0.5, None, ALU.mult))
                own.step(V.tensor_copy(rlat[:, 2:4], rs_y[:, 2:4]))
                V.tensor_copy(mark[:], rs_y[:, 0:1]).then_inc(sem("dve_stage"), 1)

            def lat_lo(blocks):
                for b in blocks:
                    dve.wait_ge(sem("lat_hi"), b // 2 * 2 + 2)
                    V.scalar_tensor_tensor(latTl[:, b], aux[:, b // 2 % 4, (b % 2) * TOK:(b % 2 + 1) * TOK],
                                           glat_c[:, b:b + 1], f32(latTh[:, b]), ALU.mult, ALU.subtract).then_inc(sem("lat_lo"), 1)
            for c in range(2):
                for u in range(8):
                    split(UNITS["v"] + 8 * c + u, 0, 8)
                    if c == 0 and u == 1:
                        k_rope()
                    if c == 0 and u == 3:
                        lat_lo(range(8))
                    if c == 0 and u == 7:
                        lat_lo(range(8, 10))
                        dve.wait_ge(sem("act_stage"), ACT_STAGE["kr_hi"])
                        V.tensor_tensor(krl[:], aux[:, 1, 0:TOK], f32(krh[:]), ALU.subtract).then_inc(sem("kr_lo"), 1)
                    if c == 1 and u == 1:
                        lat_norms()
                ev("qkv_evD", v_sb[:, 1, c * CW:(c + 1) * CW], acc[:, c, 1], r1[:, 1:2], UNITS["v"] + 8 * (c + 1))
            dve.wait_ge(sem("qkv_evD"), 9)

            for c in range(4):
                for u in range(3):
                    split(UNITS["uq"] + 3 * c + u, 0, 4)
                    if u == 2 and c:
                        cp("uq", at(qrT, c - 1), aux[:, 1, 0:TOK], c - 1)
                ev("uq_evD", s0[:, 1, 0:384], acc[:, c % 2, 1, 0:384], rlat[:, 1:2], UNITS["uq"] + 3 * (c + 1))
                dve.wait_ge(sem("uq_evA"), c + 1)
                dve.wait_ge(sem("uq_evD"), c + 1)
                for t in range(T):
                    src = s0[:, t, 0:384].rearrange("p (h d) -> p h d", h=2)[:, :, HD:QK_DIM]
                    last = rotate(s1[:, t, 0:P].rearrange("p (h d) -> p h d", h=2),
                                  rtmp[:, t].rearrange("p (h d) -> p h d", h=2), src,
                                  cos_m[:, t:t + 1].broadcast_to([P, 2, ROPE]), sin_m[:, t:t + 1].broadcast_to([P, 2, ROPE]), 32)
                last.then_inc(sem("uq_rope"), 1)
            for c in range(4):
                for u in range(2):
                    split(UNITS["ukv"] + 2 * c + u, 0, 4)
                    if u == 1 and c == 0:
                        cp("uq", at(qrT, 3), aux[:, 1, 0:TOK], 3)
                dve.wait_ge(used, UNITS["ukv"] + 2 * (c + 1))
                at_least(dve, sem("ukv_tr"), c)
                src = acc[:, c % 2, 1].rearrange("p (h v d) -> p h v d", h=2, v=2)
                V.tensor_scalar(s0[:, 1, 0:256].rearrange("p (h d) -> p h d", h=2), src[:, :, 0], rlat[:, 3:4], None, ALU.mult)
                V.tensor_scalar(vm[:, 1, 2 * c:2 * c + 2], src[:, :, 1], rlat[:, 3:4], None, ALU.mult).then_inc(sem("ukv_evD"), 1)

            dve.wait_ge(sem("ukv_evD"), 4)

            def two(t_, n):
                return t_[:, n:n + 2] if isinstance(n, int) else t_[:, ds(n, 2)]

            def sb_stage(n):
                dve.wait_ge(sem("sb_sthi"), n + 1)
                V.scalar_tensor_tensor(stl[:, :, 0], two(qkT, n * 2), HD ** -0.5, f32(sth[:, :, 0]), ALU.mult, ALU.subtract)
                V.tensor_tensor(stl[:, :, 1], two(qkT, n * 2 + 8), f32(sth[:, :, 1]), ALU.subtract)
                for t in range(T):
                    tok = slice(t * P, (t + 1) * P)
                    last = V.tensor_tensor(stl[:, :, 2, tok],
                                           v_sb[:, t, ds(n * 2 * HD, 2 * HD)].rearrange("p (h d) -> p h d", h=2),
                                           f32(sth[:, :, 2, tok]), ALU.subtract)
                last.then_inc(sem("sb_stage"), 1)

            def sb_softplus(n):
                dve.wait_ge(sem("sb_ln"), n + 1)
                V.scalar_tensor_tensor(sbt[:], aux[:, 0:2, 0:384], 0.0, sbt[:], ALU.max, ALU.add).then_inc(sem("sb_L"), 1)

            def sb_rest(n, hi):
                dve.wait_ge(sem(hi), n + 1)
                if hi == "sb_hi":
                    dve.wait_ge(sem("sb_L"), n + 1)
                V.tensor_tensor(sbl[:], sbt[:], f32(sbh[:]), ALU.subtract).then_inc(sem("sb_split"), 1)

            def sb_out(n):
                dve.wait_ge(sem("sb_yh"), n + 1)
                V.tensor_tensor(two(yTl, n * 2), aux[:, 2:4, 0:TOK], f32(two(yTh, n * 2)), ALU.subtract).then_inc(sem("sb_y"), 1)

            def gate_ev(i, pair, done):
                dve.wait_ge(sem("bias_in"), 16 * (i + 1) if isinstance(i, int) else i * 16 + 16)
                at_least(dve, sem("gate_out"), i * 16)
                dve.wait_ge(used, done)
                for t in range(T):
                    last = V.scalar_tensor_tensor(s0[:, t], acc[:, pair, t], r1[:, t:t + 1], bias_t[:], ALU.mult, ALU.add)
                last.then_inc(sem("gate_dve"), 1)

            def gates_sb(i):
                for c in range(2):
                    n = i * 2 + c
                    first = isinstance(n, int) and n == 0
                    if not first:
                        sb_out(n - 1)
                    sb_stage(n)
                    for u in range(8):
                        split(UNITS["gate"] + 8 * c + u, i, 16)
                        if u == 1:
                            sb_softplus(n)
                        if u == 3:
                            sb_rest(n, "sb_hi")
                        if u == 4 and not first:
                            gate_ev(n - 1, 1 - c, n * 8 + UNITS["gate"])
                        if u == 5:
                            sb_rest(n, "sb_w")
            repeat(dve, 2, gates_sb)
            sb_out(3)
            dve.wait_ge(sem("sb_y"), 4)

            def mla_stage(n, hh, i):
                dve.wait_ge(sem("mla_sthi"), n + 1)
                V.tensor_tensor(mql[:, hh, 0], at(qnT, n), f32(mqh[:, hh, 0]), ALU.subtract)
                V.tensor_tensor(mql[:, hh, 1], at(qrT, i), f32(mqh[:, hh, 1]), ALU.subtract)
                V.tensor_tensor(mql[:, hh, 2], at(knT, n), f32(mqh[:, hh, 2]), ALU.subtract)
                V.tensor_tensor(mql[:, hh, 3].rearrange("p (t d) -> p t d", t=T),
                                vm[:, :, ds(n, 1)].squeeze(2) if not isinstance(n, int) else vm[:, :, n],
                                f32(mqh[:, hh, 3]).rearrange("p (t d) -> p t d", t=T), ALU.subtract).then_inc(sem("mla_stage"), 1)

            def mla_softmax(n):
                dve.wait_ge(sem("mla_s"), n + 1)
                V.tensor_reduce(nmax[:, 0], aux[:, 0].rearrange("p (t k) -> p t k", t=T), AX.X, ALU.max,
                                negate=True).then_inc(sem("mla_max"), 1)
                dve.wait_ge(sem("mla_exp"), n + 1)
                own.step(V.reciprocal(prec[:, 0], psum_[:, 0]))
                for t in range(T):
                    last = V.tensor_scalar(mp[:, t], mp[:, t], prec[:, 0, t:t + 1], None, ALU.mult)
                last.then_inc(sem("mla_norm"), 1)

            def mla_pl(n):
                dve.wait_ge(sem("mla_ph"), n + 1)
                V.tensor_tensor(flat(mpl[:]), aux[:, 1], f32(flat(mph[:])), ALU.subtract).then_inc(sem("mla_pl"), 1)

            def mla_out(n):
                dve.wait_ge(sem("mla_yh"), n + 1)
                V.tensor_tensor(at(yTl, n + 8), aux[:, 2, 0:TOK], f32(at(yTh, n + 8)), ALU.subtract).then_inc(sem("mla_y"), 1)

            def gates_mla(i):
                for c in range(2):
                    n = i * 2 + c
                    mla_stage(n * 2, 0, n)
                    for u in range(8):
                        split(UNITS["gate"] + 32 + 8 * c + u, i, 16)
                        if u == 5:
                            gate_ev(n + 3, 1 - c, n * 8 + UNITS["gate"] + 32)
                        for hh in range(2):
                            if u == 3 * hh + 1:
                                mla_softmax(n * 2 + hh)
                            if u == 3 * hh + 3:
                                mla_pl(n * 2 + hh)
                            if u == 3 * hh + 4:
                                mla_out(n * 2 + hh)
                        if u == 0:
                            mla_stage(n * 2 + 1, 1, n)
            repeat(dve, 2, gates_mla, own)
            gate_ev(7, 1, UNITS["mix"])
            dve.wait_ge(sem("mla_y"), 8)
            V.tensor_copy(mark[:], rs_y[:, 0:1]).then_inc(sem("dve_stage"), 1)

            def mix_cp(j):
                dve.wait_ge(sem("mix_tr"), j + 1)
                V.tensor_copy(flat(mixT[:, ds(j * 4 + 2, 2)]), aux[:, 1]).then_inc(sem("mix_cpD"), 1)

            def mix(i):
                for u in range(8):
                    split(UNITS["mix"] + u, i, 8)
                    if u == 6 and isinstance(i, int) and i == 3:
                        for kt in range(4):
                            stage("out", mixT, osh1, osl1, kt)
                    if u == 4 and not (isinstance(i, int) and i == 0):
                        mix_cp(i - 1)
                    if u == 4:
                        at_least(dve, sem("gate_out"), 16 * 8)
                        dve.wait_ge(sem("gt_in0"), i * 16 + 16)
                        for t in range(T):
                            last = V.tensor_tensor(s0[:, t], acc[:, 0, t], gt[:, 0, t], ALU.mult)
                        last.then_inc(sem("mix_free0"), 1)
                dve.wait_ge(sem("gt_in1"), i * 16 + 16)
                dve.wait_ge(used, i * 8 + UNITS["mix"] + 8)
                for t in range(T):
                    last = V.tensor_tensor(s1[:, t], acc[:, 1, t], gt[:, 1, t], ALU.mult)
                last.then_inc(sem("mix_free1"), 1)
                dve.wait_ge(sem("mix_free1"), i + 1)
                V.tensor_tensor(s0[:], s0[:], s1[:], ALU.add).then_inc(sem("mix_dve"), 1)
            repeat(dve, 4, mix, last=True)

            def mix_turned():
                mix_cp(3)
                dve.wait_ge(sem("mix_cpA"), 4)
                dve.wait_ge(sem("mix_cpD"), 4)
            rows("out", DK, mixT, osh1, osl1, mix_turned)

            def bank_ready(name, end, b):
                if b < 7:
                    dve.wait_ge(sem("bank_done"), BANKED[name] + b + 1)
                else:
                    dve.wait_ge(used, end)

            def lo_of_tile(name, t, b, gain=None):
                dve.wait_ge(sem(name + "_xhi"), 4 * t + b + 1)
                src, tok = banks[4 * t + b], slice(t * P, (t + 1) * P)
                if gain is None:
                    last = V.tensor_tensor(xl[:, 4 * b:4 * b + 4, tok], src.rearrange("p (k n) -> p k n", k=4),
                                           f32(xh[:, 4 * b:4 * b + 4, tok]), ALU.subtract)
                else:
                    for k in range(4):
                        kt = 4 * b + k
                        last = V.scalar_tensor_tensor(xl[:, kt, tok], src[:, k * P:(k + 1) * P], gain[:, kt:kt + 1],
                                                      f32(xh[:, kt, tok]), ALU.mult, ALU.subtract)
                last.then_inc(sem(name + "_xlo"), 1)

            def add_normed(n_before, name, gain_row, tmp, done, gain=None):
                def cols(x_, b):
                    return x_[:, b * CW:(b + 1) * CW]

                for t in range(T):
                    for b in range(4):
                        dve.wait_ge(sem("ss_banks"), n_before + 4 * t + b + 1)
                        if t == 1:
                            dve.wait_ge(sem(done), b + 1)
                        own.mark(V.tensor_tensor(cols(tmp, b), banks[4 * t + b], cols(gain_row, b), ALU.mult))
                        if t == 1 and b:
                            lo_of_tile(name, 0, b - 1, gain)
                    if t == 1:
                        lo_of_tile(name, 0, 3, gain)
                    own.step(V.tensor_reduce(rs_t[:, 8 + t:9 + t], ssum[:, 4 * t:4 * t + 4], AX.X, ALU.add))
                    own.step(V.tensor_scalar(rs_v[:, t:t + 1], rs_t[:, 8 + t:9 + t], 1.0 / D, EPS, ALU.mult, ALU.add))
                    rsqrt_one(t, lambda b: None)
                    for b in range(4):
                        V.scalar_tensor_tensor(cols(h[:, t], b), cols(tmp, b), rs_y[:, t:t + 1], cols(h[:, t], b),
                                               ALU.mult, ALU.add).then_inc(sem(done), 1)
                for b in range(4):
                    lo_of_tile(name, 1, b, gain)

            dve.wait_ge(sem("x_again"), 16)
            dve.wait_ge(sem("gains_in"), 16)
            add_normed(0, "ffn", gbc1, tmp1, "mixer_done", gffn_c)

            def ffn_norm():
                dve.wait_ge(sem("ss_ffn"), 4)
                own.step(V.tensor_tensor(ssum[:, 0:2], ssum[:, 8:12:2], ssum[:, 9:13:2], ALU.add))
                own.step(V.tensor_scalar(rs_v[:, 0:2], ssum[:, 0:2], 1.0 / D, EPS, ALU.mult, ALU.add))
                rsqrt(2)
                own.step(V.tensor_copy(r2[:], rs_y[:, 0:2]))
                V.tensor_copy(mark[:], rs_y[:, 0:1]).then_inc(sem("dve_stage"), 1)

            def up_cp(j):
                dve.wait_ge(sem("up_tr"), j + 1)
                V.tensor_copy(flat(actT[:, ds(j * 4 + 2, 2)]), aux[:, 1]).then_inc(sem("up_cpD"), 1)

            def up(i):
                for u in range(16):
                    split(UNITS["up"] + u, i, 16)
                    if u == 14 and isinstance(i, int) and i == 10:
                        for kt in range(4):
                            stage("down", actT, osh2, osl2, kt)
                    if u == 3 and isinstance(i, int) and i == 0:
                        ffn_norm()
                    if u == 4 and not (isinstance(i, int) and i == 0):
                        up_cp(i - 1)
                dve.wait_ge(used, i * 16 + UNITS["up"] + 16)
                dve.wait_ge(sem("up_act"), i + 1)
                for t in range(T):
                    last = V.scalar_tensor_tensor(s0[:, t], acc[:, 1, t], r2[:, t:t + 1], s0[:, t], ALU.mult, ALU.mult)
                last.then_inc(sem("up_dve"), 1)
            repeat(dve, 11, up, last=True)

            def up_turned():
                up_cp(10)
                dve.wait_ge(sem("up_cpA"), 11)
                dve.wait_ge(sem("up_cpD"), 11)
            rows("down", 44, actT, osh2, osl2, up_turned)
            dve.wait_ge(sem("gains_in"), 32)
            add_normed(8, "a", gbc2, tmp2, "ffn_done")

            dve.wait_ge(sem("tables_in"), 64)
            for w in range(2):
                gain = gtab[:, w:w + 1]
                own.mark(V.tensor_tensor(cgs[:, 2 * w], ctab[:, 0], gain.broadcast_to([P, T, HD]), ALU.mult))
                for q in range(4):
                    other = q ^ 1
                    own.mark(V.tensor_tensor(cgs[:, 2 * w + 1, :, 32 * q:32 * q + 32], ctab[:, 1, :, 32 * q:32 * q + 32],
                                             gain[:, :, 32 * other:32 * other + 32].broadcast_to([P, T, 32]), ALU.mult))
            own.wait()

            def a_ev(c, pair, done):
                dve.wait_ge(used, done)
                V.tensor_copy(s0[:, 1], acc[:, pair, 1]).then_inc(sem("a_evD"), 1)

            def heads_rotate(dst, tmp, src, cos, sin, heads, quarter):
                n = 4 * quarter
                dv, sv = (x_.rearrange("p (h d) -> p h d", h=heads) for x_ in (dst, src))
                tv = tmp.rearrange("p (h d) -> p h d", h=heads)
                own.mark(V.tensor_tensor(dv, sv, cos.broadcast_to([P, heads, n]), ALU.mult))
                for q in range(4):
                    other = (q ^ 1) * quarter
                    own.mark(V.tensor_tensor(tv[:, :, q * quarter:(q + 1) * quarter], sv[:, :, other:other + quarter],
                                             sin[:, :, q * quarter:(q + 1) * quarter].broadcast_to([P, heads, quarter]),
                                             ALU.mult))
                own.wait()
                return V.tensor_tensor(dst, dst, tmp, ALU.add)

            def a_norm(c, w):
                dve.wait_ge(sem("a_sq"), c + 1)
                own.step(V.tensor_reduce(ssum[:, 0:8].rearrange("p (t h) -> p t h", t=T),
                                         sqt[:].rearrange("p t (h d) -> p t h d", h=4), AX.X, ALU.add))
                own.step(V.tensor_scalar(rs_v[:, 0:8], ssum[:, 0:8], 1.0 / HD, EPS, ALU.mult, ALU.add))
                rsqrt(8)
                if w == 0:
                    own.step(V.tensor_scalar(rs_y[:, 0:8], rs_y[:, 0:8], HD ** -0.5, None, ALU.mult))

            def a_rotate(c, w, t):
                at_least(dve, sem("a_ctr"), c)
                own.step(heads_rotate(s1[:, t], sqt[:, t], s0[:, t], cgs[:, 2 * w, t:t + 1], cgs[:, 2 * w + 1, t:t + 1], 4, 32))
                v = s1[:, t].rearrange("p (h d) -> p h d", h=4)
                last = V.tensor_tensor(v, v, rs_y[:, 4 * t:4 * t + 4].unsqueeze(2).broadcast_to([P, 4, HD]), ALU.mult)
                if t == 1:
                    last.then_inc(sem("a_rot"), 1)

            def a_cp(c):
                dve.wait_ge(sem("a_ctr"), c + 1)
                V.tensor_copy(flat(aqT[:, ds(c * 4 + 2, 2)]), aux[:, 1]).then_inc(sem("a_cpD"), 1)

            def a_part(base, i, per, c, skip_cp, w):
                for u in range(8):
                    split(base + u, i, per)
                    if u == 0 and not skip_cp:
                        a_norm(c - 1, w)
                    if u in (1, 3) and not skip_cp:
                        a_rotate(c - 1, w, u // 2)
                if not skip_cp:
                    a_cp(c - 1)

            def a_q(i):
                for c in range(2):
                    n = i * 2 + c
                    if c == 0 and isinstance(i, int) and i == 0:
                        for u in range(8):
                            split(UNITS["aqkv"] + u, 0, 16)
                    else:
                        a_part(UNITS["aqkv"] + 8 * c, i, 16, n, False, 0)
                    a_ev(n, c, i * 16 + 8 * (c + 1) + UNITS["aqkv"])
            for i in range(2):
                a_q(i)
            a_part(UNITS["aqkv"] + 32, 0, 8, 4, False, 0)
            a_ev(4, 0, UNITS["aqkv"] + 40)
            a_part(UNITS["aqkv"] + 40, 0, 8, 5, False, 1)
            dve.wait_ge(used, UNITS["aqkv"] + 48)
            V.tensor_copy(av[:, 1], acc[:, 1, 1]).then_inc(sem("a_evD"), 1)

            def ag_q(n, e):
                dve.wait_ge(sem("ag_qh"), n + 1)
                V.tensor_tensor(aql[:, e % 2], at(aqT, n), f32(aqh[:, e % 2]), ALU.subtract).then_inc(sem("ag_q"), 1)

            def ag_max(n, e):
                dve.wait_ge(sem("ag_s"), n + 1)
                V.tensor_reduce(nmax[:, e], aux[:, e % 2].rearrange("p (t k) -> p t k", t=T), AX.X, ALU.max,
                                negate=True).then_inc(sem("ag_max"), 1)
                dve.wait_ge(sem("ag_exp"), n + 1)
                V.reciprocal(prec[:, e], psum_[:, e])

            def ag_pl(n):
                dve.wait_ge(sem("ag_ph"), n + 1)
                V.tensor_tensor(flat(apl[:]), aux[:, 2], f32(flat(aph[:])), ALU.subtract).then_inc(sem("ag_pl"), 1)

            def ag_out(n, e):
                dve.wait_ge(sem("ag_v"), n + 1)
                own.wait()
                for t in range(T):
                    last = V.tensor_scalar(obuf[:, t, e * HD:(e + 1) * HD], aux[:, 3, t * P:(t + 1) * P],
                                           prec[:, e, t:t + 1], None, ALU.mult)
                last.then_inc(sem("ag_o"), 1)

            def ag_cp(j, src):
                dve.wait_ge(sem("ag_ctr"), j + 1)
                V.tensor_copy(flat(agT[:, ds(j * 4 + 2, 2)]), src).then_inc(sem("ag_cpD"), 1)

            def ag_gate(g):
                dve.wait_ge(sem("ag_o"), g * 4 + 4)
                dve.wait_ge(sem("ag_silu"), g + 1)
                at_least(dve, sem("ag_ctr"), g)
                V.tensor_tensor(s1[:], s0[:], obuf[:], ALU.mult).then_inc(sem("ag_gated"), 1)

            def ag(i):
                for c in range(2):
                    g = i * 2 + c
                    first = isinstance(g, int) and g == 0
                    ag_q(g * 4, 0)
                    ag_q(g * 4 + 1, 1)
                    dve.wait_ge(sem("ag_kvh"), g + 1)
                    V.tensor_tensor(kvl[:, c, 0], at(aqT, g + 16), f32(kvh[:, c, 0]), ALU.subtract)
                    V.tensor_tensor(kvl[:, c, 1].rearrange("p (t d) -> p t d", t=T), av[:, :, ds(g * HD, HD)],
                                    f32(kvh[:, c, 1]).rearrange("p (t d) -> p t d", t=T),
                                    ALU.subtract).then_inc(sem("ag_kv"), 1)
                    for u in range(8):
                        split(UNITS["ag"] + 8 * c + u, i, 16)
                        if c == 1 and u == 6 and isinstance(i, int) and i == 1:
                            for kt in range(4):
                                stage("aout", agT, osh3, osl3, kt)
                        if u % 2 == 0:
                            ag_max(g * 4 + u // 2, u // 2)
                            if u:
                                if u == 2:
                                    at_least(dve, sem("ag_gated"), g)
                                ag_out(g * 4 + u // 2 - 1, u // 2 - 1)
                        else:
                            ag_pl(g * 4 + u // 2)
                            if u < 5:
                                ag_q(g * 4 + u // 2 + 2, u // 2 + 2)
                        if u == 0 and not first:
                            ag_out(g * 4 - 1, 3)
                            ag_gate(g - 1)
                        if u == 4 and not first:
                            ag_cp(g - 1, acc[:, 1 - c, 1])
            repeat(dve, 2, ag, last=True)

            def ag_turned():
                ag_out(15, 3)
                ag_gate(3)
                ag_cp(3, aux[:, 1])
                V.tensor_copy(mark[:], rs_y[:, 0:1]).then_inc(sem("dve_stage"), 1)
                dve.wait_ge(sem("ag_cpA"), 4)
                dve.wait_ge(sem("ag_cpD"), 4)
            rows("aout", DK, agT, osh3, osl3, ag_turned)

            def add_layer_norm(product, end, tab, done, name=None):
                def cols(x_, b):
                    return x_[:, b * CW:(b + 1) * CW]

                def added(t, b):
                    bank_ready(product, end, 4 * t + b)
                    own.mark(V.scalar_tensor_tensor(cols(h[:, t], b), cols(h[:, t], b), float(ALPHA), banks[4 * t + b],
                                                    ALU.mult, ALU.add))
                    return own.now()

                for t in range(T):
                    for b in range(4):
                        ready = added(t, b)
                        if t == 1 and b and name:
                            lo_of_tile(name, 0, b - 1)
                        dve.wait_ge(dve_own, ready)
                        own.mark(V.bn_stats(stats[:, t, b], cols(h[:, t], b)))
                    if t == 1 and name:
                        lo_of_tile(name, 0, 3)
                    own.wait()
                    own.step(V.bn_aggr(mv[:, t], stats[:, t].rearrange("p a b -> p (a b)")))
                    own.step(V.tensor_scalar(rs_v[:, t:t + 1], mv[:, t, 1:2], LN_EPS, None, ALU.add))
                    if t == 0 and not name:
                        rsqrt_one(0, lambda b: None)
                        V.scalar_tensor_tensor(shift[:], mv[:, 0, 0:1], -1.0, rs_y[:, 0:1], ALU.mult,
                                               ALU.mult).then_inc(sem("shift_in"), 1)
                        continue
                    rsqrt_one(t, lambda b: own.mark(V.scalar_tensor_tensor(
                        cols(h[:, t], b), cols(h[:, t], b), mv[:, t, 0:1], cols(tab[:, 0], b), ALU.subtract, ALU.mult)))
                    for b in range(4):
                        V.scalar_tensor_tensor(cols(h[:, t], b), cols(h[:, t], b), rs_y[:, t:t + 1], cols(tab[:, 1], b),
                                               ALU.mult, ALU.add).then_inc(sem(done), 1)
                if name:
                    for b in range(4):
                        lo_of_tile(name, 1, b)

            dve.wait_ge(sem("gains_in"), 64)
            add_layer_norm("aout", UNITS["ret"], lng1, "attn_done", "r")


            def r_ev(i, c):
                dve.wait_ge(used, i * 48 + 8 * (c + 1) + UNITS["ret"])
                if c == 0:
                    at_least(dve, sem("r_gtr"), i * 2)
                    V.tensor_copy(s0[:, 1], acc[:, 0, 1]).then_inc(sem("r_evD"), 1)
                elif c == 1:
                    V.tensor_scalar(s0[:, 1], acc[:, 1, 1], R_QK ** -0.5, None, ALU.mult).then_inc(sem("r_evD"), 1)
                elif c < 4:
                    dve.wait_ge(sem("r_evA"), i * 6 + c + 1)
                    V.tensor_tensor(rvl[:, c - 2], acc[:, c % 2], f32(rvh[:, c - 2]), ALU.subtract).then_inc(sem("r_evD"), 1)
                else:
                    dve.wait_ge(sem("r_evA"), i * 6 + c + 1)
                    dve.wait_ge(sem("r_norm"), i * 2 + c - 3)
                    V.tensor_tensor(s0[:], s0[:], onorm[:, c - 4], ALU.mult).then_inc(sem("r_evD"), 1)

            def r_rotate(n):
                dve.wait_ge(sem("r_evA"), 1)
                for t in range(T):
                    last = heads_rotate(s1[:, t], rt[:], s0[:, t], rcs[:, 0, t:t + 1], rcs[:, 1, t:t + 1], 2, 64)
                    if t == 0:
                        own.step(last)
                last.then_inc(sem("r_rot"), 1)

            def r_decay_arg(n, hh):
                head = n
                own.step(V.tensor_scalar(dmat[:, hh], dist[:, 0], at2(lg, head), None, ALU.mult))
                V.scalar_tensor_tensor(dmat[:, hh], dist[:, 1], at2(lg, head + 8), dmat[:, hh], ALU.mult,
                                       ALU.add).then_inc(sem("r_dexp"), 1)

            def at2(t_, n):
                return t_[:, n:n + 1] if isinstance(n, int) else t_[:, ds(n, 1)]

            def r_qlo(n, which):
                for b in range(2):
                    dve.wait_ge(sem("r_qhi"), n * 2 + b + 1)
                    V.tensor_tensor(flat(rql[:, which, 2 * b:2 * b + 2]), aux[:, b],
                                    f32(flat(rqh[:, which, 2 * b:2 * b + 2])), ALU.subtract).then_inc(sem("r_qlo"), 1)

            def r_decayed(n, hh):
                dve.wait_ge(sem("r_s"), n + 1)
                dve.wait_ge(sem("r_d"), n + 1)
                V.tensor_tensor(flat(dmat[:, hh]), aux[:, 2 + hh], flat(dmat[:, hh]), ALU.mult).then_inc(sem("r_p"), 1)

            def r_plo(n, hh):
                dve.wait_ge(sem("r_ph"), n + 1)
                V.tensor_tensor(ptl[:, hh], dmat[:, hh], f32(pth[:, hh]), ALU.subtract).then_inc(sem("r_pl"), 1)

            def r_norm(n, hh):
                dve.wait_ge(sem("r_o"), n + 1)
                for t in range(T):
                    own.mark(V.bn_stats(stats[:, t, 0], aux[:, 2 * hh + t]))
                own.wait()
                V.tensor_copy(rs_t[:, 0:1], rs_y[:, 0:1])
                for t in range(T):
                    own.mark(V.bn_aggr(mv[:, t], stats[:, t, 0]))
                own.wait()
                own.step(V.tensor_scalar(rs_v[:, 0:2], mv[:, :, 1], LN_EPS, None, ALU.add))
                rsqrt(2)
                for t in range(T):
                    last = V.tensor_scalar(onorm[:, hh, t], aux[:, 2 * hh + t], mv[:, t, 0:1], rs_y[:, t:t + 1],
                                           ALU.subtract, ALU.mult)
                last.then_inc(sem("r_norm"), 1)

            def r_gcp(n):
                dve.wait_ge(sem("r_gtr"), n + 1)
                V.tensor_copy(flat(rgT[:, ds(n * 4 + 2, 2)]), aux[:, 1]).then_inc(sem("r_gcpD"), 1)

            def ret(i):
                first = isinstance(i, int) and i == 0
                for c in range(6):
                    for u in range(8):
                        split(UNITS["ret"] + 8 * c + u, i, 48)
                        if c == 5 and u == 6 and isinstance(i, int) and i == 3:
                            for kt in range(4):
                                stage("rout", rgT, osh4, osl4, kt)
                        if c == 0 and u == 4 and not first:
                            r_gcp(i * 2 - 1)
                        if c == 1 and u == 0:
                            if first:
                                dve.wait_ge(sem("tables_in"), 144)
                                dve.wait_ge(sem("act_stage"), ACT_STAGE["lg"])
                            dve.wait_ge(sem("r_evA"), i * 6 + 1)
                            dve.wait_ge(sem("r_evD"), i * 6 + 1)
                            r_rotate(i * 2)
                            r_decay_arg(i * 2, 0)
                            r_decay_arg(i * 2 + 1, 1)
                        if c == 1 and u == 5:
                            r_qlo(i * 2, 0)
                        if c == 2 and u == 0:
                            dve.wait_ge(sem("r_evA"), i * 6 + 2)
                            dve.wait_ge(sem("r_evD"), i * 6 + 2)
                            r_rotate(i * 2 + 1)
                        if c == 2 and u == 5:
                            r_qlo(i * 2 + 1, 1)
                        if c == 3 and u == 2:
                            r_decayed(i * 2, 0)
                            r_decayed(i * 2 + 1, 1)
                        if c == 3 and u == 4:
                            r_plo(i * 2, 0)
                            r_plo(i * 2 + 1, 1)
                        if c == 4 and u == 4:
                            r_norm(i * 2, 0)
                        if c == 4 and u == 6:
                            r_norm(i * 2 + 1, 1)
                        if c == 5 and u == 5:
                            r_gcp(i * 2)
                    r_ev(i, c)
            repeat(dve, 4, ret, own, last=True)

            def r_turned():
                r_gcp(7)
                V.tensor_copy(mark[:], rs_y[:, 0:1]).then_inc(sem("dve_stage"), 1)
                dve.wait_ge(sem("r_gcpA"), 8)
                dve.wait_ge(sem("r_gcpD"), 8)
            rows("rout", 32, rgT, osh4, osl4, r_turned)
            dve.wait_ge(sem("gains_in"), 96)
            add_layer_norm("rout", N_UNITS, lng2, "result")


def constants():
    f = np.float32
    j, q = np.arange(P)[:, None], np.arange(P)[None, :]
    mask_sb = np.zeros((P, 3 * P), f)
    mask_sb[:, 0:P] = np.where(j >= q, BIG, 0)
    mask_sb[:, 2 * P:] = np.where(j >= q, BIG, 0)
    mask_mla = np.zeros((P, T, TOK), f)
    for t in range(T):
        rows, keys = t * P + np.arange(P)[:, None], np.arange(TOK)[None, :]
        mask_mla[:, t] = np.where(keys // 64 <= rows // 64, 0, BIG)
    half = ROPE // 2
    invf = (10000.0 ** (-np.arange(half) / half)).astype(f)

    def axial(dim):
        row = np.repeat(np.arange(TOK // 64, dtype=f), 64)
        col = np.tile(np.arange(64, dtype=f), TOK // 64)
        hf = dim // 2
        inv = (10000.0 ** (-np.arange(0, hf, 2) / hf)).astype(f)
        ar, ac = row[:, None] * inv, col[:, None] * inv
        sign = np.concatenate([-np.ones(dim // 4), np.ones(dim // 4)] * 2).astype(f)
        a = np.concatenate([ar, ar, ac, ac], axis=-1).astype(np.float64)
        return np.cos(a).astype(f), (np.sin(a) * sign).astype(f)

    cos_a, sin_a = axial(HD)
    cos_r, sin_r = axial(R_QK)
    keys, qs = np.arange(TOK)[:, None], np.arange(TOK)[None, :]
    return {
        "c_ident": np.eye(P, dtype=f), "c_ntri": -(j >= q).astype(f), "c_nones": -np.ones((P, P), f),
        "c_mask_sb": mask_sb, "c_mask_mla": mask_mla.reshape(P, T * TOK), "c_invf": invf,
        "c_cos_a": cos_a, "c_sin_a": sin_a, "c_cos_r": cos_r, "c_sin_r": sin_r,
        "c_dist_f": np.maximum(qs - keys, 0).astype(f), "c_dist_b": np.maximum(keys - qs, 0).astype(f),
    }


def kernel(**inputs):
    import concourse.bacc as bacc
    from concourse.bass_utils import run_bass_kernel_spmd

    a = {k: np.asarray(v) for k, v in inputs.items()}

    def columns(v):
        return v.reshape(-1, P).T

    arrays = {
        "x": a["x"][0], "xT": a["x"][0].T, "positions": columns(a["positions"][0]),
        "g_pre": columns(a["norm_pre_mix"][0]), "w_in": a["w_in"][0], "b_gate": a["b_gate"][0],
        "g_lat": columns(np.concatenate([a["q_norm"][0], a["kv_norm"][0]])),
        "w_uq": a["w_uq"][0], "w_ukv": a["w_ukv"][0], "w_o_sb": a["w_o_sb"][0], "w_o_mla": a["w_o_mla"][0],
        "w_out": a["w_out"][0], "g_post_mix": a["norm_post_mix"][0], "g_ffn": columns(a["norm_pre_ffn"][0]),
        "w_gate_up": a["w_gate_up"][0], "w_down": a["w_down"][0], "g_post_ffn": a["norm_post_ffn"][0],
        "a_w_in": a["attn_w_in_2"][0], "a_q_gain": a["attn_q_gain_2"][0], "a_k_gain": a["attn_k_gain_2"][0],
        "a_w_out": a["attn_w_out_2"][0], "r_w_in": a["ret_w_in_2"][0],
        "r_decay": a["ret_decay_exp_2"][0].reshape(-1), "r_w_out": a["ret_w_out_2"][0],
        "ln_gain": a["ln_gain_2"], "ln_bias": a["ln_bias_2"],
    }
    arrays.update(constants())
    arrays = {k: np.ascontiguousarray(v) for k, v in arrays.items()}
    nc = bacc.Bacc("TRN2", target_bir_lowering=False, num_devices=1)
    args = {k: nc.dram_tensor(k, v.shape, mybir.dt.from_np(v.dtype), kind="ExternalInput").ap() for k, v in arrays.items()}
    args["out"] = nc.dram_tensor("out", (TOK, D), F32, kind="ExternalOutput").ap()
    build(nc, **args)
    r = run_bass_kernel_spmd(nc, [arrays], core_ids=[0])
    return r.results[0]["out"].reshape(1, TOK, D)
```
